# Optimizing a Trainium2 kernel written in Bass

```python
import jax, jax.numpy as jnp
from jax import lax
import numpy as np

D_MODEL = 1024
BATCH = 1
SEQ = 512
DEPTH = 2

CHUNK = 64
N_MIXERS = 2
RWKV_HEAD = 64
RWKV_HEADS = D_MODEL // RWKV_HEAD
DECAY_LORA = 64
AAA_LORA = 64
MV_LORA = 32
GATE_LORA = 160
GN_EPS = 64e-5
CONV_WIDTH = 31
FFN_CONV_WIDTH = 3
D_FF = 2816
MEM_TOKENS = 256
XATTN_HEADS = 4
XATTN_HEAD_DIM = D_MODEL // XATTN_HEADS
NORM_EPS = 1e-6
LN_EPS = 1e-5


def rmsnorm(x, g):
    x32 = x.astype(jnp.float32)
    y = x32 * lax.rsqrt(jnp.mean(x32 * x32, axis=-1, keepdims=True) + NORM_EPS)
    return (y * g).astype(x.dtype)

def layernorm(x, g, b):
    x32 = x.astype(jnp.float32)
    mu = jnp.mean(x32, axis=-1, keepdims=True)
    var = jnp.mean(jnp.square(x32 - mu), axis=-1, keepdims=True)
    return ((x32 - mu) * lax.rsqrt(var + LN_EPS) * g + b).astype(x.dtype)

def causal_dwconv(x, w):
    k_w = w.shape[0]
    return lax.conv_general_dilated(
        x, w[:, None, :].astype(x.dtype), window_strides=(1,), padding=[(k_w - 1, 0)],
        dimension_numbers=('NWC', 'WIO', 'NWC'), feature_group_count=x.shape[-1])

def rwkv7_step(S, inp):
    r_t, dec_t, k_t, v_t, kk_t, a_t = inp
    sa = jnp.einsum('bhij,bhj->bhi', S, -kk_t)
    S = (S * dec_t[:, :, None, :]
         + sa[..., None] * (kk_t * a_t)[:, :, None, :]
         + v_t[..., None] * k_t[:, :, None, :])
    y = jnp.einsum('bhij,bhj->bhi', S, r_t)
    return S, y

def rwkv7_time_mix(h, mu, w_r, w_k, w_v, w_o, w0, w1, w2, a0, a1, a2, g1, g2,
                   k_k, k_a, r_k, ln_g, ln_b, v_first, v_res):
    B, T, D = h.shape
    H, N = RWKV_HEADS, RWKV_HEAD
    xx = jnp.pad(h, ((0, 0), (1, 0), (0, 0)))[:, :T] - h
    xr, xw, xk, xv, xa, xg = (h + xx * mu[i] for i in range(6))
    r = xr @ w_r
    k = xk @ w_k
    v = xv @ w_v
    logw = -jax.nn.softplus(-(w0 + jnp.tanh(xw @ w1) @ w2)) - 0.5
    decay = jnp.exp(-jnp.exp(logw.astype(jnp.float32)))
    a = jax.nn.sigmoid(a0 + (xa @ a1) @ a2)
    g = jax.nn.sigmoid(xg @ g1) @ g2
    kk = (k * k_k).astype(jnp.float32).reshape(B, T, H, N)
    kk = kk / jnp.maximum(jnp.sqrt(jnp.sum(kk * kk, axis=-1, keepdims=True)), 1e-12)
    k = k * (1.0 + (a - 1.0) * k_a)
    if v_res is not None:
        v0, v1, v2 = v_res
        v = v + (v_first - v) * jax.nn.sigmoid(v0 + (xv @ v1) @ v2)

    def heads_t(t):
        return t.astype(jnp.float32).reshape(B, T, H, N).transpose(1, 0, 2, 3)

    seq = (heads_t(r), heads_t(decay), heads_t(k), heads_t(v),
           kk.transpose(1, 0, 2, 3), heads_t(a))
    S0 = jnp.zeros((B, H, N, N), jnp.float32)
    _, y = lax.scan(rwkv7_step, S0, seq)
    y = y.transpose(1, 0, 2, 3)
    m = jnp.mean(y, axis=-1, keepdims=True)
    var = jnp.mean(jnp.square(y - m), axis=-1, keepdims=True)
    y = ((y - m) * lax.rsqrt(var + GN_EPS)).reshape(B, T, D) * ln_g + ln_b
    rh = r.astype(jnp.float32).reshape(B, T, H, N)
    kh = k.astype(jnp.float32).reshape(B, T, H, N)
    vh = v.astype(jnp.float32).reshape(B, T, H, N)
    bonus = (jnp.sum(rh * kh * r_k, axis=-1, keepdims=True) * vh).reshape(B, T, D)
    out = ((y + bonus) * g).astype(h.dtype) @ w_o
    return out, v

def conformer_conv(h, w_in, b_in, dw, dw_b, ln_g, ln_b, w_out, b_out):
    D = h.shape[-1]
    u = h @ w_in + b_in
    u = u[..., :D] * jax.nn.sigmoid(u[..., D:])
    u = causal_dwconv(u, dw) + dw_b
    u = jax.nn.silu(layernorm(u, ln_g, ln_b))
    return u @ w_out + b_out

def memory_cross_attention(h, memn, w_q, w_kv, w_o):
    B, T, D = h.shape
    q = (h @ w_q).reshape(B, T, XATTN_HEADS, XATTN_HEAD_DIM)
    kv = memn @ w_kv
    km = kv[..., :D].reshape(B, -1, XATTN_HEADS, XATTN_HEAD_DIM)
    vm = kv[..., D:].reshape(B, -1, XATTN_HEADS, XATTN_HEAD_DIM)
    s = jnp.einsum('bthd,bmhd->bhtm', q, km).astype(jnp.float32) * (XATTN_HEAD_DIM ** -0.5)
    p = jax.nn.softmax(s, axis=-1).astype(h.dtype)
    o = jnp.einsum('bhtm,bmhd->bthd', p, vm).reshape(B, T, D)
    return o @ w_o

def conv_ffn(h, w_in, dw, w_out):
    u = causal_dwconv(h @ w_in, dw)
    gate, val = u[..., :D_FF], u[..., D_FF:]
    return (jax.nn.silu(gate) * val) @ w_out

def first_inputs(seed: int = 0) -> dict:
    key = jax.random.key(seed)
    ks = iter(jax.random.split(key, 64))
    D = D_MODEL
    NA = (DEPTH + 1) // 2
    NB = DEPTH // 2
    NV = max(NA - 1, 0)

    def nrm(shape, scale):
        return jax.random.normal(next(ks), shape, jnp.float32) * scale

    def unif(shape, lo, hi):
        return jax.random.uniform(next(ks), shape, jnp.float32, lo, hi)

    def gain(shape):
        return 1.0 + nrm(shape, 0.05)

    sd = D ** -0.5
    return {
        'x': nrm((BATCH, SEQ, D), 1.0),
        'mem': nrm((BATCH, MEM_TOKENS, D), 1.0),
        'mem_norm_g': gain((D,)),
        'norm_mix_g': gain((DEPTH, D)),
        'norm_xattn_g': gain((DEPTH, D)),
        'norm_ffn_g': gain((DEPTH, D)),
        'final_norm_g': gain((D,)),
        'rwkv_mu': unif((NA, 6, D), 0.0, 1.0),
        'rwkv_w_r': nrm((NA, D, D), sd),
        'rwkv_w_k': nrm((NA, D, D), sd),
        'rwkv_w_v': nrm((NA, D, D), sd),
        'rwkv_w_o': nrm((NA, D, D), sd),
        'rwkv_w0': unif((NA, D), -6.0, 1.0),
        'rwkv_w1': nrm((NA, D, DECAY_LORA), sd),
        'rwkv_w2': nrm((NA, DECAY_LORA, D), 0.5 * DECAY_LORA ** -0.5),
        'rwkv_a0': nrm((NA, D), 0.3),
        'rwkv_a1': nrm((NA, D, AAA_LORA), sd),
        'rwkv_a2': nrm((NA, AAA_LORA, D), 0.5 * AAA_LORA ** -0.5),
        'rwkv_g1': nrm((NA, D, GATE_LORA), sd),
        'rwkv_g2': nrm((NA, GATE_LORA, D), GATE_LORA ** -0.5),
        'rwkv_k_k': 0.85 + nrm((NA, D), 0.05),
        'rwkv_k_a': 1.0 + nrm((NA, D), 0.05),
        'rwkv_r_k': nrm((NA, RWKV_HEADS, RWKV_HEAD), 0.1),
        'rwkv_ln_g': gain((NA, D)),
        'rwkv_ln_b': nrm((NA, D), 0.02),
        'rwkv_v0': nrm((NV, D), 0.3),
        'rwkv_v1': nrm((NV, D, MV_LORA), sd),
        'rwkv_v2': nrm((NV, MV_LORA, D), 0.5 * MV_LORA ** -0.5),
        'conv_w_in': nrm((NB, D, 2 * D), sd),
        'conv_b_in': nrm((NB, 2 * D), 0.02),
        'conv_dw': nrm((NB, CONV_WIDTH, D), CONV_WIDTH ** -0.5),
        'conv_dw_b': nrm((NB, D), 0.02),
        'conv_ln_g': gain((NB, D)),
        'conv_ln_b': nrm((NB, D), 0.02),
        'conv_w_out': nrm((NB, D, D), sd),
        'conv_b_out': nrm((NB, D), 0.02),
        'xattn_w_q': nrm((DEPTH, D, D), sd),
        'xattn_w_kv': nrm((DEPTH, D, 2 * D), sd),
        'xattn_w_o': nrm((DEPTH, D, D), sd),
        'ffn_w_in': nrm((DEPTH, D, 2 * D_FF), sd),
        'ffn_dw': nrm((DEPTH, FFN_CONV_WIDTH, 2 * D_FF), FFN_CONV_WIDTH ** -0.5),
        'ffn_w_out': nrm((DEPTH, D_FF, D), D_FF ** -0.5),
    }

def first_block(x, mem, mem_norm_g, norm_mix_g, norm_xattn_g, norm_ffn_g, final_norm_g,
              rwkv_mu, rwkv_w_r, rwkv_w_k, rwkv_w_v, rwkv_w_o, rwkv_w0, rwkv_w1, rwkv_w2,
              rwkv_a0, rwkv_a1, rwkv_a2, rwkv_g1, rwkv_g2, rwkv_k_k, rwkv_k_a, rwkv_r_k,
              rwkv_ln_g, rwkv_ln_b, rwkv_v0, rwkv_v1, rwkv_v2,
              conv_w_in, conv_b_in, conv_dw, conv_dw_b, conv_ln_g, conv_ln_b,
              conv_w_out, conv_b_out, xattn_w_q, xattn_w_kv, xattn_w_o,
              ffn_w_in, ffn_dw, ffn_w_out):
    memn = rmsnorm(mem, mem_norm_g)
    v_first = None
    ia = 0
    ib = 0
    for layer in range(DEPTH):
        h = rmsnorm(x, norm_mix_g[layer])
        if layer % N_MIXERS == 0:
            v_res = None if ia == 0 else (rwkv_v0[ia - 1], rwkv_v1[ia - 1], rwkv_v2[ia - 1])
            out, v = rwkv7_time_mix(
                h, rwkv_mu[ia], rwkv_w_r[ia], rwkv_w_k[ia], rwkv_w_v[ia], rwkv_w_o[ia],
                rwkv_w0[ia], rwkv_w1[ia], rwkv_w2[ia], rwkv_a0[ia], rwkv_a1[ia], rwkv_a2[ia],
                rwkv_g1[ia], rwkv_g2[ia], rwkv_k_k[ia], rwkv_k_a[ia], rwkv_r_k[ia],
                rwkv_ln_g[ia], rwkv_ln_b[ia], v_first, v_res)
            if ia == 0:
                v_first = v
            ia += 1
        else:
            out = conformer_conv(h, conv_w_in[ib], conv_b_in[ib], conv_dw[ib], conv_dw_b[ib],
                                 conv_ln_g[ib], conv_ln_b[ib], conv_w_out[ib], conv_b_out[ib])
            ib += 1
        x = x + out
        x = x + memory_cross_attention(rmsnorm(x, norm_xattn_g[layer]), memn,
                                       xattn_w_q[layer], xattn_w_kv[layer], xattn_w_o[layer])
        x = x + conv_ffn(rmsnorm(x, norm_ffn_g[layer]), ffn_w_in[layer], ffn_dw[layer],
                         ffn_w_out[layer])
    return rmsnorm(x, final_norm_g)


DEPTH_2 = 1

Q_BLOCK = 128
GLA_HEADS = 4
GLA_DK = 64
GLA_DV = 128
GLA_LOWRANK = 16
GLA_TAU = 16.0
FOX_HEADS = 8
FOX_HD = 64
CONV_W = 3
EPS = 1e-6

GLA_WIDTH = GLA_HEADS * GLA_DV
FOX_WIDTH = FOX_HEADS * FOX_HD
IN_SPLITS = (GLA_HEADS * GLA_DK, GLA_HEADS * GLA_DK, GLA_WIDTH, GLA_WIDTH, GLA_LOWRANK,
             FOX_WIDTH, FOX_WIDTH, FOX_WIDTH, FOX_HEADS, D_MODEL, D_MODEL)
IN_COLS = sum(IN_SPLITS)
IN_OFFSETS = tuple(int(v) for v in np.cumsum(IN_SPLITS)[:-1])


def rmsnorm_2(x, g):
    xf = x.astype(jnp.float32)
    y = xf * lax.rsqrt(jnp.mean(xf * xf, axis=-1, keepdims=True) + EPS)
    return (y * g.astype(jnp.float32)).astype(x.dtype)

def gla_chunked(q, k, v, log_a):
    B, S, H, dk = q.shape
    dv = v.shape[-1]
    n = S // CHUNK
    def blocks(t):
        return t.astype(jnp.float32).reshape(B, n, CHUNK, H, t.shape[-1]).transpose(0, 3, 1, 2, 4)
    qc, kc, vc, la = blocks(q), blocks(k), blocks(v), blocks(log_a)
    b = jnp.cumsum(la, axis=3)
    q_e = qc * jnp.exp(b)
    k_e = kc * jnp.exp(-b)
    causal = jnp.tril(jnp.ones((CHUNK, CHUNK), dtype=bool))
    scores = jnp.where(causal, jnp.einsum('bhnld,bhnmd->bhnlm', q_e, k_e), 0.0)
    o_intra = jnp.einsum('bhnlm,bhnmv->bhnlv', scores, vc)
    b_last = b[:, :, :, -1:, :]
    chunk_kv = jnp.einsum('bhnld,bhnlv->bhndv', kc * jnp.exp(b_last - b), vc)
    decay = jnp.exp(b_last[:, :, :, 0, :])

    def step(state, inp):
        dec, kv = inp
        return dec[..., None] * state + kv, state

    _, prev = lax.scan(step, jnp.zeros((B, H, dk, dv), jnp.float32),
                       (jnp.moveaxis(decay, 2, 0), jnp.moveaxis(chunk_kv, 2, 0)))
    prev = jnp.moveaxis(prev, 0, 2)
    o = o_intra + jnp.einsum('bhnld,bhndv->bhnlv', q_e, prev)
    return o.transpose(0, 2, 3, 1, 4).reshape(B, S, H, dv).astype(v.dtype)

def fox_attention(q, k, v, log_f):
    B, S, H, d = q.shape
    scale = d ** -0.5
    qh, kh, vh = (t.transpose(0, 2, 1, 3) for t in (q, k, v))
    c = jnp.cumsum(log_f.astype(jnp.float32), axis=1).transpose(0, 2, 1)
    outs = []
    for i in range(S // Q_BLOCK):
        lo, hi = i * Q_BLOCK, (i + 1) * Q_BLOCK
        logits = jnp.einsum('bhqd,bhkd->bhqk', qh[:, :, lo:hi], kh[:, :, :hi]).astype(jnp.float32) * scale
        logits = logits + c[:, :, lo:hi, None] - c[:, :, None, :hi]
        mask = jnp.arange(hi)[None, :] <= jnp.arange(lo, hi)[:, None]
        p = jax.nn.softmax(jnp.where(mask, logits, -jnp.inf), axis=-1)
        outs.append(jnp.einsum('bhqk,bhkd->bhqd', p.astype(v.dtype), vh[:, :, :hi]))
    return jnp.concatenate(outs, axis=2).transpose(0, 2, 1, 3)

def causal_dwconv_2(u, w, bias):
    S = u.shape[1]
    up = jnp.pad(u, ((0, 0), (CONV_W - 1, 0), (0, 0)))
    out = bias
    for j in range(CONV_W):
        out = out + w[j] * up[:, j:j + S]
    return out

def hybrid_layer(x, norm_mix_g, w_in, gla_alpha_w2, gla_alpha_b, gla_out_norm_g,
                 fox_forget_b, fox_q_norm_g, fox_k_norm_g, gate_b, w_gla_branch,
                 w_fox_branch, w_out, norm_ffn_g, w_up, conv_w, conv_b, w_down):
    B, S, _ = x.shape
    h = rmsnorm_2(x, norm_mix_g)
    gq, gk, gv, gr, glr, fq, fk, fv, ff, g_gla, g_fox = jnp.split(h @ w_in, IN_OFFSETS, axis=-1)

    log_a = jax.nn.log_sigmoid(glr @ gla_alpha_w2 + gla_alpha_b) / GLA_TAU
    o_gla = gla_chunked(gq.reshape(B, S, GLA_HEADS, GLA_DK) * (GLA_DK ** -0.5),
                        gk.reshape(B, S, GLA_HEADS, GLA_DK),
                        gv.reshape(B, S, GLA_HEADS, GLA_DV),
                        log_a.reshape(B, S, GLA_HEADS, GLA_DK))
    o_gla = rmsnorm_2(o_gla, gla_out_norm_g.reshape(GLA_HEADS, GLA_DV)).reshape(B, S, GLA_WIDTH) * jax.nn.silu(gr)

    fqh = rmsnorm_2(fq.reshape(B, S, FOX_HEADS, FOX_HD), fox_q_norm_g)
    fkh = rmsnorm_2(fk.reshape(B, S, FOX_HEADS, FOX_HD), fox_k_norm_g)
    log_f = jax.nn.log_sigmoid(ff + fox_forget_b)
    o_fox = fox_attention(fqh, fkh, fv.reshape(B, S, FOX_HEADS, FOX_HD), log_f).reshape(B, S, FOX_WIDTH)

    y = jax.nn.sigmoid(g_gla + gate_b[0]) * (o_gla @ w_gla_branch) \
        + jax.nn.sigmoid(g_fox + gate_b[1]) * (o_fox @ w_fox_branch)
    x = x + y @ w_out

    a, val = jnp.split(rmsnorm_2(x, norm_ffn_g) @ w_up, 2, axis=-1)
    a = causal_dwconv_2(a, conv_w, conv_b)
    return x + (jax.nn.gelu(a) * val) @ w_down

def second_inputs(seed: int = 0) -> dict:
    key = jax.random.key(seed)
    ks = jax.random.split(key, 20)
    L = DEPTH_2
    nrm = jax.random.normal
    return {
        'x': nrm(ks[0], (BATCH, SEQ, D_MODEL), jnp.float32),
        'norm_mix_g': 1.0 + 0.02 * nrm(ks[1], (L, D_MODEL), jnp.float32),
        'w_in': nrm(ks[2], (L, D_MODEL, IN_COLS), jnp.float32) * D_MODEL ** -0.5,
        'gla_alpha_w2': nrm(ks[3], (L, GLA_LOWRANK, GLA_HEADS * GLA_DK), jnp.float32) * GLA_LOWRANK ** -0.5,
        'gla_alpha_b': 0.1 * nrm(ks[4], (L, GLA_HEADS * GLA_DK), jnp.float32),
        'gla_out_norm_g': 1.0 + 0.02 * nrm(ks[5], (L, GLA_WIDTH), jnp.float32),
        'fox_forget_b': 3.0 + nrm(ks[6], (L, FOX_HEADS), jnp.float32),
        'fox_q_norm_g': 1.0 + 0.02 * nrm(ks[7], (L, FOX_HD), jnp.float32),
        'fox_k_norm_g': 1.0 + 0.02 * nrm(ks[8], (L, FOX_HD), jnp.float32),
        'gate_b': 0.1 * nrm(ks[9], (L, 2, D_MODEL), jnp.float32),
        'w_gla_branch': nrm(ks[10], (L, GLA_WIDTH, D_MODEL), jnp.float32) * GLA_WIDTH ** -0.5,
        'w_fox_branch': nrm(ks[11], (L, FOX_WIDTH, D_MODEL), jnp.float32) * FOX_WIDTH ** -0.5,
        'w_out': nrm(ks[12], (L, D_MODEL, D_MODEL), jnp.float32) * D_MODEL ** -0.5,
        'norm_ffn_g': 1.0 + 0.02 * nrm(ks[13], (L, D_MODEL), jnp.float32),
        'w_up': nrm(ks[14], (L, D_MODEL, 2 * D_FF), jnp.float32) * D_MODEL ** -0.5,
        'conv_w': nrm(ks[15], (L, CONV_W, D_FF), jnp.float32) * CONV_W ** -0.5,
        'conv_b': 0.02 * nrm(ks[16], (L, D_FF), jnp.float32),
        'w_down': nrm(ks[17], (L, D_FF, D_MODEL), jnp.float32) * D_FF ** -0.5,
        'norm_final_g': 1.0 + 0.02 * nrm(ks[18], (D_MODEL,), jnp.float32),
    }

def second_block(x, norm_mix_g, w_in, gla_alpha_w2, gla_alpha_b, gla_out_norm_g,
              fox_forget_b, fox_q_norm_g, fox_k_norm_g, gate_b, w_gla_branch,
              w_fox_branch, w_out, norm_ffn_g, w_up, conv_w, conv_b, w_down, norm_final_g):
    for l in range(DEPTH_2):
        x = hybrid_layer(x, norm_mix_g[l], w_in[l], gla_alpha_w2[l], gla_alpha_b[l], gla_out_norm_g[l],
                         fox_forget_b[l], fox_q_norm_g[l], fox_k_norm_g[l], gate_b[l], w_gla_branch[l],
                         w_fox_branch[l], w_out[l], norm_ffn_g[l], w_up[l], conv_w[l], conv_b[l], w_down[l])
    return rmsnorm_2(x, norm_final_g)


def setup_inputs(seed=0):
    out = dict(first_inputs(seed))
    for name, value in second_inputs(seed + 1).items():
        if name != "x":
            out[name + "_2"] = value
    return out


def reference(
    x, mem, mem_norm_g, norm_mix_g, norm_xattn_g, norm_ffn_g, final_norm_g, rwkv_mu, rwkv_w_r,
    rwkv_w_k, rwkv_w_v, rwkv_w_o, rwkv_w0, rwkv_w1, rwkv_w2, rwkv_a0, rwkv_a1, rwkv_a2, rwkv_g1,
    rwkv_g2, rwkv_k_k, rwkv_k_a, rwkv_r_k, rwkv_ln_g, rwkv_ln_b, rwkv_v0, rwkv_v1, rwkv_v2,
    conv_w_in, conv_b_in, conv_dw, conv_dw_b, conv_ln_g, conv_ln_b, conv_w_out, conv_b_out,
    xattn_w_q, xattn_w_kv, xattn_w_o, ffn_w_in, ffn_dw, ffn_w_out, norm_mix_g_2, w_in_2,
    gla_alpha_w2_2, gla_alpha_b_2, gla_out_norm_g_2, fox_forget_b_2, fox_q_norm_g_2,
    fox_k_norm_g_2, gate_b_2, w_gla_branch_2, w_fox_branch_2, w_out_2, norm_ffn_g_2, w_up_2,
    conv_w_2, conv_b_2, w_down_2, norm_final_g_2,
):
    x = first_block(
        x, mem, mem_norm_g, norm_mix_g, norm_xattn_g, norm_ffn_g, final_norm_g, rwkv_mu,
        rwkv_w_r, rwkv_w_k, rwkv_w_v, rwkv_w_o, rwkv_w0, rwkv_w1, rwkv_w2, rwkv_a0, rwkv_a1,
        rwkv_a2, rwkv_g1, rwkv_g2, rwkv_k_k, rwkv_k_a, rwkv_r_k, rwkv_ln_g, rwkv_ln_b, rwkv_v0,
        rwkv_v1, rwkv_v2, conv_w_in, conv_b_in, conv_dw, conv_dw_b, conv_ln_g, conv_ln_b,
        conv_w_out, conv_b_out, xattn_w_q, xattn_w_kv, xattn_w_o, ffn_w_in, ffn_dw, ffn_w_out,
    )
    return second_block(
        x, norm_mix_g_2, w_in_2, gla_alpha_w2_2, gla_alpha_b_2, gla_out_norm_g_2,
        fox_forget_b_2, fox_q_norm_g_2, fox_k_norm_g_2, gate_b_2, w_gla_branch_2,
        w_fox_branch_2, w_out_2, norm_ffn_g_2, w_up_2, conv_w_2, conv_b_2, w_down_2,
        norm_final_g_2,
    )


_drawn_inputs = setup_inputs


def setup_inputs(seed=0):
    import zlib

    import numpy as np

    out = dict(_drawn_inputs(seed))
    spreads = {}
    factors = {'mem_norm_g': 4.211,
     'norm_xattn_g': 6.365,
     'rwkv_w1': 2.908,
     'rwkv_w2': 2.832,
     'rwkv_ln_b': 3.326,
     'conv_b_in': 4.234,
     'conv_ln_b': 4.352,
     'conv_b_out': 2.736,
     'norm_mix_g_2': 3.566,
     'gla_alpha_b_2': 3.462,
     'gla_out_norm_g_2': 8.0,
     'fox_q_norm_g_2': 8.0,
     'fox_k_norm_g_2': 8.0,
     'gate_b_2': 3.801,
     'norm_ffn_g_2': 12.033,
     'conv_b_2': 16.646,
     'norm_final_g_2': 7.821}
    for name, (base, spread) in spreads.items():
        noise = np.random.default_rng([zlib.crc32(name.encode()), seed]).standard_normal(out[name].shape)
        drawn = base * np.exp(spread * noise) if base else spread * noise
        out[name] = __import__('jax').numpy.asarray(drawn.astype(out[name].dtype))
    for name, factor in factors.items():
        out[name] = (out[name] * factor).astype(out[name].dtype)
    return out
```

```python
from contextlib import ExitStack

import numpy as np
import concourse.bass as bass
from concourse import mybir

F32 = mybir.dt.float32
F32R = mybir.dt.float32r
ALU = mybir.AluOpType
ACT = mybir.ActivationFunctionType
AX = mybir.AxisListType

P = 128
D = 1024
KT = D // P
T = 512
MEM = 256
FF = 2816
FT = FF // P
BLOCKS = 8
SLOTS = 4
CH = 64
NCH = T // CH
CONVW = 31
EPS = 1e-6
LN_EPS = 1e-5
GN_EPS = 64e-5
RSQRT_E = float(np.exp(-0.5))
LN2 = float(np.log(2.0))

STREAM = [
    ("lora_in", 1), ("gate_in", 2), ("w2", 1), ("a2", 1), ("k", 8), ("r", 8), ("v", 8),
    ("g2", 2), ("o", 8),
    ("kv0", 16), ("q0", 8), ("xo0", 8), ("up0", 2 * FT), ("down0", 24),
    ("cin", 16), ("kv1", 16), ("cout", 8),
    ("q1", 8), ("xo1", 8), ("up1", 2 * FT), ("down1", 24),
    ("in2", 41), ("branch", 8), ("out2", 8), ("up2", 2 * FT), ("down2", 24),
]
UNIT0 = {}
_u = 0
for _name, _n in STREAM:
    UNIT0[_name] = _u
    _u += _n
UNITS = _u
assert UNITS % SLOTS == 0

PARAMS = [
    ("mem_norm_g", KT), ("norm_mix_g", 2 * KT), ("norm_xattn_g", 2 * KT), ("norm_ffn_g", 2 * KT),
    ("final_norm_g", KT), ("mu", 6 * KT), ("w0", KT), ("a0", KT), ("k_k", KT), ("k_a", KT), ("r_k", KT),
    ("ln_g", KT), ("ln_b", KT), ("conv_b_in", 2 * KT), ("conv_dw", KT * CONVW), ("conv_dw_b", KT),
    ("conv_ln_g", KT), ("conv_ln_b", KT), ("conv_b_out", KT), ("ffn_dw", 2 * FT * 2 * 3),
    ("norm_mix_g_2", KT), ("gla_b", 2), ("gla_norm_g", 4), ("fox_q_g", 1), ("fox_k_g", 1),
    ("gate_b_2", 2 * KT), ("norm_ffn_g_2", KT), ("conv_w_2", FT * 3), ("conv_b_2", FT),
    ("norm_final_g_2", KT), ("fox_fb", 1),
]
PCOL = {}
_c = 0
for _name, _n in PARAMS:
    PCOL[_name] = _c
    _c += _n
NPAR = _c


def constants():
    i = np.arange(P)
    s, t = i[:, None], i[None, :]
    same64 = (s // 64) == (t // 64)
    f = lambda m: m.astype(np.float32)
    common = np.concatenate([f(s == t), np.ones((P, P), np.float32), f(same64)], 1)
    tt = np.arange(64)[None, :]
    ac = np.concatenate([f(same64 & (s < t)), f((s % 64) <= tt)], 1)
    n16 = f((s // 16 == t // 16) & (s < t))
    a16 = f((s // 16 == t // 16) & (t < s))
    a32 = f((s // 32 == t // 32) & (s // 16 != t // 16) & (t < s))
    a64 = f(same64 & (s // 32 != t // 32) & (t < s))
    scan = np.broadcast_to(f(np.arange(T) % CH != 0)[None, :], (P, T))
    prep = np.zeros((P, 4, 8), np.float32)
    for k in range(4):
        prep[:64, k, 2 * k] = 1
        prep[64:, k, 2 * k + 1] = 1
    bsel = np.zeros((P, 4, P), np.float32)
    for k in range(4):
        bsel[2 * k, k, :64] = 1
        bsel[2 * k + 1, k, 64:] = 1
    gla = f(same64 & (s <= t))
    fox = np.where(t <= s, 0.0, -1e30).astype(np.float32)
    negsel = np.zeros((P, 8, P), np.float32)
    for h in range(8):
        negsel[32 + h, h, :] = -1
    return {
        "c_common": common,
        "c_prep": prep.reshape(P, -1),
        "c_core": np.concatenate([ac, n16, a16, a32, a64], 1),
        "c_post": bsel.reshape(P, -1),
        "c_hybrid": np.concatenate([scan, gla, fox, negsel.reshape(P, -1)], 1),
    }


CONST_COLS = {"c_common": 3 * P, "c_prep": 4 * 8, "c_core": 192 + 4 * P, "c_post": 4 * P,
              "c_hybrid": T + 2 * P + 8 * P}


class Chain:

    def __init__(self, eng, sem):
        self.eng, self.sem, self.base, self.n, self.at = eng, sem, 0, 0, None

    def step(self, ins):
        ins.then_inc(self.sem, 1)
        self.n += 1

    def wait(self, back=0):
        v = self.base + self.n - back
        self.eng.wait_ge(self.sem, v if self.at is None else self.at + v)

    def enter(self, i, stride):
        self.base, self.n, self.at = self.base + self.n, 0, i * stride

    def leave(self, rounds, stride):
        assert self.n == stride, (self.n, stride)
        self.base, self.n, self.at = self.base + stride * rounds, 0, None


class Plan:

    def __init__(self):
        self.total, self.first = {}, {}

    def take(self, stage, **counts):
        for what, n in counts.items():
            self.first[stage, what] = self.total.get(what, 0)
            self.total[what] = self.first[stage, what] + n

    def norm(self, stage, split=True):
        n = KT if split else 0
        self.take(stage, sq=KT, rstd=1, split=n, val=n)

    def __call__(self, stage, what):
        return self.first[stage, what]


def build_program(nc, dram):
    plan = Plan()
    plan.norm("norm0", split=False)
    for m in "wag":
        plan.take("mix" + m, split=KT, val=KT)
    plan.take("mid", split=1)
    plan.take("mixk", split=KT, val=KT)
    plan.take("gmid", split=2)
    for m in "rv":
        plan.take("mix" + m, split=KT, val=KT)
    plan.take("knorm", sq=KT)
    for stage, n in (("lora_in", 2), ("gate_in", 2), ("w2", 8), ("a2", 8), ("k", 8), ("r", 8), ("v", 8),
                     ("g2", 8), ("o", 8)):
        plan.take(stage, tile=n)
    plan.take("g2", full=0)
    plan.total["full"] = 1 + 7 + 7 + 6
    plan.take("post", split=KT, val=KT)
    plan.take("o", x=KT)
    for l in range(2):
        if l == 1:
            plan.norm("norm_conv")
            plan.take("cin", tile=16)
        plan.norm(f"norm_mem{l}")
        plan.take(f"kv{l}", tile=16)
        if l == 1:
            plan.take("ln", sq=KT, rstd=1, split=KT)
            plan.take("cout", tile=8, x=KT)
        plan.norm(f"norm_x{l}")
        plan.take(f"q{l}", tile=8)
        plan.take(f"heads{l}", tile=8, split=8, full=8)
        plan.take(f"xo{l}", tile=8, x=KT)
        plan.norm(f"norm_ffn{l}")
        plan.take(f"up{l}", tile=2 * FT, split=FT, val=FT, conv=2 * FT)
        plan.take(f"down{l}", tile=8, x=KT)
    plan.take("final", sq=KT, rstd=1, x=KT)
    plan.norm("norm_h")
    plan.take("in2", tile=41)
    plan.take("fox_norm", sq=8)
    plan.take("gla", sq=4, split=4)
    plan.take("fox", split=4)
    plan.take("branch", tile=16, full=8, split=KT, val=KT)
    plan.take("out2", tile=8, x=KT)
    plan.norm("norm_ffn2")
    plan.take("up2", tile=2 * FT, split=FT, val=FT, conv=FT)
    plan.take("down2", tile=8, x=KT)
    plan.take("last", sq=KT, rstd=1, x=KT)

    ctx = ExitStack()
    with ctx:
        cursor = [2048]

        def size(shape):
            return 4 * int(np.prod(shape[1:]))

        def at(name, shape, dtype, offset):
            assert offset + size(shape) <= nc.sbuf_usable_end, (name, offset)
            return nc.alloc_sbuf_tensor_at(name, shape, dtype, offset=offset)

        def place(name, shape, dtype=F32):
            t = at(name, shape, dtype, cursor[0])
            cursor[0] += (size(shape) + 31) // 32 * 32
            return t

        def sem(name):
            return ctx.enter_context(nc.semaphore(name))

        raw = place("raw", [P, SLOTS, BLOCKS * P])
        wh = place("wh", [P, SLOTS, BLOCKS * P], F32R)
        wl = place("wl", [P, SLOTS, BLOCKS * P], F32R)
        xt_at = cursor[0]
        xt = place("xt", [P, KT, T + 1])
        act_at = cursor[0]
        acth = place("acth", [P, KT, T], F32R)
        actl = place("actl", [P, KT, T], F32R)
        par = place("par", [P, NPAR])
        common = place("common", [P, 3 * P])
        omu = place("omu", [P, 7 * KT])
        zero = place("zero", [P, 1])
        eps = place("eps", [P, 5])
        tmp_at = cursor[0]
        tmp = place("tmp", [P, 2, T])
        sq_at = cursor[0]
        sq = place("sq", [P, 2, T])
        rstd_at = cursor[0]
        rstd = place("rstd", [P, T])
        zone = cursor[0]
        ident, ones, blk64 = (common[:, j * P:(j + 1) * P] for j in range(3))
        b_eps, b_ln, b_gn, b_rn, b_q = (eps[:, j:j + 1] for j in range(5))

        def x(k):
            return xt[:, k, 1:T + 1]

        def pc(name, k=0):
            c = k + PCOL[name]
            return par[:, c:c + 1] if isinstance(c, int) else par[:, bass.ds(c, 1)]

        cursor[0] = zone
        seq = {n: place("seq_" + n, [P, 16, 4, CH]) for n in "wakr"}
        v_at = cursor[0]
        seq["v"] = place("seq_v", [P, 16, 4, CH])
        yx_at = cursor[0]
        mixl = {0: place("mixl", [P, KT, T], F32R), 1: actl}
        mixh = {0: at("mixh", [P, KT, T], F32R, v_at), 1: acth}
        rn = at("rn", [P, KT, T], F32, yx_at)
        midh = at("midh", [P, T], F32R, sq_at)
        midl = at("midl", [P, T], F32R, sq_at + 2048)
        gmidh = place("gmidh", [P, 2, T], F32R)
        gmidl = place("gmidl", [P, 2, T], F32R)
        bonus = place("bonus", [8, 2, T])
        plast = place("plast", [P, 16, 4])
        selk = place("selk", [P, 4, 8])
        kk, cs, pp, pi = (at("prep_" + n, [P, 2, T], F32, xt_at + 4096 * j)
                          for j, n in enumerate(("kk", "cs", "pp", "pi")))
        room = [[act_at, act_at + 32768], [yx_at, yx_at + 16384], [xt_at, xt_at + 16384], [tmp_at, tmp_at + 10240]]

        def core(name, shape):
            r = next(r for r in room if r[0] + size(shape) <= r[1])
            r[0] += size(shape)
            return at("core_" + name, shape, F32, r[0] - size(shape))

        def both(name, shape):
            return [core(name + str(j), shape) for j in range(2)]

        TMA = core("tma", [P, 4, 384])
        TZ = core("tz", [P, 4, 256])
        TBK = both("tbk", [P, 4, 256])
        AR = both("ar", [P, 4, 192])
        BE = both("be", [P, 4, 192])
        c_core = core("consts", [P, CONST_COLS["c_core"]])
        BB, KB, VB = (core(n, [P, 4, P]) for n in ("bb", "kb", "vb"))
        XX, UU, SS = (core(n, [P, 4, P]) for n in ("x", "u", "s"))
        VT, AD, ND, T1, AO32, AO64 = (both(n, [P, 4, P]) for n in ("vt", "ad", "nd", "t1", "ao32", "ao64"))
        CC = both("c", [P, 4, CH])
        m_ac = c_core[:, 0:192]
        m_n16, m_a16, m_a32, m_a64 = (c_core[:, 192 + j * P:192 + (j + 1) * P] for j in range(4))
        c_post = at("c_post", [P, 4, P], F32, yx_at)
        yc, bv, grs, delta0 = (at("post_" + n, [P, 2, T], F32, zone + 4096 * j)
                               for j, n in enumerate(("yc", "bv", "grs", "delta")))
        g_all = at("g_all", [P, KT, T], F32, zone + 16384)

        cursor[0] = zone
        mem = place("mem", [P, KT, MEM])
        memh, meml = place("memh", [P, KT, MEM], F32R), place("meml", [P, KT, MEM], F32R)
        keys = place("keys", [P, KT, MEM])
        vals = place("vals", [P, KT, MEM])
        vtok = place("vtok", [P, 2, D])
        conv_at = cursor[0]
        query = place("query", [P, KT, T])
        prob = place("prob", [P, 2, 4, MEM])
        probt = place("probt", [P, 2, 2, T])
        delta1 = place("delta1", [P, 2, T])
        smax, snegm, ssum, srec = (place("soft_" + n, [P, 4, 4]) for n in ("max", "negm", "sum", "rec"))

        cursor[0] = zone
        hidh, hidl = place("hidh", [P, FT, T], F32R), place("hidl", [P, FT, T], F32R)
        cu_at = cursor[0]
        cu = place("cu", [P, 4, T + 2])
        cg, cv, sg = (place("ffn_" + n, [P, 2, T]) for n in ("cg", "cv", "sg"))
        delta2 = at("delta2", [P, 2, T], F32, cu_at)

        cursor[0] = conv_at
        gp = place("gp", [P, KT, T + CONVW - 1])
        ub = place("ub", [P, KT, T])
        glu = place("glu", [P, KT, T])
        delta3 = place("delta3", [P, 2, T])

        cursor[0] = zone
        gqk = place("gqk", [P, 4, T])
        gv, fv = place("gv", [P, 4, T]), place("fv", [P, 4, T])
        fq, fk = place("fq", [P, 4, T]), place("fk", [P, 4, T])
        gr = place("gr", [P, 4, T])
        gate_a, gate_b = place("gate_a", [P, KT, T]), place("gate_b", [P, KT, T])
        small = place("small", [P, T])
        gvt, fvt = place("gvt", [P, 4, T]), place("fvt", [P, 4, T])
        ket = place("ket", [P, 4, 256])
        hyb = place("hyb", [P, CONST_COLS["c_hybrid"]])
        w2g = place("w2g", [P, 256])
        gdec = place("gdec", [P, 2, NCH])
        fmax, fneg, fsum, frec = (place("fox_" + n, [P, 8, 4]) for n in ("max", "neg", "sum", "rec"))
        assert cursor[0] <= nc.sbuf_usable_end
        over = zone + 8192
        ls, le = at("ls", [P, 3, T], F32, over), at("le", [P, 3, T], F32, over + 6144)
        eb = at("eb", [P, 2, T], F32, over + 12288)
        enb = at("enb", [P, 2, T], F32, over + 6144)
        sct = at("sct", [P, 2, T], F32, over)
        states = at("gla_states", [P, NCH - 1, 2, P], F32, over + 4096)
        frs = at("frs", [P, 2, T], F32, over + 12288)
        fp = at("fox_p", [P, 2, 10 * P], F32, zone)
        fpt = at("fox_pt", [P, 2, 10 * P], F32, zone + 10240)
        yh, yl = at("yh", [P, KT, T], F32R, zone), at("yl", [P, KT, T], F32R, zone + 16384)
        delta4 = at("delta4", [P, 2, T], F32, zone + 32768)
        gmask, fmask = hyb[:, T:T + P], hyb[:, T + P:T + 2 * P]
        FOX_OFF = [0, P, 3 * P, 6 * P]
        FOX_TOFF = [0, 4 * P, 7 * P, 9 * P]

        psum = ctx.enter_context(nc.psum_tensor("psum", [P, 8, T], F32))
        bank = [psum[:, i, :] for i in range(8)]

        raw_in = [sem(f"raw_in{i}") for i in range(SLOTS)]
        par_in, common_in, x_in, selk_in, ccore_in, cpost_in, xagain_in = (
            sem(n) for n in ("par_in", "common_in", "x_in", "selk_in", "ccore_in", "cpost_in", "xagain_in"))
        zero_ready = sem("zero_ready")
        split_hi = sem("split_hi")
        split_done = sem("split_done")
        units_used = sem("units_used")
        tile_full = sem("tile_full")
        evacuated = sem("evacuated")
        omu_ready = sem("omu_ready")
        sq_ready, sq_used = sem("sq_ready"), sem("sq_used")
        rstd_ready = sem("rstd_ready")
        val_ready, hi_ready, lo_ready = sem("val_ready"), sem("hi_ready"), sem("lo_ready")
        delta_ready, x_ready = sem("delta_ready"), sem("x_ready")
        dve_chain, act_chain = sem("dve_chain"), sem("act_chain")
        kss_ready, rn_ready = sem("kss_ready"), sem("rn_ready")
        scan_ready, decay_ready = sem("scan_ready"), sem("decay_ready")
        bonus_mm = sem("bonus_mm")
        prep_done = sem("prep_done")
        core_clear = sem("core_clear")
        core_pe, core_v, core_a = sem("core_pe"), sem("core_v"), sem("core_a")
        pro_pe, pro_v, pro_a = sem("pro_pe"), sem("pro_v"), sem("pro_a")
        post_pe, post_v, post_a = sem("post_pe"), sem("post_v"), sem("post_a")
        act_held, pe_held = sem("act_held"), sem("pe_held")
        out_in = sem("out_in")
        mem_in = [sem("mem_in0"), sem("mem_in1")]
        vt_mm, vt_ready = sem("vt_mm"), sem("vt_ready")
        sc_mm, smax_ready, p_exp, p_ready = sem("sc_mm"), sem("smax_ready"), sem("p_exp"), sem("p_ready")
        pt_mm, pt_v, pt_a = sem("pt_mm"), sem("pt_v"), sem("pt_a")
        conv_ready, gate_ready = sem("conv_ready"), sem("gate_ready")
        pad_ready, glu_ready, u_ready, mean_mm, uc_ready = (
            sem(n) for n in ("pad_ready", "glu_ready", "u_ready", "mean_mm", "uc_ready"))

        hyb_in, vt2_mm, vt2_ready, z_mm, z_ready, log_ready, cum_ready, eb_ready, qk_ready = (
            sem(n) for n in ("hyb_in", "vt2_mm", "vt2_ready", "z_mm", "z_ready", "log_ready", "cum_ready",
                             "eb_ready", "qk_ready"))
        ket_mm, ket_ready, kv_mm, kv_ready = (sem(n) for n in ("ket_mm", "ket_ready", "kv_mm", "kv_ready"))
        frs_ready, fox_scaled = sem("frs_ready"), sem("fox_scaled")
        gs_mm, gs_ready, go_mm, gla_scale, gla_done = (
            sem(n) for n in ("gs_mm", "gs_ready", "go_mm", "gla_scale", "gla_done"))
        fs_mm, fmax_ready, f_exp, fp_ready, fpt_mm, fpt_v, fpt_a, fo_mm, fo_a = (
            sem(n) for n in ("fs_mm", "fmax_ready", "f_exp", "fp_ready", "fpt_mm", "fpt_v", "fpt_a", "fo_mm", "fo_a"))

        UC = SLOTS
        SC = 2

        def numbered(*names):
            return {n: 2 * j + 1 for j, n in enumerate(names)}

        CPE = numbered("M2", "M4", "M8", "T4", "TT", "TZ", "Z", "X", "T64", "U", "Y")
        CV = numbered("T2", "T3", "T4", "TZ", "T64", "S")
        CA = numbered("M2", "M4", "M8", "TT", "Z", "X", "U", "Y")
        PPE = numbered("AC", "N", "BE", "T")
        PV, PA = {"load": 1, "AC": 2, "N": 4, "BE": 6}, {"load": 1, "V": 2, "T": 4}
        NCPE, NCV, NCA, NPPE, NPV, NPA = 22, 12, 16, 8, 7, 5

        def count(r, per, n):
            return r * per + n if isinstance(r, int) else r[0] * (2 * per) + (r[1] * per + n)

        def index(r, ahead=0):
            return count(r, 1, ahead)

        def parity(r):
            return r % 2 if isinstance(r, int) else r[1]
        POST_A = 4

        block = ctx.enter_context(nc.Block())

        @block.sync
        def _(sp):
            sp.dma_start(xt[:, :, 1:T + 1], dram["x"]).then_inc(x_in, 16)
            sp.dma_start(par[:, :], dram["par"]).then_inc(par_in, 16)
            sp.dma_start(common[:, :], dram["c_common"]).then_inc(common_in, 16)
            sp.dma_start(selk[:, :, :], dram["c_prep"].rearrange("p (k h) -> p k h", k=4)).then_inc(selk_in, 16)
            with sp.Fori(0, UNITS // SLOTS) as i:
                for s in range(SLOTS):
                    sp.wait_ge(split_done, i * SLOTS + s + 1)
                    sp.dma_start(raw[:, s, :], dram["weights"][i * SLOTS + s]).then_inc(raw_in[s], 16)

        @block.gpsimd
        def _(pool):
            pool.sem_inc(split_done, UC)
            pool.memset(zero[:, :], 0.0).then_inc(zero_ready, 1)
            pool.wait_ge(zero_ready, 1)
            with pool.Fori(0, UNITS // SLOTS) as i:
                for s in range(SLOTS):
                    pool.wait_ge(units_used, i * SLOTS + s + 1)
                    pool.wait_ge(raw_in[s], i * 16 + 16)
                    pool.tensor_tensor(wh[:, s, :], raw[:, s, :],
                                       zero[:, :].to_broadcast([P, BLOCKS * P]), ALU.add).then_inc(split_hi, 1)
                    pool.wait_ge(split_hi, i * SLOTS + s + 1)
                    pool.tensor_tensor(wl[:, s, :], raw[:, s, :], wh[:, s, :].bitcast(F32),
                                       ALU.subtract).then_inc(split_done, 1)

        @block.tensor
        def _(pe):
            pe.sem_inc(units_used, UC)
            pe.sem_inc(sq_used, SC)
            pe.sem_inc(core_pe, NCPE)
            pe.sem_inc(bonus_mm, SC)

            def product(out, slot, b, hi, lo, start, stop):
                w_h, w_l = wh[:, slot, b * P:(b + 1) * P], wl[:, slot, b * P:(b + 1) * P]
                pe.matmul(out, w_h, hi, start=start, stop=False)
                pe.matmul(out, w_h, lo, start=False, stop=False)
                return pe.matmul(out, w_l, hi, start=False, stop=stop)

            def split_unit(u):
                pe.wait_ge(split_done, u + 1 + UC)

            def free_bank(t):
                pe.wait_ge(evacuated, t + 1)

            def part(stage, k):
                pe.wait_ge(lo_ready, plan(stage, "split") + k + 1 + SC)

            def dense(stage, source, hi, lo, n=T, units=None, skip=0, also=None):
                u0, t0 = UNIT0[stage] + skip, plan(stage, "tile") + skip
                with pe.Fori(0, (units or dict(STREAM)[stage]) // SLOTS) as i:
                    for s in range(SLOTS):
                        split_unit(i * SLOTS + (u0 + s))
                        free_bank(i * SLOTS + (t0 + s))
                        for k in range(KT):
                            if s == 0:
                                part(source, k)
                            mm = product(bank[(t0 + s) % 4][:, 0:n], (u0 + s) % SLOTS, k,
                                         hi[:, k, 0:n], lo[:, k, 0:n], k == 0, k == KT - 1)
                        mm.then_inc(units_used, 1)
                        if also:
                            also(i, s)

            def down(stage, source, hi, lo):
                u0, t0 = UNIT0[stage], plan(stage, "tile")
                with pe.Fori(0, 2) as i:
                    for s in range(4):
                        free_bank(i * 4 + (t0 + s))
                        for k in range(FT):
                            j = 3 * s + k // BLOCKS
                            if k % BLOCKS == 0:
                                split_unit(i * 12 + (u0 + j))
                            if s == 0:
                                part(source, k)
                            mm = product(bank[(t0 + s) % 4][:, :], (u0 + j) % SLOTS, k % BLOCKS,
                                         hi[:, k, :], lo[:, k, :], k == 0, k == FT - 1)
                            if k % BLOCKS == BLOCKS - 1 or k == FT - 1:
                                mm.then_inc(units_used, 1)

            def norm_sum(stage, n=T):
                for k in range(KT):
                    pe.wait_ge(sq_ready, plan(stage, "sq") + k + 1)
                    pe.matmul(bank[4][:, 0:n], ones, sq[:, k % 2, 0:n], start=(k == 0),
                              stop=(k == KT - 1)).then_inc(sq_used, 1)

            pe.wait_ge(common_in, 16)
            norm_sum("norm0")
            split_unit(0)
            for j, m in enumerate("wa"):
                free_bank(j)
                for k in range(KT):
                    part("mix" + m, k)
                    mm = product(bank[j][:, :], 0, k, mixh[j][:, k, :], mixl[j][:, k, :], k == 0, k == KT - 1)
                mm.then_inc(units_used if j else tile_full, 1)
            for j in range(2):
                split_unit(1 + j)
                free_bank(2 + j)
                for k in range(KT):
                    part("mixg", k)
                    mm = product(bank[2 + j][:, :], 1 + j, k, mixh[0][:, k, :], mixl[0][:, k, :],
                                 k == 0, k == KT - 1)
                mm.then_inc(units_used, 1)
            part("mid", 0)
            for stage in ("w2", "a2"):
                u, t0 = UNIT0[stage], plan(stage, "tile")
                split_unit(u)
                for j in range(KT):
                    free_bank(t0 + j)
                    product(bank[(t0 + j) % 4][:, :], u % SLOTS, j, midh[:, :], midl[:, :], True, True)\
                        .then_inc(units_used if j == KT - 1 else tile_full, 1)
            dense("k", "mixk", mixh[1], mixl[1])
            dense("r", "mixr", mixh[0], mixl[0])
            for k in range(KT):
                pe.wait_ge(sq_ready, plan("knorm", "sq") + k + 1)
                if k >= 2:
                    pe.wait_ge(kss_ready, k - 1)
                pe.matmul(bank[4 + k % 2][:, :], blk64, sq[:, k % 2, :], start=True, stop=True).then_inc(sq_used, 1)

            pe.wait_ge(selk_in, 16)

            def bonus_sum(i, s):
                pe.wait_ge(scan_ready, i * 4 + (s + 1))
                pe.sem_inc(pe_held, 1)
                pe.matmul(psum[0:8, i + 6, :], selk[:, s, :], sq[:, s % 2, :], start=(s == 0),
                          stop=(s == 3)).then_inc(bonus_mm, 1)

            dense("v", "mixv", mixh[1], mixl[1], also=bonus_sum)

            pe.wait_ge(prep_done, 4 + 1)
            pe.wait_ge(evacuated, plan("v", "tile") + 8 + UC)

            def core_round(r, last=False):
                c, n = parity(r), 1 - parity(r)

                def seen_v(what, g):
                    pe.wait_ge(core_v, count(r, NCV, NCV + CV[what] + g))

                def seen_a(what, g):
                    pe.wait_ge(core_a, count(r, NCA, NCA + CA[what] + g))

                def each(step, count_=True):
                    for g in range(2):
                        for j, q in enumerate((2 * g, 2 * g + 1)):
                            ins = step(4 * g, g, j, q)
                        if count_:
                            ins.then_inc(core_pe, 1)

                def mm(out, lhsT, rhs, start=True, stop=True):
                    return pe.matmul(out, lhsT, rhs, start=start, stop=stop)

                def s2(o, g, j, q):
                    b = bank[o + c]
                    mm(b[:, j * 256:j * 256 + P], AD[c][:, q, :], ND[c][:, q, :])
                    return mm(b[:, j * 256 + P:j * 256 + 256], ND[c][:, q, :], AD[c][:, q, :])

                def s3(o, g, j, q):
                    if j == 0:
                        seen_a("M2", g)
                    b = bank[o + n]
                    mm(b[:, j * 256:j * 256 + P], TMA[:, q, 256:384], T1[c][:, q, :])
                    mm(b[:, j * 256 + P:j * 256 + 256], TMA[:, q, 256:384], TMA[:, q, P:256])
                    return mm(bank[o + 2][:, j * P:(j + 1) * P], TMA[:, q, P:256], TMA[:, q, 256:384])

                def s4(o, g, j, q):
                    if j == 0:
                        seen_v("T2", g)
                        seen_a("M4", g)
                    b = bank[o + c]
                    mm(b[:, j * 256:j * 256 + P], TMA[:, q, 256:384], TMA[:, q, 0:P])
                    return mm(b[:, j * 256 + P:j * 256 + 256], TMA[:, q, P:256], TMA[:, q, 256:384])

                def s5(o, g, j, q):
                    if j == 0:
                        seen_v("T3", g)
                        seen_a("M8", g)
                    return mm(bank[o + n][:, j * P:(j + 1) * P], TMA[:, q, 256:384], TMA[:, q, 0:P])

                def s6(o, g, j, q):
                    if j == 0:
                        seen_v("T4", g)
                    pe.transpose(bank[o + 2][:, j * 256:j * 256 + P], TMA[:, q, 0:P], ident)
                    return mm(bank[o + 2][:, j * 256 + P:j * 256 + 256], AO32[c][:, q, :], TMA[:, q, 0:P])

                def s7(o, g, j, q):
                    if j == 0:
                        seen_a("TT", g)
                    b = bank[o + c]
                    mm(b[:, j * 256:j * 256 + P], TZ[:, q, 0:P], TZ[:, q, P:256])
                    return mm(b[:, j * 256 + P:j * 256 + 256], TZ[:, q, P:256], TZ[:, q, 0:P])

                def s8(o, g, j, q):
                    if j == 0:
                        seen_v("TZ", g)
                    return mm(bank[o + n][:, j * P:(j + 1) * P], AO64[c][:, q, :], TMA[:, q, 0:P])

                def sx(o, g, j, q):
                    x_ = bank[o + 2][:, j * P:(j + 1) * P]
                    mm(x_, AR[c][:, q, 0:P], SS[:, q, :], stop=False)
                    return mm(x_, BE[c][:, q, 0:P], VT[c][:, q, :], start=False)

                def s9(o, g, j, q):
                    if j == 0:
                        seen_a("Z", g)
                    return mm(bank[o + c][:, j * P:(j + 1) * P], TZ[:, q, 0:P], TZ[:, q, P:256])

                def su(o, g, j, q):
                    if j == 0:
                        seen_v("T64", g)
                        seen_a("X", g)
                    return mm(bank[o + n][:, j * P:(j + 1) * P], TMA[:, q, 0:P], XX[:, q, :])

                def y_d(o, j):
                    return bank[o + 2][:, j * CH:(j + 1) * CH], bank[o + c][:, j * P:(j + 1) * P]

                def sy(o, g, j, q):
                    y, d = y_d(o, j)
                    mm(y, SS[:, q, :], AR[c][:, q, P:192], start=(j == 0), stop=False)
                    mm(y, VT[c][:, q, :], BE[c][:, q, P:192], start=False, stop=False)
                    return mm(d, TBK[c][:, q, P:256], VT[c][:, q, :], start=(j == 0), stop=False)

                def sz(o, g, j, q):
                    if j == 0:
                        seen_a("U", g)
                    y, d = y_d(o, j)
                    mm(y, UU[:, q, :], CC[c][:, q, :], start=False, stop=(j == 1))
                    return mm(d, TBK[c][:, q, 0:P], UU[:, q, :], start=False, stop=(j == 1))

                pe.wait_ge(pro_v, count(r, NPV, NPV))
                pe.wait_ge(pro_a, count(r, NPA, NPA))
                each(s2)
                pe.wait_ge(core_v, count(r, NCV, NCV))
                pe.wait_ge(core_a, count(r, NCA, NCA))
                def more(what, *groups):
                    if not last:
                        prepare(r, 1, what, groups)

                each(s3)
                each(s4)
                more("AC", 0)
                each(s5)
                more("AC", 1)
                each(s6)
                more("N", 0)
                each(s7)
                more("N", 1)
                each(s8)
                more("BE", 0)
                each(sx)
                more("BE", 1)
                each(s9)
                more("T", 0, 1)
                each(su)
                each(sy, False)
                each(sz)

            def prepare(r, ahead, what, groups=(0, 1)):
                c = (parity(r) + ahead) % 2

                def ready(sem_, per, n):
                    pe.wait_ge(sem_, count(r, per, ahead * per + n))

                for g in groups:
                    b = bank[4 * g + 3]
                    if what == "AC":
                        ready(pro_v, NPV, PV["load"])
                        ready(pro_a, NPA, PA["load"])
                    elif what == "N":
                        ready(pro_v, NPV, PV["AC"] + g)
                    elif what == "BE":
                        ready(pro_a, NPA, PA["V"] + g)
                    else:
                        ready(pro_v, NPV, PV["BE"] + g)
                    for j, q in enumerate((2 * g, 2 * g + 1)):
                        if what == "AC":
                            ins = pe.matmul(b[:, j * 192:(j + 1) * 192], BB[:, q, :], AR[c][:, q, :], start=True, stop=True)
                        elif what == "BE":
                            ins = pe.matmul(b[:, j * 192:(j + 1) * 192], KB[:, q, :], AR[c][:, q, :], start=True, stop=True)
                        elif what == "N":
                            pe.matmul(b[:, j * P:(j + 1) * P], AR[c][:, q, 0:P], BB[:, q, :], start=True, stop=True)
                            ins = pe.transpose(b[:, 256 + j * P:256 + (j + 1) * P], VB[:, q, :], ident)
                        else:
                            pe.transpose(b[:, j * 256:j * 256 + P], BB[:, q, :], ident)
                            ins = pe.transpose(b[:, j * 256 + P:j * 256 + 256], KB[:, q, :], ident)
                    ins.then_inc(pro_pe, 1)

            for what in ("AC", "N", "BE", "T"):
                prepare(0, 0, what)
            with pe.Fori(0, 7) as i:
                core_round((i, 0))
                core_round((i, 1))
            core_round(14)
            core_round(15, last=True)

            pe.wait_ge(core_v, NCV * 17)
            pe.wait_ge(core_a, NCA * 17)
            for j in range(KT):
                u, t = UNIT0["g2"] + j // 4, plan("g2", "tile") + j
                part("gmid", 1)
                if j % 4 == 0:
                    split_unit(u)
                free_bank(t)
                for b in range(2):
                    mm_ = product(bank[t % 4][:, :], u % SLOTS, 2 * (j % 4) + b, gmidh[:, b, :], gmidl[:, b, :],
                                  b == 0, b == 1)
                mm_.then_inc(units_used if j % 4 == 3 else tile_full, 1)
            pe.wait_ge(cpost_in, 16)
            for k in range(0, KT, 2):
                for s in range(2):
                    pe.wait_ge(post_a, 2 * k + POST_A)
                    pe.wait_ge(post_v, k + 2)
                    half, q = divmod(k + s, 4)
                    pe.matmul(bank[4 + s][:, :], blk64, seq["r"][:, 8 * half:8 * half + 8, q, :],
                              start=True, stop=True)
                    pe.matmul(bank[6 + s][:, :], c_post[0:8, q, :], bonus[0:8, half, :],
                              start=True, stop=True).then_inc(post_pe, 1)
                for s in range(2):
                    pe.wait_ge(post_a, 2 * k + s + 1 + POST_A)
                    pe.matmul(bank[4 + s][:, :], blk64, sq[:, s, :], start=True, stop=True).then_inc(post_pe, 1)
            dense("o", "post", acth, actl)

            def memory_side(l):
                if l == 0:
                    norm_sum("norm_mem0", MEM)
                    dense("kv0", "norm_mem0", memh, meml, n=MEM, units=4)
                    norm_sum("norm_x0")
                    dense("kv0", "norm_mem0", memh, meml, n=MEM, units=12, skip=4)
                    pe.wait_ge(rstd_ready, plan("norm_x0", "rstd") + 1)
                else:
                    dense("kv1", "norm_mem1", memh, meml, n=MEM)
                pe.wait_ge(evacuated, plan(f"kv{l}", "tile") + 16 + UC)
                for mt in range(2):
                    for c in range(2):
                        for j in range(4):
                            ins = pe.transpose(bank[4 + 2 * mt + c][:, j * P:(j + 1) * P],
                                               vals[:, 4 * c + j, mt * P:(mt + 1) * P], ident)
                        ins.then_inc(vt_mm, 1)

            def attention(l):
                if l == 1:
                    norm_sum("norm_x1")
                def scores(h):
                    for tt in range(4):
                        for k in range(2):
                            ins = pe.matmul(bank[4 + tt // 2][:, (tt % 2) * MEM:(tt % 2 + 1) * MEM],
                                            query[:, 2 * h + k, tt * P:(tt + 1) * P], keys[:, 2 * h + k, :],
                                            start=(k == 0), stop=(k == 1))
                    ins.then_inc(sc_mm, 1)

                dense(f"q{l}", f"norm_x{l}", acth, actl, units=4)
                pe.wait_ge(vt_ready, 4 * (l + 1))
                pe.wait_ge(evacuated, plan(f"q{l}", "tile") + 2 + UC)
                scores(0)
                dense(f"q{l}", f"norm_x{l}", acth, actl, units=4, skip=4)
                pe.wait_ge(evacuated, plan(f"q{l}", "tile") + 8 + UC)
                pe.wait_ge(p_exp, 4 * l + 1)
                scores(1)
                for h in range(4):
                    n = 4 * l + h
                    pe.wait_ge(p_ready, n + 1)
                    if h:
                        pe.wait_ge(pt_v, n)
                        pe.wait_ge(pt_a, n)
                    for mt in range(2):
                        for tt in range(4):
                            ins = pe.transpose(bank[6 + mt][:, tt * P:(tt + 1) * P],
                                               prob[:, h % 2, tt, mt * P:(mt + 1) * P], ident)
                    ins.then_inc(pt_mm, 1)
                    if h < 2:
                        pe.wait_ge(p_exp, n + 2)
                        scores(h + 2)
                    pe.wait_ge(pt_v, n + 1)
                    pe.wait_ge(pt_a, n + 1)
                    for dt in range(2):
                        t = plan(f"heads{l}", "tile") + 2 * h + dt
                        free_bank(t)
                        for mt in range(2):
                            ins = pe.matmul(bank[t % 4][:, :], vtok[:, mt, (2 * h + dt) * P:(2 * h + dt + 1) * P],
                                            probt[:, h % 2, mt, :], start=(mt == 0), stop=(mt == 1))
                        ins.then_inc(tile_full, 1)
                dense(f"xo{l}", f"heads{l}", acth, actl)

            def ffn(l):
                norm_sum(f"norm_ffn{l}")
                dense(f"up{l}", f"norm_ffn{l}", acth, actl)
                down(f"down{l}", f"up{l}", hidh, hidl)

            def convolution():
                norm_sum("norm_conv")
                dense("cin", "norm_conv", acth, actl, units=4)
                norm_sum("norm_mem1", MEM)
                dense("cin", "norm_conv", acth, actl, units=12, skip=4)
                memory_side(1)
                pe.wait_ge(vt_ready, 8)
                for k in range(KT):
                    pe.wait_ge(u_ready, k + 1)
                    ins = pe.matmul(bank[5][:, :], ones, ub[:, k, :], start=(k == 0), stop=(k == KT - 1))
                ins.then_inc(mean_mm, 1)
                norm_sum("ln")
                dense("cout", "ln", acth, actl)

            def final_norm():
                norm_sum("final")

            def hybrid():
                norm_sum("norm_h")
                u0, t0 = UNIT0["in2"], plan("in2", "tile")
                split_unit(u0)
                free_bank(t0)
                for k in range(KT):
                    part("norm_h", k)
                    ins = product(bank[t0 % 4][:, :], u0 % SLOTS, k, acth[:, k, :], actl[:, k, :], k == 0, k == KT - 1)
                ins.then_inc(units_used, 1)

                def inner(skip, n):
                    dense("in2", "norm_h", acth, actl, units=n, skip=skip)

                inner(1, 12)
                pe.wait_ge(evacuated, t0 + 13 + UC)
                for j in range(8):
                    tt = j % 4
                    if j >= 4:
                        pe.wait_ge(vt2_ready, j - 3)
                    for k in range(4):
                        ins = pe.transpose(bank[4 + tt][:, k * P:(k + 1) * P],
                                           (gv if j < 4 else fv)[:, k, tt * P:(tt + 1) * P], ident)
                    ins.then_inc(vt2_mm, 1)
                inner(13, 4)
                pe.wait_ge(hyb_in, 32)
                for p in range(2):
                    pe.wait_ge(vt2_ready, 5 + p)
                    pe.matmul(bank[4 + p][:, :], w2g[:, p * P:(p + 1) * P], small[:, :], start=True,
                              stop=True).then_inc(z_mm, 1)
                inner(17, 8)

                def gate(n):
                    u, t = UNIT0["in2"] + 25 + n, t0 + 25 + n
                    split_unit(u)
                    free_bank(t)
                    for k in range(KT):
                        ins = product(bank[t % 4][:, :], u % SLOTS, k, acth[:, k, :], actl[:, k, :], k == 0, k == KT - 1)
                    ins.then_inc(units_used, 1)

                def chunk_kv(c):
                    if c >= 4:
                        pe.wait_ge(kv_ready, c - 3)
                    r = slice(64 * (c % 2), 64 * (c % 2) + 64)
                    for p in range(2):
                        ins = pe.matmul(bank[4 + c % 4][:, p * 256:(p + 1) * 256], ket[r, c // 2, p * P:(p + 1) * P],
                                        gvt[r, c // 2, p * 256:(p + 1) * 256], start=True, stop=True)
                    ins.then_inc(kv_mm, 1)

                def fox_sum(j):
                    pe.wait_ge(sq_ready, plan("fox_norm", "sq") + j + 1)
                    if j >= 2:
                        pe.wait_ge(frs_ready, j - 1)
                    pe.matmul(bank[6 + j % 2][:, :], blk64, sq[:, j % 2, :], start=True, stop=True).then_inc(sq_used, 1)

                def gla_scores(h):
                    r, p = slice(64 * (h % 2), 64 * (h % 2) + 64), h // 2
                    if h >= 2:
                        pe.wait_ge(gla_scale, h - 1)
                    for tt in range(4):
                        t_ = slice(tt * P, (tt + 1) * P)
                        ins = pe.matmul(bank[4 + h % 2][:, t_], gqk[r, 2 + p, t_], gqk[r, p, t_], start=True, stop=True)
                    ins.then_inc(gs_mm, 1)

                def gla_head(h):
                    r, p = slice(64 * (h % 2), 64 * (h % 2) + 64), h // 2
                    if h >= 2:
                        pe.wait_ge(gla_done, h - 1)
                    pe.wait_ge(gs_ready, h + 1)
                    o = bank[6 + h % 2]
                    for tt in range(4):
                        pe.matmul(o[:, tt * P:(tt + 1) * P], gvt[:, tt, h * P:(h + 1) * P],
                                  sct[:, h % 2, tt * P:(tt + 1) * P], start=(tt == 0), stop=False)
                    for c in range(1, NCH):
                        ins = pe.matmul(o[:, c * CH:(c + 1) * CH], states[r, c - 1, p, :],
                                        gqk[r, p, c * CH:(c + 1) * CH], start=False, stop=(c == NCH - 1))
                    ins.then_inc(go_mm, 1)

                def gla_sum(h):
                    pe.wait_ge(sq_ready, plan("gla", "sq") + h + 1)
                    pe.matmul(bank[4 + h % 2][:, :], ones, sq[:, h % 2, :], start=True, stop=True).then_inc(sq_used, 1)

                gate(0)
                gate(1)
                pe.wait_ge(qk_ready, 1)
                pe.wait_ge(vt2_ready, 8)
                for b in range(2):
                    for tt in range(2):
                        for p in range(2):
                            ins = pe.transpose(bank[6 + b][:, tt * 256 + p * P:tt * 256 + (p + 1) * P],
                                               gqk[:, 2 + p, (2 * b + tt) * P:(2 * b + tt + 1) * P], ident)
                    ins.then_inc(ket_mm, 1)
                gate(2)
                pe.wait_ge(ket_ready, 2)
                pe.wait_ge(z_ready, 2)
                for c in range(4):
                    chunk_kv(c)
                gate(3)
                for c in range(4, NCH - 1):
                    chunk_kv(c)
                gate(4)
                pe.wait_ge(kv_ready, NCH - 1)
                for j in range(0, 8, 2):
                    fox_sum(j)
                    fox_sum(j + 1)
                    gate(5 + j // 2)
                pe.wait_ge(frs_ready, 8)
                gla_scores(0)
                gate(9)
                for h in range(4):
                    gla_head(h)
                    if h < 3:
                        gla_scores(h + 1)
                    gate(10 + h)
                    gla_sum(h)
                gate(14)
                gate(15)

                def fox_scores(h):
                    r, p = slice(64 * (h % 2), 64 * (h % 2) + 64), h // 2
                    for qt in range(4):
                        b, o = ((4, 0), (4, P), (5, 0), (6, 0))[qt]
                        n = (qt + 1) * P
                        pe.matmul(bank[b][:, o:o + n], fq[r, p, qt * P:n], fk[r, p, 0:n], start=True, stop=False)
                        pe.matmul(bank[b][:, o:o + n], hyb[:, T + 2 * P + h * P:T + 3 * P + h * P], small[:, 0:n],
                                  start=False, stop=False)
                        ins = pe.matmul(bank[b][:, o + qt * P:o + n], ident, fmask, start=False, stop=True)
                    ins.then_inc(fs_mm, 1)

                pe.wait_ge(fox_scaled, 8)
                pe.wait_ge(gla_scale, 4)
                pe.wait_ge(gla_done, 4)
                pe.wait_ge(evacuated, t0 + 41 + UC)
                fox_scores(0)
                pe.wait_ge(f_exp, 1)
                fox_scores(1)
                for h in range(8):
                    p = h // 2
                    pe.wait_ge(fp_ready, h + 1)
                    if h:
                        pe.wait_ge(fpt_v, h)
                        pe.wait_ge(fpt_a, h)
                    for kt in range(4):
                        for qt in range(kt, 4):
                            b, o = ((0, 0), (1, 0), (2, 0), (2, 256))[kt]
                            ins = pe.transpose(bank[b][:, o + (qt - kt) * P:o + (qt - kt + 1) * P],
                                               fp[:, h % 2, FOX_OFF[qt] + kt * P:FOX_OFF[qt] + (kt + 1) * P], ident)
                    ins.then_inc(fpt_mm, 1)
                    if h < 6:
                        pe.wait_ge(f_exp, h + 2)
                        fox_scores(h + 2)
                    pe.wait_ge(fpt_v, h + 1)
                    pe.wait_ge(fpt_a, h + 1)
                    if h >= 2:
                        pe.wait_ge(fo_a, h - 1)
                    for kt in range(4):
                        n = (4 - kt) * P
                        ins = pe.matmul(bank[3 + 4 * (h % 2)][:, kt * P:T], fvt[:, kt, p * P:(p + 1) * P],
                                        fpt[:, h % 2, FOX_TOFF[kt]:FOX_TOFF[kt] + n], start=(kt == 0), stop=(kt == 3))
                    ins.then_inc(fo_mm, 1)
                pe.wait_ge(fo_a, 8)
                u0, t0 = UNIT0["branch"], plan("branch", "tile")
                with pe.Fori(0, 2) as i:
                    for s in range(4):
                        split_unit(i * 4 + (u0 + s))
                        for b, source in enumerate(("gla", "fox")):
                            free_bank(i * 8 + (t0 + 2 * s + b))
                            for k in range(4):
                                if s == 0:
                                    part(source, k)
                                ins = product(bank[(t0 + 2 * s + b) % 4][:, :], (u0 + s) % SLOTS, 4 * b + k,
                                              acth[:, 4 * b + k, :], actl[:, 4 * b + k, :], k == 0, k == 3)
                            ins.then_inc(units_used if b else tile_full, 1)
                dense("out2", "branch", yh, yl)

            def ffn2():
                norm_sum("norm_ffn2")
                dense("up2", "norm_ffn2", acth, actl)
                down("down2", "up2", hidh, hidl)

            def last_norm():
                norm_sum("last")

            memory_side(0)
            attention(0)
            ffn(0)
            convolution()
            attention(1)
            ffn(1)
            final_norm()
            hybrid()
            ffn2()
            last_norm()

        @block.scalar
        def _(act):
            act.sem_inc(evacuated, UC)
            act.sem_inc(post_a, POST_A)
            chain = Chain(act, act_chain)

            def hold():
                act.sem_inc(act_held, 1)

            def square(stage, source, n=T, ready=None):
                with act.Fori(0, KT // 2) as i:
                    for s in range(2):
                        if ready:
                            ready(i * 2 + s)
                        act.wait_ge(sq_used, i * 2 + (plan(stage, "sq") + s + 1))
                        hold()
                        act.activation(sq[:, s, 0:n], source(i * 2 + s), ACT.Square).then_inc(sq_ready, 1)

            def rsqrt(stage, bias, n=T):
                act.wait_ge(sq_used, plan(stage, "sq") + KT + SC)
                chain.step(act.activation(rstd[:, 0:n], bank[4][:, 0:n], ACT.Ln, bias=bias, scale=1.0 / D))
                chain.wait()
                act.activation(rstd[:, 0:n], rstd[:, 0:n], ACT.Exp, scale=-0.5).then_inc(rstd_ready, 1)

            def x_is_ready(stage):
                return lambda k: act.wait_ge(x_ready, k + (plan(stage, "x") + 1 + SC))

            def high_part(stage, to, n=T, count=KT, before=None):
                g0, v0 = plan(stage, "split"), plan(stage, "val")
                if before:
                    before()
                with act.Fori(0, count // 2) as i:
                    for s in range(2):
                        act.wait_ge(val_ready, i * 2 + (v0 + s + 1))
                        hold()
                        act.activation(to[:, i * 2 + s, 0:n], tmp[:, (g0 + s) % 2, 0:n],
                                       ACT.Identity).then_inc(hi_ready, 1)

            def bank_of(t):
                return bank[t % 4]

            def tile_seq(name):
                u0, t0 = UNIT0[name], plan(name, "tile")
                with act.Fori(0, 2) as i:
                    for s in range(4):
                        act.wait_ge(units_used, i * 4 + (u0 + s + 1 + UC))
                        hold()
                        act.activation(seq[name][:, bass.ds(i * 8, 8), s, :],
                                       bank_of(t0 + s)[:, :].rearrange("p (c t) -> p c t", t=CH),
                                       ACT.Identity).then_inc(evacuated, 1)

            def deltas(stage, buf, last_units, bias=None):
                t0, x0 = plan(stage, "tile"), plan(stage, "x")
                per = last_units
                with act.Fori(0, 2) as i:
                    for s in range(4):
                        act.wait_ge(units_used, i * (4 * per) + (UNIT0[stage] + (s + 1) * per + UC))
                        act.wait_ge(x_ready, i * 4 + (x0 + s + 1))
                        hold()
                        act.activation(buf[:, s % 2, :], bank_of(t0 + s)[:, :], ACT.Identity,
                                       bias=bias(i * 4 + s) if bias else 0.0).then_inc(evacuated, 1)

            act.wait_ge(x_in, 16)
            square("norm0", lambda k: xt[:, k, 1:T + 1])
            act.wait_ge(omu_ready, 1)
            rsqrt("norm0", b_eps)
            high_part("mixw", mixh[0])
            high_part("mixa", mixh[1])

            def reuse(stage):
                return lambda: act.wait_ge(units_used, UNIT0[stage] + dict(STREAM)[stage] + UC)

            high_part("mixg", mixh[0], before=reuse("lora_in"))
            g = plan("mid", "split")
            act.wait_ge(tile_full, 1)
            act.wait_ge(lo_ready, g + 1)
            act.activation(tmp[0:64, g % 2, :], bank[0][0:64, :], ACT.Tanh).then_inc(evacuated, 1)
            act.wait_ge(units_used, 1 + UC)
            act.activation(tmp[64:P, g % 2, :], bank[1][64:P, :], ACT.Identity).then_inc(evacuated, 1)
            act.wait_ge(evacuated, 2 + UC)
            act.activation(midh[:, :], tmp[:, g % 2, :], ACT.Identity).then_inc(hi_ready, 1)
            high_part("mixk", mixh[1], before=reuse("lora_in"))
            g = plan("gmid", "split")
            for j in range(2):
                act.wait_ge(units_used, 2 + j + UC)
                act.wait_ge(lo_ready, g + j + 1)
                act.activation(tmp[:, (g + j) % 2, :], bank[2 + j][:, :], ACT.Sigmoid).then_inc(evacuated, 1)
                act.wait_ge(evacuated, 3 + j + UC)
                act.activation(gmidh[:, j, :], tmp[:, (g + j) % 2, :], ACT.Identity).then_inc(hi_ready, 1)
            for stage, bias, to, full in (("w2", "w0", "w", 2), ("a2", "a0", "a", 9)):
                for j in range(KT):
                    if j < KT - 1:
                        act.wait_ge(tile_full, full + j)
                    else:
                        act.wait_ge(units_used, UNIT0[stage] + 1 + UC)
                    half, q = divmod(j, 4)
                    act.activation(seq[to][:, 8 * half:8 * half + 8, q, :],
                                   bank_of(plan(stage, "tile") + j)[:, :].rearrange("p (c t) -> p c t", t=CH),
                                   ACT.Sigmoid, bias=pc(bias, j)).then_inc(evacuated, 1)
            high_part("mixr", mixh[0], before=reuse("gate_in"))
            tile_seq("k")
            high_part("mixv", mixh[1], before=reuse("k"))
            tile_seq("r")

            def knorm_square(j):
                half, q = divmod(j, 4)
                act.wait_ge(sq_used, plan("knorm", "sq") + j + 1)
                act.activation(sq[:, j % 2, :].rearrange("p (c t) -> p c t", t=CH),
                               seq["k"][:, 8 * half:8 * half + 8, q, :], ACT.Square,
                               scale=pc("k_k", j)).then_inc(sq_ready, 1)

            act.wait_ge(evacuated, plan("r", "tile") + 8 + UC)
            knorm_square(0)
            for j in range(KT):
                if j + 1 < KT:
                    knorm_square(j + 1)
                act.wait_ge(kss_ready, j + 1)
                chain.step(act.activation(rn[:, j, :], rn[:, j, :], ACT.Ln))
                chain.wait()
                act.activation(rn[:, j, :], rn[:, j, :], ACT.Exp, bias=b_rn, scale=-0.5).then_inc(rn_ready, 1)
            assert plan("v", "tile") % 4 == 0
            for half in range(2):
                with act.Fori(0, 2) as i:
                    for s in range(2):
                        act.wait_ge(units_used, i * 2 + (UNIT0["v"] + 4 * half + s + 1 + UC))
                        hold()
                        act.activation(seq["v"][:, 8 * half:8 * half + 8, i * 2 + s, :],
                                       psum[:, i * 2 + s, :].rearrange("p (c t) -> p c t", t=CH),
                                       ACT.Identity).then_inc(evacuated, 1)
                    for s in range(2):
                        act.wait_ge(scan_ready, i * 2 + (4 * half + s + 1))
                        act.activation(pp[:, s, :], cs[:, s, :], ACT.Exp, scale=-RSQRT_E)
                        act.activation(pi[:, s, :], cs[:, s, :], ACT.Exp, scale=RSQRT_E)
                        w_ = seq["w"][:, 8 * half:8 * half + 8, i * 2 + s, :]
                        act.activation(w_, w_, ACT.Exp, scale=-RSQRT_E).then_inc(decay_ready, 1)
            act.wait_ge(prep_done, 4 + 1)
            act.dma_start(c_core[:, :], dram["c_core"]).then_inc(ccore_in, 16)

            act.sem_inc(core_a, NCA)

            def two(ap):
                return ap.rearrange("p (q t) -> p q t", q=2)

            def core_load(r, ahead):
                act.wait_ge(core_pe, count(r, NCPE, NCPE))
                if ahead:
                    act.wait_ge(pro_pe, count(r, NPPE, NPPE))
                hold()
                it, c = index(r, ahead), (parity(r) + ahead) % 2
                for h in range(2):
                    p = slice(64 * h, 64 * h + 64)
                    act.activation(BB[p, :, p], seq["a"][p, it, :, :], ACT.Identity)
                    act.activation(VB[p, :, p], seq["v"][p, it, :, :], ACT.Identity)
                act.activation(AR[c][:, :, P:192], seq["r"][:, it, :, :], ACT.Identity).then_inc(pro_a, 1)

            def core_prepared(r, ahead, what, groups=(0, 1)):
                c = (parity(r) + ahead) % 2
                for g in groups:
                    b = bank[4 * g + 3]
                    if what == "V":
                        act.wait_ge(pro_pe, count(r, NPPE, ahead * NPPE + PPE["N"] + g))
                        act.wait_ge(pro_v, count(r, NPV, ahead * NPV + PV["N"] + g))
                        act.activation(VT[c][:, 2 * g:2 * g + 2, :], two(b[:, 256:512]), ACT.Identity).then_inc(pro_a, 1)
                    else:
                        act.wait_ge(pro_pe, count(r, NPPE, ahead * NPPE + PPE["T"] + g))
                        act.activation(TBK[c][:, 2 * g:2 * g + 2, :], two(b), ACT.Identity).then_inc(pro_a, 1)

            def core_round(r, last=False):
                c, n = parity(r), 1 - parity(r)

                def pe_step(what, g):
                    act.wait_ge(core_pe, count(r, NCPE, NCPE + CPE[what] + g))

                for g in range(2):
                    pe_step("M2", g)
                    act.activation(TMA[:, 2 * g:2 * g + 2, P:384], two(bank[4 * g + c]), ACT.Identity).then_inc(core_a, 1)
                for g in range(2):
                    pe_step("M4", g)
                    act.activation(TMA[:, 2 * g:2 * g + 2, P:256], two(bank[4 * g + n])[:, :, P:256], ACT.Identity)
                    act.activation(TMA[:, 2 * g:2 * g + 2, 256:384], two(bank[4 * g + 2][:, 0:256]),
                                   ACT.Identity).then_inc(core_a, 1)
                if not last:
                    core_load(r, 1)
                for g in range(2):
                    pe_step("M8", g)
                    act.activation(TMA[:, 2 * g:2 * g + 2, 256:384], two(bank[4 * g + c])[:, :, P:256],
                                   ACT.Identity).then_inc(core_a, 1)
                for g in range(2):
                    pe_step("TT", g)
                    act.activation(TZ[:, 2 * g:2 * g + 2, :], two(bank[4 * g + 2]), ACT.Identity).then_inc(core_a, 1)
                if not last:
                    core_prepared(r, 1, "V", [0])
                for what, to, b in (("Z", TZ[:, :, P:256], n), ("X", XX, 2)):
                    for g in range(2):
                        pe_step(what, g)
                        act.activation(to[:, 2 * g:2 * g + 2, :], two(bank[4 * g + b][:, 0:256]),
                                       ACT.Identity).then_inc(core_a, 1)
                    if what == "Z" and not last:
                        core_prepared(r, 1, "V", [1])
                if not last:
                    core_prepared(r, 1, "T")
                for g in range(2):
                    pe_step("U", g)
                    act.activation(UU[:, 2 * g:2 * g + 2, :], two(bank[4 * g + n][:, 0:256]),
                                   ACT.Identity).then_inc(core_a, 1)
                for g in range(2):
                    pe_step("Y", g)
                    hold()
                    act.activation(seq["r"][:, index(r), 2 * g:2 * g + 2, :], two(bank[4 * g + 2][:, 0:P]),
                                   ACT.Identity).then_inc(core_a, 1)

            act.wait_ge(core_clear, 1)
            core_load(0, 0)
            core_prepared(0, 0, "V")
            core_prepared(0, 0, "T")
            with act.Fori(0, 7) as i:
                core_round((i, 0))
                core_round((i, 1))
            core_round(14)
            core_round(15, last=True)

            act.wait_ge(core_v, NCV * 17)
            act.wait_ge(core_a, NCA * 17)
            act.wait_ge(core_pe, NCPE * 17)
            act.dma_start(xt[:, :, 1:T + 1], dram["x"]).then_inc(xagain_in, 16)
            act.dma_start(c_post[:, :, :], dram["c_post"].rearrange("p (k m) -> p k m", k=4)).then_inc(cpost_in, 16)
            for j in range(KT):
                if j % 4 == 3:
                    act.wait_ge(units_used, UNIT0["g2"] + j // 4 + 1 + UC)
                else:
                    act.wait_ge(tile_full, 16 + 3 * (j // 4) + j % 4)
                act.activation(g_all[:, j, :], bank_of(plan("g2", "tile") + j)[:, :],
                               ACT.Identity).then_inc(evacuated, 1)
            g0, v0 = plan("post", "split"), plan("post", "val")

            def post_high(k):
                for s in range(2):
                    act.wait_ge(val_ready, v0 + k + s + 1)
                    act.activation(acth[:, k + s, :], tmp[:, (g0 + s) % 2, :], ACT.Identity).then_inc(hi_ready, 1)

            for k in range(0, KT, 2):
                for s in range(2):
                    act.wait_ge(post_v, k + s + 1 + SC)
                    act.wait_ge(post_pe, 2 * k)if k else None
                    act.activation(sq[:, s, :], yc[:, s, :], ACT.Square).then_inc(post_a, 1)
                for s in range(2):
                    act.wait_ge(post_pe, 2 * k + 3 + s)
                    chain.step(act.activation(grs[:, s, :], bank[4 + s][:, :], ACT.Ln, bias=b_gn, scale=1.0 / CH))
                    chain.wait()
                    act.activation(grs[:, s, :], grs[:, s, :], ACT.Exp, scale=-0.5).then_inc(post_a, 1)
                post_high(k)
            deltas("o", delta0, 1)


            def evac(stage, to, func=ACT.Identity, n=T, count=None, skip=0, bias=None):
                u0, t0 = UNIT0[stage] + skip, plan(stage, "tile") + skip
                with act.Fori(0, (count or dict(STREAM)[stage]) // 4) as i:
                    for s in range(4):
                        act.wait_ge(units_used, i * 4 + (u0 + s + 1 + UC))
                        hold()
                        act.activation(to(i * 4 + skip + s), bank_of(t0 + s)[:, 0:n], func).then_inc(evacuated, 1)

            def memory_norm(l):
                stage = f"norm_mem{l}"
                square(stage, lambda k: mem[:, k, :], MEM)
                rsqrt(stage, b_eps, MEM)
                high_part(stage, memh, MEM)

            def stream_norm(l):
                stage = f"norm_x{l}"
                square(stage, x, ready=x_is_ready("o" if l == 0 else "cout"))
                rsqrt(stage, b_eps)
                high_part(stage, acth)

            def memory_side(l):
                if l == 0:
                    act.dma_start(mem[:, :, :], dram["mem"]).then_inc(mem_in[l], 16)
                    act.wait_ge(mem_in[l], 16)
                    memory_norm(l)
                evac(f"kv{l}", lambda k: keys[:, k, :], n=MEM, count=4)
                if l == 0:
                    stream_norm(l)
                evac(f"kv{l}", lambda k: keys[:, k, :], n=MEM, count=4, skip=4)
                evac(f"kv{l}", lambda k: vals[:, k - 8, :], n=MEM, count=8, skip=8)
                for j in range(4):
                    act.wait_ge(vt_mm, 4 * l + j + 1)
                    act.activation(vtok[:, j // 2, (j % 2) * T:(j % 2 + 1) * T], bank[4 + j],
                                   ACT.Identity).then_inc(vt_ready, 1)

            def attention(l):
                if l == 1:
                    stream_norm(l)
                def exps(h):
                    act.wait_ge(smax_ready, 4 * l + h + 1)
                    for tt in range(4):
                        ins = act.activation(prob[:, h % 2, tt, :],
                                             bank[4 + tt // 2][:, (tt % 2) * MEM:(tt % 2 + 1) * MEM], ACT.Exp,
                                             bias=snegm[:, h, tt:tt + 1], scale=1.0 / 16,
                                             accum_out=ssum[:, h, tt:tt + 1])
                    ins.then_inc(p_exp, 1)

                evac(f"q{l}", lambda k: query[:, k, :], count=4)
                exps(0)
                evac(f"q{l}", lambda k: query[:, k, :], count=4, skip=4)
                exps(1)
                g0 = plan(f"heads{l}", "split")
                for h in range(4):
                    act.wait_ge(pt_mm, 4 * l + h + 1)
                    act.activation(probt[:, h % 2, 1, :], bank[7], ACT.Identity).then_inc(pt_a, 1)
                    if h < 2:
                        exps(h + 2)
                    for j in range(2 * h, 2 * h + 2):
                        t = plan(f"heads{l}", "tile") + j
                        act.wait_ge(tile_full, plan(f"heads{l}", "full") + j + 1)
                        act.wait_ge(lo_ready, g0 + j + 1)
                        act.activation(tmp[:, (g0 + j) % 2, :], bank_of(t), ACT.Identity).then_inc(evacuated, 1)
                        act.wait_ge(evacuated, t + 1 + UC)
                        act.activation(acth[:, j, :], tmp[:, (g0 + j) % 2, :], ACT.Identity).then_inc(hi_ready, 1)
                deltas(f"xo{l}", delta1, 1)

            def ffn(l):
                stage = f"norm_ffn{l}"
                square(stage, x, ready=x_is_ready(f"xo{l}"))
                rsqrt(stage, b_eps)
                high_part(stage, acth)
                u0, t0, c0 = UNIT0[f"up{l}"], plan(f"up{l}", "tile"), plan(f"up{l}", "conv")
                g0, v0 = plan(f"up{l}", "split"), plan(f"up{l}", "val")
                act.wait_ge(pad_ready, l + 1)
                with act.Fori(0, FT // 2) as i:
                    for s in range(4):
                        act.wait_ge(units_used, i * 4 + (u0 + s + 1 + UC))
                        act.wait_ge(conv_ready, i * 4 + (c0 + s + 1))
                        act.activation(cu[:, s, 2:T + 2], bank_of(t0 + s), ACT.Identity).then_inc(evacuated, 1)
                    for s in range(2):
                        act.wait_ge(conv_ready, i * 4 + (c0 + 2 * s + 1 + UC))
                        act.activation(sg[:, s, :], cg[:, s, :], ACT.Silu).then_inc(gate_ready, 1)
                    for s in range(2):
                        act.wait_ge(val_ready, i * 2 + (v0 + s + 1))
                        hold()
                        act.activation(hidh[:, i * 2 + s, :], tmp[:, (g0 + s) % 2, :],
                                       ACT.Identity).then_inc(hi_ready, 1)
                deltas(f"down{l}", delta2, 3)

            def convolution():
                act.wait_ge(x_ready, plan("down0", "x") + KT + SC)
                act.dma_start(mem[:, :, :], dram["mem"]).then_inc(mem_in[1], 16)
                square("norm_conv", x, ready=x_is_ready("down0"))
                rsqrt("norm_conv", b_eps)
                high_part("norm_conv", acth)

                def gated(first, rounds):
                    u0, t0 = UNIT0["cin"] + 4 * first, plan("cin", "tile")
                    with act.Fori(0, rounds) as i:
                        for s in range(4):
                            k = i * 2 + (2 * first + s // 2)
                            act.wait_ge(units_used, i * 4 + (u0 + s + 1 + UC))
                            hold()
                            if s % 2:
                                ins = act.activation(glu[:, k, :], bank_of(t0 + s), ACT.Sigmoid,
                                                     bias=pc("conv_b_in", k + KT))
                            else:
                                ins = act.activation(gp[:, k, CONVW - 1:], bank_of(t0 + s), ACT.Identity,
                                                     bias=pc("conv_b_in", k))
                            ins.then_inc(evacuated, 1)

                gated(0, 1)
                act.wait_ge(mem_in[1], 16)
                memory_norm(1)
                gated(1, 3)
                memory_side(1)
                square("ln", lambda k: ub[:, k, :], ready=lambda k: act.wait_ge(uc_ready, k + 1))
                rsqrt("ln", b_ln)
                g0 = plan("ln", "split")
                with act.Fori(0, KT // 2) as i:
                    for s in range(2):
                        act.wait_ge(lo_ready, i * 2 + (g0 + s + 1))
                        act.wait_ge(uc_ready, i * 2 + (KT + s + 1))
                        hold()
                        chain.enter(i, 2) if s == 0 else None
                        chain.step(act.activation(tmp[:, (g0 + s) % 2, :], ub[:, i * 2 + s, :], ACT.Silu,
                                                  bias=pc("conv_ln_b", i * 2 + s)))
                    for s in range(2):
                        chain.wait(1 - s)
                        hold()
                        act.activation(acth[:, i * 2 + s, :], tmp[:, (g0 + s) % 2, :],
                                       ACT.Identity).then_inc(hi_ready, 1)
                    chain.leave(KT // 2, 2)
                deltas("cout", delta3, 1, bias=lambda k: pc("conv_b_out", k))

            def final_norm():
                square("final", x, ready=x_is_ready("down1"))
                rsqrt("final", b_eps)

            def hybrid():
                act.wait_ge(x_ready, plan("down1", "x") + KT + SC)
                act.dma_start(hyb[:, :], dram["c_hybrid"]).then_inc(hyb_in, 16)
                act.dma_start(w2g[:, :], dram["w2g"]).then_inc(hyb_in, 16)
                square("norm_h", x, ready=x_is_ready("final"))
                rsqrt("norm_h", b_eps)
                high_part("norm_h", acth)
                t0 = plan("in2", "tile")
                act.wait_ge(units_used, UNIT0["in2"] + 1 + UC)
                act.activation(small[:, :], bank_of(t0), ACT.Identity).then_inc(evacuated, 1)

                def inner(to, skip, n, **k):
                    evac("in2", lambda j: to(j - skip), count=n, skip=skip, **k)

                inner(lambda k: gv[:, k, :], 1, 4)
                inner(lambda k: fv[:, k, :], 5, 4)
                inner(lambda k: gqk[:, k, :], 9, 4)
                for j in range(8):
                    act.wait_ge(vt2_mm, j + 1)
                    act.activation((gvt if j < 4 else fvt)[:, j % 4, :], bank[4 + j % 4],
                                   ACT.Identity).then_inc(vt2_ready, 1)
                inner(lambda k: gr[:, k, :], 13, 4, func=ACT.Silu)
                act.wait_ge(vt2_ready, 8)
                act.activation(ls[:, 2, :], small[:, :], ACT.Identity, bias=pc("fox_fb"))
                for p in range(2):
                    act.wait_ge(z_mm, p + 1)
                    act.activation(ls[:, p, :], bank[4 + p], ACT.Identity, bias=pc("gla_b", p)).then_inc(z_ready, 1)
                act.wait_ge(z_ready, 2)
                chain.step(act.activation(le[:, :, :], ls[:, :, :], ACT.Abs))
                chain.wait()
                chain.step(act.activation(le[:, :, :], le[:, :, :], ACT.Exp, scale=-1.0))
                chain.wait()
                act.activation(le[:, :, :], le[:, :, :], ACT.Ln, bias=ones[:, 0:1]).then_inc(log_ready, 1)
                inner(lambda k: fq[:, k, :], 17, 4)
                act.wait_ge(cum_ready, 1)
                act.activation(eb[:, :, :], ls[:, 0:2, :], ACT.Exp, scale=1.0 / 16)
                act.activation(enb[:, :, :], ls[:, 0:2, :], ACT.Exp, scale=-1.0 / 16).then_inc(eb_ready, 1)
                inner(lambda k: fk[:, k, :], 21, 4)

                def gate(n):
                    act.wait_ge(units_used, UNIT0["in2"] + 25 + n + 1 + UC)
                    act.activation((gate_b if n // KT else gate_a)[:, n % KT, :], bank_of(t0 + 25 + n), ACT.Sigmoid,
                                   bias=pc("gate_b_2", n)).then_inc(evacuated, 1)

                def fox_square(j):
                    act.wait_ge(sq_used, plan("fox_norm", "sq") + j + 1)
                    act.activation(sq[:, j % 2, :], (fq if j < 4 else fk)[:, j % 4, :],
                                   ACT.Square).then_inc(sq_ready, 1)

                def fox_rms(j):
                    act.wait_ge(sq_used, plan("fox_norm", "sq") + j + 1 + SC)
                    if j >= 2:
                        act.wait_ge(fox_scaled, j - 1)
                    chain.step(act.activation(frs[:, j % 2, :], bank[6 + j % 2], ACT.Ln, bias=b_eps, scale=1.0 / 64))
                    chain.wait()
                    act.activation(frs[:, j % 2, :], frs[:, j % 2, :], ACT.Exp, bias=b_q if j < 4 else 0.0,
                                   scale=-0.5).then_inc(frs_ready, 1)

                def gla_square(h):
                    act.wait_ge(sq_used, plan("gla", "sq") + h + 1)
                    act.wait_ge(go_mm, h + 1)
                    act.activation(sq[:, h % 2, :], bank[6 + h % 2], ACT.Square).then_inc(sq_ready, 1)

                def gla_rms(h):
                    act.wait_ge(sq_used, plan("gla", "sq") + h + 1 + SC)
                    if h >= 2:
                        act.wait_ge(gla_done, h - 1)
                    chain.step(act.activation(frs[:, h % 2, :], bank[4 + h % 2], ACT.Ln, bias=b_eps, scale=1.0 / P))
                    chain.wait()
                    act.activation(frs[:, h % 2, :], frs[:, h % 2, :], ACT.Exp, scale=-0.5).then_inc(gla_scale, 1)

                gate(0)
                gate(1)
                for b in range(2):
                    act.wait_ge(ket_mm, b + 1)
                    act.activation(ket[:, 2 * b:2 * b + 2, :], bank[6 + b].rearrange("p (a m) -> p a m", a=2),
                                   ACT.Identity).then_inc(ket_ready, 1)
                gate(2)
                act.wait_ge(evacuated, t0 + 25 + UC)
                fox_square(0)
                fox_square(1)
                gate(3)
                act.wait_ge(qk_ready, 1)
                for j in range(0, 8, 2):
                    gate(4 + j // 2)
                    for s in range(2):
                        fox_rms(j + s)
                    if j < 6:
                        for s in range(2, 4):
                            fox_square(j + s)
                gate(8)
                act.wait_ge(fox_scaled, 8)
                gate(9)
                for h in range(4):
                    gla_square(h)
                    gate(10 + h)
                    gla_rms(h)
                gate(14)
                gate(15)
                act.wait_ge(gla_done, 4)
                for h in range(4):
                    act.activation(acth[:, h, :], gr[:, h, :], ACT.Identity).then_inc(hi_ready, 1)

                def fox_exps(h):
                    act.wait_ge(fmax_ready, h + 1)
                    if h >= 2:
                        act.wait_ge(fpt_mm, h - 1)
                    for qt in range(4):
                        b, o = ((4, 0), (4, P), (5, 0), (6, 0))[qt]
                        n = (qt + 1) * P
                        ins = act.activation(fp[:, h % 2, FOX_OFF[qt]:FOX_OFF[qt] + n], bank[b][:, o:o + n], ACT.Exp,
                                             bias=fneg[:, h, qt:qt + 1], accum_out=fsum[:, h, qt:qt + 1])
                    ins.then_inc(f_exp, 1)

                fox_exps(0)
                fox_exps(1)
                g0 = plan("fox", "split")
                for h in range(8):
                    act.wait_ge(fpt_mm, h + 1)
                    act.activation(fpt[:, h % 2, 4 * P:7 * P], bank[1][:, 0:3 * P], ACT.Identity)
                    act.activation(fpt[:, h % 2, 7 * P:10 * P], bank[2][:, 0:3 * P], ACT.Identity).then_inc(fpt_a, 1)
                    if h < 6:
                        fox_exps(h + 2)
                    r, p = slice(64 * (h % 2), 64 * (h % 2) + 64), h // 2
                    act.wait_ge(fo_mm, h + 1)
                    act.wait_ge(lo_ready, g0 + p + 1)
                    act.activation(tmp[r, (g0 + p) % 2, :], bank[3 + 4 * (h % 2)][r, :],
                                   ACT.Identity).then_inc(fo_a, 1)
                    if h % 2:
                        act.wait_ge(fo_a, h + 1)
                        act.activation(acth[:, 4 + p, :], tmp[:, (g0 + p) % 2, :], ACT.Identity).then_inc(hi_ready, 1)
                high_part("branch", yh)
                deltas("out2", delta4, 1)

            def ffn2():
                square("norm_ffn2", x, ready=x_is_ready("out2"))
                rsqrt("norm_ffn2", b_eps)
                high_part("norm_ffn2", acth)
                u0, t0, c0 = UNIT0["up2"], plan("up2", "tile"), plan("up2", "conv")
                g0, v0 = plan("up2", "split"), plan("up2", "val")
                act.wait_ge(pad_ready, 3)
                with act.Fori(0, FT // 2) as i:
                    for s in range(4):
                        act.wait_ge(units_used, i * 4 + (u0 + s + 1 + UC))
                        if s % 2:
                            act.wait_ge(val_ready, i * 2 + (v0 - 1 + s // 2))
                        else:
                            act.wait_ge(conv_ready, i * 2 + (c0 + s // 2 + 1 + UC - 2))
                        act.activation(cu[:, s, 2:T + 2], bank_of(t0 + s), ACT.Identity).then_inc(evacuated, 1)
                    for s in range(2):
                        act.wait_ge(conv_ready, i * 2 + (c0 + s + 1 + UC))
                        act.activation(sg[:, s, :], cg[:, s, :], ACT.Gelu_apprx_tanh).then_inc(gate_ready, 1)
                    for s in range(2):
                        act.wait_ge(val_ready, i * 2 + (v0 + s + 1))
                        hold()
                        act.activation(hidh[:, i * 2 + s, :], tmp[:, (g0 + s) % 2, :],
                                       ACT.Identity).then_inc(hi_ready, 1)
                deltas("down2", delta2, 3)

            def last_norm():
                square("last", x, ready=x_is_ready("down2"))
                rsqrt("last", b_eps)
                for k in range(0, KT, 2):
                    act.wait_ge(x_ready, plan("last", "x") + k + 2 + SC)
                    act.dma_start(dram["out"][:, k:k + 2, :], xt[:, k:k + 2, 1:T + 1]).then_inc(out_in, 16)
                act.wait_ge(out_in, 16 * (KT // 2))

            memory_side(0)
            attention(0)
            ffn(0)
            convolution()
            attention(1)
            ffn(1)
            final_norm()
            hybrid()
            ffn2()
            last_norm()

        @block.vector
        def _(dve):
            dve.sem_inc(x_ready, SC)
            dve.sem_inc(lo_ready, SC)
            dve.sem_inc(prep_done, 1)
            dve.sem_inc(conv_ready, UC)
            dve.sem_inc(post_v, SC)
            chain = Chain(dve, dve_chain)
            mul, add, sub = ALU.mult, ALU.add, ALU.subtract

            def bank_of(t):
                return bank[t % 4]

            def lows(stage, h, l, i, n=T):
                g = plan(stage, "split")
                for s in range(2):
                    dve.wait_ge(hi_ready, i * 2 + (g + s + 1))
                    dve.tensor_tensor(l[:, i * 2 + s, 0:n], tmp[:, (g + s) % 2, 0:n],
                                      h[:, i * 2 + s, 0:n].bitcast(F32), sub).then_inc(lo_ready, 1)

            def normed(stage, source, gain, h=None, l=None, n=T):
                dve.wait_ge(rstd_ready, plan(stage, "rstd") + 1)
                with dve.Fori(0, KT // 2) as i:
                    for s in range(2):
                        dve.wait_ge(lo_ready, i * 2 + (plan(stage, "split") + s + 1))
                        dve.scalar_tensor_tensor(
                            out=tmp[:, (plan(stage, "split") + s) % 2, 0:n], in0=source(i * 2 + s),
                            scalar=gain(i * 2 + s), in1=rstd[:, 0:n], op0=mul, op1=mul).then_inc(val_ready, 1)
                    lows(stage, h or acth, l or actl, i, n)

            def residual(stage, buf):
                t0, x0 = plan(stage, "tile"), plan(stage, "x")
                with dve.Fori(0, KT // 2) as i:
                    for s in range(2):
                        xk = xt[:, i * 2 + s, 1:T + 1]
                        dve.wait_ge(evacuated, i * 2 + (t0 + s + 1 + UC))
                        dve.tensor_tensor(xk, xk, buf[:, s, :], add).then_inc(x_ready, 1)

            dve.memset(xt[:, :, 0:1], 0.0)
            for j, v in enumerate((EPS, LN_EPS, GN_EPS, 10 * LN2, -3 * LN2)):
                dve.memset(eps[:, j:j + 1], v)
            dve.memset(plast[:, 7:16:8, :], 0.0)
            dve.wait_ge(par_in, 16)
            dve.tensor_scalar(omu[:, 0:6 * KT], par[:, PCOL["mu"]:PCOL["mu"] + 6 * KT], -1.0, 1.0, mul, add)
            dve.tensor_scalar(omu[:, 6 * KT:7 * KT], par[:, PCOL["k_a"]:PCOL["k_a"] + KT], -1.0, 1.0,
                              mul, add).then_inc(omu_ready, 1)
            dve.wait_ge(rstd_ready, 1)
            with dve.Fori(0, KT) as k:
                xk = xt[:, k, 1:T + 1]
                chain.enter(k, 1)
                chain.step(dve.scalar_tensor_tensor(out=xk, in0=xk, scalar=pc("norm_mix_g", k), in1=rstd[:, :],
                                                    op0=mul, op1=mul))
                chain.leave(KT, 1)
            after = {"mixg": "lora_in", "mixk": "lora_in", "mixr": "gate_in", "mixv": "k"}

            def mix(m, name):
                stage = "mix" + name
                j = {"r": 0, "w": 1, "k": 2, "v": 3, "a": 4, "g": 5}[name]
                if stage in after:
                    st = after[stage]
                    dve.wait_ge(units_used, UNIT0[st] + dict(STREAM)[st] + UC)
                chain.wait()
                with dve.Fori(0, KT // 2) as i:
                    chain.enter(i, 2)
                    for s in range(2):
                        k = i * 2 + s
                        dve.wait_ge(lo_ready, i * 2 + (plan(stage, "split") + s + 1))
                        chain.step(dve.tensor_scalar(tmp[:, (plan(stage, "split") + s) % 2, :],
                                                     xt[:, k, 1:T + 1],
                                                     omu[:, bass.ds(k + j * KT, 1)], None, mul))
                    for s in range(2):
                        k = i * 2 + s
                        t_ = tmp[:, (plan(stage, "split") + s) % 2, :]
                        chain.wait(1 - s)
                        dve.scalar_tensor_tensor(out=t_, in0=xt[:, k, 0:T], scalar=pc("mu", k + j * KT),
                                                 in1=t_, op0=mul, op1=add).then_inc(val_ready, 1)
                    lows(stage, mixh[m], mixl[m], i)
                    chain.leave(KT // 2, 2)

            mix(0, "w")
            mix(1, "a")
            mix(0, "g")
            g = plan("mid", "split")
            dve.wait_ge(hi_ready, g + 1)
            dve.tensor_tensor(midl[:, :], tmp[:, g % 2, :], midh[:, :].bitcast(F32), sub).then_inc(lo_ready, 1)
            mix(1, "k")
            g = plan("gmid", "split")
            for j in range(2):
                dve.wait_ge(hi_ready, g + j + 1)
                dve.tensor_tensor(gmidl[:, j, :], tmp[:, (g + j) % 2, :], gmidh[:, j, :].bitcast(F32),
                                  sub).then_inc(lo_ready, 1)
            mix(0, "r")
            mix(1, "v")
            for j in range(KT):
                dve.wait_ge(sq_used, plan("knorm", "sq") + j + 1 + SC)
                dve.tensor_scalar(rn[:, j, :], bank[4 + j % 2][:, :], 2.0 ** 20, 1e-24 * 2.0 ** 20, mul,
                                  ALU.max).then_inc(kss_ready, 1)

            def seq_tile(name, half, q):
                return seq[name][:, 8 * half:8 * half + 8, q, :]

            def chunks(ap):
                return ap.rearrange("p (c t) -> p c t", t=CH)

            dve.wait_ge(evacuated, plan("r", "tile") + 8 + UC)
            for half in range(2):
                with dve.Fori(0, 2) as i:
                    stride = 12
                    chain.enter(i, stride)
                    dve.wait_ge(prep_done, i + (2 * half + 1))
                    for s in range(2):
                        q = i * 2 + s
                        k = i * 2 + (4 * half + s)
                        W_, A_, K_, R_ = (seq_tile(n, half, q) for n in "wakr")
                        dve.wait_ge(rn_ready, k + 1)
                        chain.step(dve.scalar_tensor_tensor(
                            out=chunks(kk[:, s, :]), in0=K_, scalar=pc("k_k", k),
                            in1=chunks(rn[:, k, :]), op0=mul, op1=mul))
                        chain.step(dve.tensor_scalar(chunks(pp[:, s, :]), A_, pc("k_a", k),
                                                     omu[:, bass.ds(k + 6 * KT, 1)], mul, add))
                        chain.wait()
                        chain.step(dve.tensor_tensor(K_, K_, chunks(pp[:, s, :]), mul))
                        for c in range(NCH):
                            w_c = seq["w"][:, 8 * half + c, q, :]
                            ins = dve.tensor_tensor_scan(cs[:, s, c * CH:(c + 1) * CH], ones[:, 0:CH], w_c, 0.0,
                                                         mul, add)
                        chain.step(ins)
                        dve.wait_ge(sq_used, plan("knorm", "sq") + KT + SC)
                        dve.wait_ge(bonus_mm, k + 1)
                        chain.wait(1)
                        chain.step(dve.scalar_tensor_tensor(out=chunks(sq[:, s, :]), in0=R_, scalar=pc("r_k", k),
                                                            in1=K_, op0=mul, op1=mul))
                        chain.step(dve.tensor_tensor(A_, chunks(kk[:, s, :]), A_, mul))
                        chain.wait(2)
                        dve.tensor_tensor(W_, chunks(cs[:, s, :]), W_, sub).then_inc(scan_ready, 1)
                    for s in range(2):
                        q = i * 2 + s
                        k = i * 2 + (4 * half + s)
                        W_, A_, K_, R_ = (seq_tile(n, half, q) for n in "wakr")
                        dve.wait_ge(decay_ready, k + 1)
                        chain.wait()
                        dve.tensor_tensor(R_, R_, chunks(pp[:, s, :]), mul)
                        dve.tensor_tensor(K_, K_, chunks(pi[:, s, :]), mul)
                        dve.tensor_tensor(A_, A_, chunks(pi[:, s, :]), mul)
                        dve.scalar_tensor_tensor(out=W_, in0=chunks(kk[:, s, :]), scalar=-1.0, in1=W_,
                                                 op0=mul, op1=mul)
                        ins = dve.tensor_scalar(plast[:, 8 * half:8 * half + 7, q],
                                                chunks(pp[:, s, :])[:, 0:7, CH - 1], 1.0, None, mul)
                    ins.then_inc(prep_done, 1)
                    chain.leave(2, stride)
            dve.wait_ge(bonus_mm, KT + SC)
            dve.tensor_copy(bonus[0:8, :, :], psum[0:8, 6:8, :])
            dve.wait_ge(evacuated, plan("v", "tile") + 8 + UC)
            dve.wait_ge(prep_done, 4 + 1)
            for b in (AR[0], AR[1], BB, KB, VB):
                dve.memset(b[:, :, :], 0.0)
            dve.memset(SS[:, :, :], 0.0).then_inc(core_clear, 1)
            dve.wait_ge(core_clear, 1)
            dve.wait_ge(ccore_in, 16)
            dve.sem_inc(core_v, NCV)

            def two(ap):
                return ap.rearrange("p (q t) -> p q t", q=2)

            def mask(m, n):
                return m.rearrange("p (o t) -> p o t", o=1).to_broadcast([P, 2, n])

            def core_load(r, ahead):
                dve.wait_ge(core_pe, count(r, NCPE, NCPE))
                if ahead:
                    dve.wait_ge(pro_pe, count(r, NPPE, NPPE))
                it, c = index(r, ahead), (parity(r) + ahead) % 2
                for h in range(2):
                    p = slice(64 * h, 64 * h + 64)
                    dve.tensor_scalar(AR[c][p, :, p], seq["w"][p, it, :, :], 1.0, None, mul)
                    ins = dve.tensor_scalar(KB[p, :, p], seq["k"][p, it, :, :], 1.0, None, mul)
                ins.then_inc(pro_v, 1)

            def core_prepared(r, ahead, what, groups=(0, 1)):
                c = (parity(r) + ahead) % 2
                for g in groups:
                    b, q = bank[4 * g + 3], slice(2 * g, 2 * g + 2)
                    dve.wait_ge(pro_pe, count(r, NPPE, ahead * NPPE + PPE[what] + g))
                    if what == "AC":
                        ac = two(b[:, 0:384])
                        chain.step(dve.tensor_tensor(ND[c][:, q, :], ac[:, :, 0:P], mask(m_n16, P), mul))
                        dve.tensor_tensor(CC[c][:, q, :], ac[:, :, P:192], mask(m_ac[:, P:192], CH), mul)
                        chain.wait()
                        dve.tensor_tensor(T1[c][:, q, :], ND[c][:, q, :], mask(ident, P), add).then_inc(pro_v, 1)
                    elif what == "N":
                        for to, m in ((AD, m_a16), (AO32, m_a32), (AO64, m_a64)):
                            ins = dve.tensor_tensor(to[c][:, q, :], two(b[:, 0:256]), mask(m, P), mul)
                        ins.then_inc(pro_v, 1)
                    else:
                        dve.tensor_tensor(BE[c][:, q, :], two(b[:, 0:384]), mask(m_ac, 192), mul).then_inc(pro_v, 1)

            def core_round(r, last=False):
                c, n = parity(r), 1 - parity(r)

                def pe_step(what, g):
                    dve.wait_ge(core_pe, count(r, NCPE, NCPE + CPE[what] + g))

                def act_done(what, g):
                    dve.wait_ge(core_a, count(r, NCA, NCA + CA[what] + g))

                def tt(g):
                    return TMA[:, 2 * g:2 * g + 2, 0:P]

                if not last:
                    core_load(r, 1)
                for g in range(2):
                    pe_step("M4", g)
                    act_done("M4", g)
                    dve.tensor_tensor(tt(g), two(bank[4 * g + n])[:, :, 0:P], T1[c][:, 2 * g:2 * g + 2, :],
                                      add).then_inc(core_v, 1)
                for g in range(2):
                    pe_step("M8", g)
                    act_done("M8", g)
                    dve.tensor_tensor(tt(g), two(bank[4 * g + c])[:, :, 0:P], tt(g), add).then_inc(core_v, 1)
                def more(what, *groups):
                    if not last:
                        core_prepared(r, 1, what, groups)

                more("AC", 0)
                for g in range(2):
                    pe_step("T4", g)
                    dve.tensor_tensor(tt(g), two(bank[4 * g + n][:, 0:256]), tt(g), add).then_inc(core_v, 1)
                more("AC", 1)
                more("N", 0)
                for g in range(2):
                    pe_step("TZ", g)
                    z = two(bank[4 * g + c])
                    dve.tensor_tensor(tt(g), z[:, :, 0:P], tt(g), add)
                    t_ = TZ[:, 2 * g:2 * g + 2, 0:P]
                    dve.tensor_tensor(t_, z[:, :, P:256], t_, add).then_inc(core_v, 1)
                more("N", 1)
                more("BE", 0)
                more("BE", 1)
                for g in range(2):
                    pe_step("T64", g)
                    dve.tensor_tensor(tt(g), two(bank[4 * g + c][:, 0:256]), tt(g), add).then_inc(core_v, 1)
                for g in range(2):
                    pe_step("Y", g)
                    s_ = SS[:, 2 * g:2 * g + 2, :]
                    chain.step(dve.tensor_tensor(s_, two(bank[4 * g + c][:, 0:256]), s_, add))
                    chain.wait()
                    for p in (2 * g, 2 * g + 1):
                        ins = dve.tensor_scalar(SS[:, p, :], SS[:, p, :], plast[:, index(r), p:p + 1], None, mul)
                    ins.then_inc(core_v, 1)

            core_load(0, 0)
            for what in ("AC", "N", "BE"):
                core_prepared(0, 0, what)
            with dve.Fori(0, 7) as i:
                chain.enter(i, 8)
                core_round((i, 0))
                core_round((i, 1))
                chain.leave(7, 8)
            core_round(14)
            core_round(15, last=True)

            v0 = plan("post", "val")
            dve.wait_ge(evacuated, plan("g2", "tile") + 8 + UC)
            for k in range(0, KT, 2):
                for s in range(2):
                    half, q = divmod(k + s, 4)
                    dve.wait_ge(post_pe, 2 * k + s + 1)
                    dve.scalar_tensor_tensor(out=chunks(yc[:, s, :]), in0=chunks(bank[4 + s]), scalar=-1.0 / CH,
                                             in1=seq["r"][:, 8 * half:8 * half + 8, q, :], op0=mul, op1=add)
                    dve.tensor_tensor(chunks(bv[:, s, :]), chunks(bank[6 + s]),
                                      seq["v"][:, 8 * half:8 * half + 8, q, :], mul).then_inc(post_v, 1)
                for s in range(2):
                    dve.wait_ge(post_a, 2 * k + 3 + s + POST_A)
                    chain.step(dve.scalar_tensor_tensor(out=yc[:, s, :], in0=yc[:, s, :], scalar=pc("ln_g", k + s),
                                                        in1=grs[:, s, :], op0=mul, op1=mul))
                for s in range(2):
                    chain.wait(1)
                    chain.step(dve.scalar_tensor_tensor(out=yc[:, s, :], in0=yc[:, s, :], scalar=pc("ln_b", k + s),
                                                        in1=bv[:, s, :], op0=add, op1=add))
                for s in range(2):
                    chain.wait(1 - s)
                    dve.wait_ge(lo_ready, plan("post", "split") + k + s + 1)
                    dve.tensor_tensor(tmp[:, (plan("post", "split") + s) % 2, :], yc[:, s, :],
                                      g_all[:, k + s, :], mul).then_inc(val_ready, 1)
                lows("post", acth, actl, k // 2)
            dve.wait_ge(xagain_in, 16)
            residual("o", delta0)

            def memory_side(l):
                dve.wait_ge(mem_in[l], 16)
                normed(f"norm_mem{l}", lambda k: mem[:, k, :], lambda k: pc("mem_norm_g", k), memh, meml, MEM)

            def attention(l):
                normed(f"norm_x{l}", x, lambda k: pc("norm_xattn_g", k + l * KT))

                def soft_max(h):
                    dve.wait_ge(sc_mm, 4 * l + h + 1)
                    chain.step(dve.tensor_reduce(smax[:, h, :], psum[:, 4:6, :].rearrange(
                        "p b (a m) -> p (b a) m", m=MEM), AX.X, ALU.max))
                    chain.wait()
                    dve.tensor_scalar(snegm[:, h, :], smax[:, h, :], -1.0 / 16, None, mul).then_inc(smax_ready, 1)

                def head_lows(h):
                    for j in range(2 * h, 2 * h + 2):
                        dve.wait_ge(hi_ready, g0 + j + 1)
                        dve.tensor_tensor(actl[:, j, :], tmp[:, (g0 + j) % 2, :], acth[:, j, :].bitcast(F32),
                                          sub).then_inc(lo_ready, 1)

                soft_max(0)
                soft_max(1)
                g0 = plan(f"heads{l}", "split")
                for h in range(4):
                    n = 4 * l + h
                    dve.wait_ge(p_exp, n + 1)
                    chain.step(dve.reciprocal(srec[:, h, :], ssum[:, h, :]))
                    chain.wait()
                    dve.tensor_tensor(prob[:, h % 2, :, :], prob[:, h % 2, :, :],
                                      srec[:, h, :].rearrange("p (a o) -> p a o", o=1).to_broadcast([P, 4, MEM]),
                                      mul).then_inc(p_ready, 1)
                    dve.wait_ge(pt_mm, n + 1)
                    dve.tensor_copy(probt[:, h % 2, 0, :], bank[6]).then_inc(pt_v, 1)
                    if h:
                        head_lows(h - 1)
                    if h < 2:
                        soft_max(h + 2)
                head_lows(3)
                residual(f"xo{l}", delta1)

            def ffn(l):
                normed(f"norm_ffn{l}", x, lambda k: pc("norm_ffn_g", k + l * KT))
                dve.memset(cu[:, :, 0:2], 0.0).then_inc(pad_ready, 1)
                dve.wait_ge(pad_ready, l + 1)
                t0, c0, v0 = plan(f"up{l}", "tile"), plan(f"up{l}", "conv"), plan(f"up{l}", "val")
                g0 = plan(f"up{l}", "split")
                with dve.Fori(0, FT // 2) as i:
                    chain.enter(i, 8)
                    for s in range(4):
                        col = (i * 2 + s // 2) * 3 + ((s % 2) * FT * 3 + l * 2 * FT * 3)
                        to = (cv if s % 2 else cg)[:, s // 2, :]
                        dve.wait_ge(evacuated, i * 4 + (t0 + s + 1 + UC))
                        chain.step(dve.tensor_scalar(to, cu[:, s, 2:T + 2], pc("ffn_dw", col + 2), None, mul))
                    for s in range(4):
                        col = (i * 2 + s // 2) * 3 + ((s % 2) * FT * 3 + l * 2 * FT * 3)
                        to = (cv if s % 2 else cg)[:, s // 2, :]
                        chain.wait(3)
                        chain.step(dve.scalar_tensor_tensor(out=to, in0=cu[:, s, 1:T + 1], scalar=pc("ffn_dw", col + 1),
                                                            in1=to, op0=mul, op1=add))
                    for s in range(4):
                        col = (i * 2 + s // 2) * 3 + ((s % 2) * FT * 3 + l * 2 * FT * 3)
                        to = (cv if s % 2 else cg)[:, s // 2, :]
                        chain.wait(3 - s)
                        dve.scalar_tensor_tensor(out=to, in0=cu[:, s, 0:T], scalar=pc("ffn_dw", col),
                                                 in1=to, op0=mul, op1=add).then_inc(conv_ready, 1)
                    for s in range(2):
                        dve.wait_ge(gate_ready, i * 2 + (c0 // 2 + s + 1))
                        dve.wait_ge(conv_ready, i * 4 + (c0 + 2 * s + 2 + UC))
                        dve.wait_ge(lo_ready, i * 2 + (g0 + s + 1))
                        dve.tensor_tensor(tmp[:, (g0 + s) % 2, :], sg[:, s, :], cv[:, s, :], mul).then_inc(val_ready, 1)
                    lows(f"up{l}", hidh, hidl, i)
                    chain.leave(FT // 2, 8)
                residual(f"down{l}", delta2)

            def convolution():
                normed("norm_conv", x, lambda k: pc("norm_mix_g", k + KT))
                memory_side(1)
                chain.step(dve.memset(gp[:, :, 0:CONVW - 1], 0.0))
                chain.wait()
                t0 = plan("cin", "tile")
                with dve.Fori(0, KT // 2) as i:
                    chain.enter(i, 2 + 2 * (CONVW - 2))
                    for s in range(2):
                        dve.wait_ge(evacuated, i * 4 + (t0 + 2 * s + 2 + UC))
                        u_ = gp[:, i * 2 + s, CONVW - 1:]
                        dve.tensor_tensor(u_, u_, glu[:, i * 2 + s, :], mul).then_inc(glu_ready, 1)
                    for s in range(2):
                        k = i * 2 + s
                        dve.wait_ge(glu_ready, k + 1)
                        chain.step(dve.tensor_scalar(ub[:, k, :], gp[:, k, CONVW - 1:],
                                                     pc("conv_dw", k * CONVW + CONVW - 1), pc("conv_dw_b", k), mul, add))
                    for j in range(CONVW - 2, -1, -1):
                        for s in range(2):
                            k = i * 2 + s
                            chain.wait(1 if j or s == 0 else 0)
                            ins = dve.scalar_tensor_tensor(out=ub[:, k, :], in0=gp[:, k, j:j + T],
                                                           scalar=pc("conv_dw", k * CONVW + j), in1=ub[:, k, :],
                                                           op0=mul, op1=add)
                            if j:
                                chain.step(ins)
                            else:
                                ins.then_inc(u_ready, 1)
                    chain.leave(KT // 2, 2 + 2 * (CONVW - 2))
                dve.wait_ge(mean_mm, 1)
                with dve.Fori(0, KT) as k:
                    dve.wait_ge(u_ready, KT)
                    dve.scalar_tensor_tensor(out=ub[:, k, :], in0=bank[5], scalar=-1.0 / D, in1=ub[:, k, :],
                                             op0=mul, op1=add).then_inc(uc_ready, 1)
                dve.wait_ge(rstd_ready, plan("ln", "rstd") + 1)
                with dve.Fori(0, KT) as k:
                    dve.scalar_tensor_tensor(out=ub[:, k, :], in0=ub[:, k, :], scalar=pc("conv_ln_g", k),
                                             in1=rstd[:, :], op0=mul, op1=mul).then_inc(uc_ready, 1)
                with dve.Fori(0, KT // 2) as i:
                    lows("ln", acth, actl, i)
                residual("cout", delta3)

            def norm_in_place(stage, gain):
                dve.wait_ge(rstd_ready, plan(stage, "rstd") + 1)
                with dve.Fori(0, KT) as k:
                    xk = xt[:, k, 1:T + 1]
                    dve.scalar_tensor_tensor(out=xk, in0=xk, scalar=pc(gain, k), in1=rstd[:, :],
                                             op0=mul, op1=mul).then_inc(x_ready, 1)

            def final_norm():
                norm_in_place("final", "final_norm_g")

            def hybrid():
                normed("norm_h", x, lambda k: pc("norm_mix_g_2", k))
                dve.wait_ge(log_ready, 1)
                chain.step(dve.tensor_scalar(ls[:, :, :], ls[:, :, :], 0.0, None, ALU.min))
                chain.wait()
                chain.step(dve.tensor_tensor(ls[:, :, :], ls[:, :, :], le[:, :, :], sub))
                chain.wait()
                chain.step(dve.memset(le[:, 0, :], 1.0))
                dve.wait_ge(hyb_in, 32)
                for p in range(2):
                    dve.tensor_tensor_scan(ls[:, p, :], hyb[:, 0:T], ls[:, p, :], 0.0, mul, add)
                chain.wait()
                dve.tensor_tensor_scan(small[:, :], le[:, 0, :], ls[:, 2, :], 0.0, mul, add).then_inc(cum_ready, 1)
                dve.wait_ge(eb_ready, 1)
                dve.scalar_tensor_tensor(out=gqk[:, 0:2, :], in0=gqk[:, 0:2, :], scalar=0.125, in1=eb[:, :, :],
                                         op0=mul, op1=mul)
                dve.tensor_tensor(gqk[:, 2:4, :], gqk[:, 2:4, :], enb[:, :, :], mul)
                dve.tensor_copy(gdec[:, :, :], eb[:, :, :].rearrange("p a (c t) -> p a c t", t=CH)[:, :, :, CH - 1])\
                    .then_inc(qk_ready, 1)
                dve.wait_ge(qk_ready, 1)
                for c in range(NCH - 1):
                    dve.wait_ge(kv_mm, c + 1)
                    kv = bank[4 + c % 4].rearrange("p (a m) -> p a m", a=2)
                    for h in range(2):
                        r, m = slice(64 * h, 64 * h + 64), slice(P * h, P * h + P)
                        if c:
                            chain.wait()
                            ins = dve.tensor_tensor(states[r, c, :, :], kv[r, :, m], states[r, c - 1, :, :], add)
                        else:
                            ins = dve.tensor_scalar(states[r, c, :, :], kv[r, :, m], 1.0, None, mul)
                    ins.then_inc(kv_ready, 1)
                    dve.wait_ge(kv_ready, c + 1)
                    for p in range(2):
                        ins = dve.tensor_scalar(states[:, c, p, :], states[:, c, p, :], gdec[:, p, c:c + 1], None, mul)
                    chain.step(ins)
                for j in range(8):
                    dve.wait_ge(frs_ready, j + 1)
                    t_ = (fq if j < 4 else fk)[:, j % 4, :]
                    dve.scalar_tensor_tensor(out=t_, in0=t_, scalar=pc("fox_q_g" if j < 4 else "fox_k_g"),
                                             in1=frs[:, j % 2, :], op0=mul, op1=mul).then_inc(fox_scaled, 1)

                def gla_mask(h):
                    dve.wait_ge(gs_mm, h + 1)
                    if h >= 2:
                        dve.wait_ge(gla_done, h - 1)
                    dve.tensor_tensor(sct[:, h % 2, :].rearrange("p (a m) -> p a m", a=4),
                                      bank[4 + h % 2].rearrange("p (a m) -> p a m", a=4),
                                      gmask.rearrange("p (o m) -> p o m", o=1).to_broadcast([P, 4, P]),
                                      mul).then_inc(gs_ready, 1)

                chain.wait()
                gla_mask(0)
                for h in range(4):
                    if h < 3:
                        gla_mask(h + 1)
                    dve.wait_ge(gla_scale, h + 1)
                    chain.step(dve.scalar_tensor_tensor(out=sct[:, h % 2, :], in0=bank[6 + h % 2],
                                                        scalar=pc("gla_norm_g", h), in1=frs[:, h % 2, :],
                                                        op0=mul, op1=mul))
                    chain.wait()
                    dve.tensor_tensor(gr[:, h, :], sct[:, h % 2, :], gr[:, h, :], mul).then_inc(gla_done, 1)

                def fox_max(h):
                    dve.wait_ge(fs_mm, h + 1)
                    for qt in range(4):
                        b, o = ((4, 0), (4, P), (5, 0), (6, 0))[qt]
                        ins = dve.tensor_reduce(fmax[:, h, qt:qt + 1], bank[b][:, o:o + (qt + 1) * P], AX.X, ALU.max)
                    chain.step(ins)
                    chain.wait()
                    dve.tensor_scalar(fneg[:, h, :], fmax[:, h, :], -1.0, None, mul).then_inc(fmax_ready, 1)

                def fox_lows(p):
                    dve.wait_ge(hi_ready, g0 + p + 1)
                    dve.tensor_tensor(actl[:, 4 + p, :], tmp[:, (g0 + p) % 2, :], acth[:, 4 + p, :].bitcast(F32),
                                      sub).then_inc(lo_ready, 1)

                fox_max(0)
                for h in range(4):
                    dve.wait_ge(hi_ready, plan("gla", "split") + h + 1)
                    dve.wait_ge(gla_done, h + 1)
                    dve.tensor_tensor(actl[:, h, :], gr[:, h, :], acth[:, h, :].bitcast(F32), sub).then_inc(lo_ready, 1)
                fox_max(1)
                g0 = plan("fox", "split")
                for h in range(8):
                    dve.wait_ge(f_exp, h + 1)
                    chain.step(dve.reciprocal(frec[:, h, :], fsum[:, h, :]))
                    chain.wait()
                    for qt in range(4):
                        p_ = fp[:, h % 2, FOX_OFF[qt]:FOX_OFF[qt] + (qt + 1) * P]
                        ins = dve.tensor_scalar(p_, p_, frec[:, h, qt:qt + 1], None, mul)
                    ins.then_inc(fp_ready, 1)
                    dve.wait_ge(fpt_mm, h + 1)
                    dve.tensor_copy(fpt[:, h % 2, 0:4 * P], bank[0]).then_inc(fpt_v, 1)
                    if h % 2 == 0 and h:
                        fox_lows(h // 2 - 1)
                    if h < 6:
                        fox_max(h + 2)
                fox_lows(3)
                t0, u0, f0 = plan("branch", "tile"), UNIT0["branch"], plan("branch", "full")
                g0 = plan("branch", "split")
                with dve.Fori(0, KT // 2) as i:
                    for s in range(2):
                        dve.wait_ge(tile_full, i * 2 + (f0 + s + 1))
                        ga, gb = gate_a[:, i * 2 + s, :], gate_b[:, i * 2 + s, :]
                        dve.tensor_tensor(ga, ga, bank_of(t0 + 2 * s), mul).then_inc(evacuated, 1)
                        dve.wait_ge(units_used, i * 2 + (u0 + s + 1 + UC))
                        dve.tensor_tensor(gb, gb, bank_of(t0 + 2 * s + 1), mul).then_inc(evacuated, 1)
                        dve.wait_ge(evacuated, i * 4 + (t0 + 2 * s + 2 + UC))
                        dve.wait_ge(lo_ready, i * 2 + (g0 + s + 1))
                        dve.tensor_tensor(tmp[:, (g0 + s) % 2, :], ga, gb, add).then_inc(val_ready, 1)
                    lows("branch", yh, yl, i)
                residual("out2", delta4)

            def ffn2():
                normed("norm_ffn2", x, lambda k: pc("norm_ffn_g_2", k))
                dve.memset(cu[:, :, 0:2], 0.0).then_inc(pad_ready, 1)
                dve.wait_ge(pad_ready, 3)
                t0, v0, g0 = plan("up2", "tile"), plan("up2", "val"), plan("up2", "split")
                with dve.Fori(0, FT // 2) as i:
                    chain.enter(i, 4)
                    for s in range(2):
                        j = i * 2 + s
                        dve.wait_ge(evacuated, i * 4 + (t0 + 2 * s + 1 + UC))
                        chain.step(dve.tensor_scalar(cg[:, s, :], cu[:, 2 * s, 2:T + 2], pc("conv_w_2", j * 3 + 2),
                                                     pc("conv_b_2", j), mul, add))
                    for s in range(2):
                        chain.wait(1)
                        chain.step(dve.scalar_tensor_tensor(
                            out=cg[:, s, :], in0=cu[:, 2 * s, 1:T + 1], scalar=pc("conv_w_2", (i * 2 + s) * 3 + 1),
                            in1=cg[:, s, :], op0=mul, op1=add))
                    for s in range(2):
                        chain.wait(1 - s)
                        dve.scalar_tensor_tensor(
                            out=cg[:, s, :], in0=cu[:, 2 * s, 0:T], scalar=pc("conv_w_2", (i * 2 + s) * 3),
                            in1=cg[:, s, :], op0=mul, op1=add).then_inc(conv_ready, 1)
                    for s in range(2):
                        dve.wait_ge(evacuated, i * 4 + (t0 + 2 * s + 2 + UC))
                        dve.wait_ge(gate_ready, i * 2 + (2 * FT + s + 1))
                        dve.wait_ge(lo_ready, i * 2 + (g0 + s + 1))
                        dve.tensor_tensor(tmp[:, (g0 + s) % 2, :], sg[:, s, :], cu[:, 2 * s + 1, 2:T + 2],
                                          mul).then_inc(val_ready, 1)
                    lows("up2", hidh, hidl, i)
                    chain.leave(FT // 2, 4)
                residual("down2", delta2)

            def last_norm():
                norm_in_place("last", "norm_final_g_2")

            memory_side(0)
            attention(0)
            ffn(0)
            convolution()
            attention(1)
            ffn(1)
            final_norm()
            hybrid()
            ffn2()
            last_norm()


def units_of(w):
    k, n = w.shape
    assert k == BLOCKS * P
    return w.reshape(BLOCKS, P, n // P, P).transpose(2, 1, 0, 3).reshape(n // P, P, BLOCKS * P)


def blocks_of(blocks):
    blocks = list(blocks) + [np.zeros((P, P), np.float32)] * (-len(blocks) % BLOCKS)
    a = np.stack(blocks).reshape(-1, BLOCKS, P, P)
    return a.transpose(0, 2, 1, 3).reshape(-1, P, BLOCKS * P)


def padded(w, rows, cols, r0=0):
    out = np.zeros((rows, cols), np.float32)
    out[r0:r0 + w.shape[0], :w.shape[1]] = w
    return out


def down_units(w):
    return np.concatenate([blocks_of([w[k * P:(k + 1) * P, j * P:(j + 1) * P] for k in range(FT)])
                           for j in range(KT)])


def paired(w, half):
    u = units_of(w)
    return np.stack([u[:half], u[half:]], 1).reshape(2 * half, P, BLOCKS * P)


def pack(i):
    g = lambda n: np.asarray(i[n], np.float32)
    cut = lambda w, k, j: w[k * P:(k + 1) * P, j * P:(j + 1) * P]
    g1 = padded(g("rwkv_g1")[0], D, 2 * P)
    g2 = padded(g("rwkv_g2")[0], 2 * P, D)
    stream = {
        "lora_in": units_of(np.concatenate([g("rwkv_w1")[0], g("rwkv_a1")[0]], 1)),
        "gate_in": units_of(g1),
        "w2": blocks_of([padded(g("rwkv_w2")[0][:, j * P:(j + 1) * P], P, P) for j in range(KT)]),
        "a2": blocks_of([padded(g("rwkv_a2")[0][:, j * P:(j + 1) * P], P, P, 64) for j in range(KT)]),
        "k": units_of(g("rwkv_w_k")[0]), "r": units_of(g("rwkv_w_r")[0]), "v": units_of(g("rwkv_w_v")[0]),
        "g2": blocks_of([cut(g2, b, j) for j in range(KT) for b in range(2)]),
        "o": units_of(g("rwkv_w_o")[0]),
        "cin": paired(g("conv_w_in")[0], KT), "cout": units_of(g("conv_w_out")[0]),
        "out2": units_of(g("w_out_2")[0]), "up2": paired(g("w_up_2")[0], FT),
        "down2": down_units(g("w_down_2")[0]),
    }
    for l in range(2):
        stream[f"kv{l}"] = units_of(g("xattn_w_kv")[l])
        stream[f"q{l}"] = units_of(g("xattn_w_q")[l])
        stream[f"xo{l}"] = units_of(g("xattn_w_o")[l])
        stream[f"up{l}"] = paired(g("ffn_w_in")[l], FT)
        stream[f"down{l}"] = down_units(g("ffn_w_out")[l])
    w = g("w_in_2")[0]
    gq, gk, gv, gr, glr, fq, fk, fv, ff, gg, gf = np.split(
        w, np.cumsum([256, 256, 512, 512, 16, 512, 512, 512, 8, D])[:].tolist(), axis=1)
    small = np.concatenate([padded(glr, D, 32), padded(ff, D, 96)], 1)
    stream["in2"] = units_of(np.concatenate([small, gv, fv, gq, gk, gr, fq, fk, gg, gf], 1))
    wg, wf = g("w_gla_branch_2")[0], g("w_fox_branch_2")[0]
    stream["branch"] = blocks_of([cut(m, k, j) for j in range(KT) for m in (wg, wf) for k in range(4)])
    weights = np.concatenate([stream[n] for n, _ in STREAM])
    for n, c in STREAM:
        assert stream[n].shape[0] == c, (n, stream[n].shape)

    vec = lambda a: np.asarray(a, np.float32).reshape(-1, P).T
    taps = lambda a, n: np.asarray(a, np.float32).reshape(a.shape[0], n, P).transpose(2, 1, 0).reshape(P, -1)
    cols = {
        "mem_norm_g": vec(g("mem_norm_g")), "norm_mix_g": vec(g("norm_mix_g")),
        "norm_xattn_g": vec(g("norm_xattn_g")), "norm_ffn_g": vec(g("norm_ffn_g")),
        "final_norm_g": vec(g("final_norm_g")), "mu": vec(g("rwkv_mu")), "w0": vec(g("rwkv_w0")),
        "a0": vec(g("rwkv_a0")), "k_k": vec(g("rwkv_k_k")), "k_a": vec(g("rwkv_k_a")),
        "r_k": vec(g("rwkv_r_k")), "ln_g": vec(g("rwkv_ln_g")), "ln_b": vec(g("rwkv_ln_b")),
        "conv_b_in": vec(g("conv_b_in")), "conv_dw": taps(g("conv_dw")[0], KT),
        "conv_dw_b": vec(g("conv_dw_b")), "conv_ln_g": vec(g("conv_ln_g")), "conv_ln_b": vec(g("conv_ln_b")),
        "conv_b_out": vec(g("conv_b_out")),
        "ffn_dw": np.concatenate([taps(g("ffn_dw")[l], 2 * FT) for l in range(2)], 1),
        "norm_mix_g_2": vec(g("norm_mix_g_2")), "gla_b": vec(g("gla_alpha_b_2")),
        "gla_norm_g": vec(g("gla_out_norm_g_2")),
        "fox_q_g": vec(np.tile(g("fox_q_norm_g_2")[0], 2)), "fox_k_g": vec(np.tile(g("fox_k_norm_g_2")[0], 2)),
        "gate_b_2": vec(g("gate_b_2")), "norm_ffn_g_2": vec(g("norm_ffn_g_2")),
        "conv_w_2": taps(g("conv_w_2")[0], FT), "conv_b_2": vec(g("conv_b_2")),
        "norm_final_g_2": vec(g("norm_final_g_2")), "fox_fb": padded(g("fox_forget_b_2")[0][:, None], P, 1, 32),
    }
    par = np.concatenate([cols[n] for n, _ in PARAMS], 1)
    assert par.shape == (P, NPAR), par.shape
    feature_major = lambda a: np.ascontiguousarray(a.T.reshape(KT, P, -1).transpose(1, 0, 2))
    return {"weights": weights, "par": np.ascontiguousarray(par), "x": feature_major(g("x")[0]),
            "mem": feature_major(g("mem")[0]),
            "w2g": padded(g("gla_alpha_w2_2")[0], P, 256), **constants()}


def kernel(**inputs):
    import concourse.bacc as bacc
    from concourse.bass_utils import run_bass_kernel_spmd

    nc = bacc.Bacc("TRN2", target_bir_lowering=False, num_devices=1, dynamic_dma_scratch_size=1024)
    arrays = {f"in_{n}": np.ascontiguousarray(a) for n, a in pack(inputs).items()}
    dram = {n[3:]: nc.dram_tensor(n, a.shape, F32, kind="ExternalInput").ap() for n, a in arrays.items()}
    dram["out"] = nc.dram_tensor("out_x", (P, KT, T), F32, kind="ExternalOutput").ap()
    build_program(nc, dram)
    r = run_bass_kernel_spmd(nc, [arrays], core_ids=[0])
    out = r.results[0]["out_x"]
    return np.ascontiguousarray(out.transpose(2, 1, 0).reshape(1, T, D))
```

```python
from contextlib import ExitStack

import numpy as np
import concourse.bass as bass
from concourse import mybir

F32 = mybir.dt.float32
F32R = mybir.dt.float32r
ALU = mybir.AluOpType
ACT = mybir.ActivationFunctionType
AX = mybir.AxisListType

P = 128
D = 1024
KT = D // P
T = 512
MEM = 256
FF = 2816
FT = FF // P
BLOCKS = 8
SLOTS = 4
CH = 64
NCH = T // CH
CONVW = 31
PETAPS = 7
EPS = 1e-6
LN_EPS = 1e-5
GN_EPS = 64e-5
RSQRT_E = float(np.exp(-0.5))
LN2 = float(np.log(2.0))

STREAM = [
    ("lora_in", 1), ("gate_in", 2), ("w2", 1), ("a2", 1), ("k", 8), ("r", 8), ("v", 8),
    ("g2", 2), ("o", 8),
    ("kv0", 16), ("q0", 8), ("xo0", 8), ("up0", 2 * FT), ("down0", 24),
    ("cin", 16), ("kv1", 12), ("cout", 8), ("kv1b", 4),
    ("q1", 8), ("xo1", 8), ("up1", 2 * FT), ("down1", 24),
    ("in2", 41), ("branch", 8), ("out2", 8), ("up2", 2 * FT), ("down2", 24),
]
UNIT0 = {}
_u = 0
for _name, _n in STREAM:
    UNIT0[_name] = _u
    _u += _n
UNITS = _u
assert UNITS % SLOTS == 0

PARAMS = [
    ("mem_norm_g", KT), ("norm_mix_g", 2 * KT), ("norm_xattn_g", 2 * KT), ("norm_ffn_g", 2 * KT),
    ("final_norm_g", KT), ("mu", 6 * KT), ("w0", KT), ("a0", KT), ("k_k", KT), ("k_a", KT), ("r_k", KT),
    ("ln_g", KT), ("ln_b", KT), ("conv_b_in", 2 * KT), ("conv_dw", KT * CONVW), ("conv_dw_b", KT),
    ("conv_ln_g", KT), ("conv_ln_b", KT), ("conv_b_out", KT), ("ffn_dw", 2 * FT * 2 * 3),
    ("norm_mix_g_2", KT), ("gla_b", 2), ("gla_norm_g", 4), ("fox_q_g", 1), ("fox_k_g", 1),
    ("gate_b_2", 2 * KT), ("norm_ffn_g_2", KT), ("conv_w_2", FT * 3), ("conv_b_2", FT),
    ("norm_final_g_2", KT), ("fox_fb", 1),
]
PCOL = {}
_c = 0
for _name, _n in PARAMS:
    PCOL[_name] = _c
    _c += _n
NPAR = _c


def constants():
    i = np.arange(P)
    s, t = i[:, None], i[None, :]
    same64 = (s // 64) == (t // 64)
    f = lambda m: m.astype(np.float32)
    common = np.concatenate([f(s == t), np.ones((P, P), np.float32), f(same64)], 1)
    tt = np.arange(64)[None, :]
    ac = np.concatenate([f(same64 & (s < t)), f((s % 64) <= tt)], 1)
    n16 = f((s // 16 == t // 16) & (s < t))
    a16 = f((s // 16 == t // 16) & (t < s))
    a32 = f((s // 32 == t // 32) & (s // 16 != t // 16) & (t < s))
    a64 = f(same64 & (s // 32 != t // 32) & (t < s))
    scan = np.broadcast_to(f(np.arange(T) % CH != 0)[None, :], (P, T))
    prep = np.zeros((P, 4, 8), np.float32)
    for k in range(4):
        prep[:64, k, 2 * k] = 1
        prep[64:, k, 2 * k + 1] = 1
    bsel = np.zeros((P, 4, P), np.float32)
    for k in range(4):
        bsel[2 * k, k, :64] = 1
        bsel[2 * k + 1, k, 64:] = 1
    gla = f(same64 & (s <= t))
    fox = np.where(t <= s, 0.0, -1e30).astype(np.float32)
    negsel = np.zeros((P, 8, P), np.float32)
    for h in range(8):
        negsel[32 + h, h, :] = -1
    return {
        "c_common": common,
        "c_prep": prep.reshape(P, -1),
        "c_core": np.concatenate([ac, n16, a16, a32, a64], 1),
        "c_post": bsel.reshape(P, -1),
        "c_hybrid": np.concatenate([scan, gla, fox, negsel.reshape(P, -1)], 1),
    }


CONST_COLS = {"c_common": 3 * P, "c_prep": 4 * 8, "c_core": 192 + 4 * P, "c_post": 4 * P,
              "c_hybrid": T + 2 * P + 8 * P}


class Chain:

    def __init__(self, eng, sem):
        self.eng, self.sem, self.base, self.n, self.at = eng, sem, 0, 0, None

    def step(self, ins):
        ins.then_inc(self.sem, 1)
        self.n += 1

    def wait(self, back=0):
        v = self.base + self.n - back
        self.eng.wait_ge(self.sem, v if self.at is None else self.at + v)

    def enter(self, i, stride):
        self.base, self.n, self.at = self.base + self.n, 0, i * stride

    def leave(self, rounds, stride):
        assert self.n == stride, (self.n, stride)
        self.base, self.n, self.at = self.base + stride * rounds, 0, None


class Plan:

    def __init__(self):
        self.total, self.first = {}, {}

    def take(self, stage, **counts):
        for what, n in counts.items():
            self.first[stage, what] = self.total.get(what, 0)
            self.total[what] = self.first[stage, what] + n

    def norm(self, stage, split=True):
        n = KT if split else 0
        self.take(stage, sq=KT, rstd=1, split=n, val=n)

    def __call__(self, stage, what):
        return self.first[stage, what]


def build_program(nc, dram):
    plan = Plan()
    plan.norm("norm0", split=False)
    plan.take("norm0", total=1)
    for m in "wag":
        plan.take("mix" + m, split=KT, val=KT)
    plan.take("mid", split=1)
    plan.take("mixk", split=KT, val=KT)
    plan.take("gmid", split=2)
    for m in "rv":
        plan.take("mix" + m, split=KT, val=KT)
    plan.take("knorm", sq=KT)
    for stage, n in (("lora_in", 2), ("gate_in", 2), ("w2", 8), ("a2", 8), ("k", 8), ("r", 8), ("v", 8),
                     ("g2", 8), ("o", 8)):
        plan.take(stage, tile=n)
    plan.take("g2", full=0)
    plan.total["full"] = 1 + 7 + 7 + 6
    plan.take("post", split=KT, val=KT)
    plan.norm("norm_mem0")
    plan.take("o", x=KT)
    for l in range(2):
        if l == 1:
            plan.norm("norm_conv")
            plan.take("norm_conv", total=1)
            plan.take("cin", tile=16)
            plan.norm("norm_mem1")
            plan.take("kv1", tile=12)
            plan.take("ln", sq=KT, rstd=1, split=KT)
            plan.take("cout", tile=8, x=KT)
            plan.take("kv1b", tile=4)
        else:
            plan.take("kv0", tile=16)
        plan.norm(f"norm_x{l}")
        plan.take(f"norm_x{l}", total=1 if l else 0)
        plan.take(f"q{l}", tile=8)
        plan.take(f"heads{l}", tile=8, split=8, full=8)
        plan.take(f"xo{l}", tile=8, x=KT)
        plan.norm(f"norm_ffn{l}")
        plan.take(f"norm_ffn{l}", total=1)
        plan.take(f"up{l}", tile=2 * FT, split=FT, val=FT, conv=2 * FT)
        plan.take(f"down{l}", tile=8, x=KT)
    plan.take("norm_h", sq=2 * KT, rstd=1, split=KT, val=KT, total=1)
    plan.take("final", x=KT)
    plan.take("in2", tile=41)
    plan.take("fox_norm", sq=8)
    plan.take("gla", sq=4, split=4)
    plan.take("fox", split=4)
    plan.take("branch", tile=16, full=8, split=KT, val=KT)
    plan.take("out2", tile=8, x=KT)
    plan.norm("norm_ffn2")
    plan.take("norm_ffn2", total=1)
    plan.take("up2", tile=2 * FT, split=FT, val=FT, conv=FT)
    plan.take("down2", tile=8, x=KT)
    plan.take("last", sq=KT, rstd=1, x=KT, total=1)

    ctx = ExitStack()
    with ctx:
        cursor = [2048]

        def size(shape):
            return 4 * int(np.prod(shape[1:]))

        def at(name, shape, dtype, offset):
            assert offset + size(shape) <= nc.sbuf_usable_end, (name, offset)
            return nc.alloc_sbuf_tensor_at(name, shape, dtype, offset=offset)

        def place(name, shape, dtype=F32):
            t = at(name, shape, dtype, cursor[0])
            cursor[0] += (size(shape) + 31) // 32 * 32
            return t

        def sem(name):
            return ctx.enter_context(nc.semaphore(name))

        raw = place("raw", [P, SLOTS, BLOCKS * P])
        wh = place("wh", [P, SLOTS, BLOCKS * P], F32R)
        wl = place("wl", [P, SLOTS, BLOCKS * P], F32R)
        xt_at = cursor[0]
        xt = place("xt", [P, KT, T + 1])
        act_at = cursor[0]
        acth = place("acth", [P, KT, T], F32R)
        actl = place("actl", [P, KT, T], F32R)
        par = place("par", [P, NPAR])
        common = place("common", [P, 3 * P])
        omu = place("omu", [P, 7 * KT])
        zero = place("zero", [P, 1])
        eps = place("eps", [P, 6])
        tmp_at = cursor[0]
        tmp = place("tmp", [P, 2, T])
        sq_at = cursor[0]
        sq = place("sq", [P, 2, T])
        rstd_at = cursor[0]
        rstd = place("rstd", [P, T])
        zone = cursor[0]
        ident, ones, blk64 = (common[:, j * P:(j + 1) * P] for j in range(3))
        b_eps, b_ln, b_gn, b_rn, b_q, b_eps2 = (eps[:, j:j + 1] for j in range(6))

        MU = {"r": 0, "w": 1, "k": 2, "v": 3, "a": 4, "g": 5}

        def x(k):
            return xt[:, k, 1:T + 1]

        def pc(name, k=0):
            c = k + PCOL[name]
            return par[:, c:c + 1] if isinstance(c, int) else par[:, bass.ds(c, 1)]

        cursor[0] = zone
        seq = {n: place("seq_" + n, [P, 16, 4, CH]) for n in "wakr"}
        v_at = cursor[0]
        seq["v"] = place("seq_v", [P, 16, 4, CH])
        yx_at = cursor[0]
        mixl = {0: place("mixl", [P, KT, T], F32R), 1: actl}
        mixh = {0: at("mixh", [P, KT, T], F32R, v_at), 1: acth}
        bsel = at("bsel", [P, 4, P], F32, rstd_at)
        midh = at("midh", [P, T], F32R, sq_at)
        parts = at("parts", [P, KT, T], F32, v_at - 32768)
        gbuf = at("gbuf", [P, 2, T], F32, v_at - 16384)

        midl = at("midl", [P, T], F32R, sq_at + 2048)
        gmidh = place("gmidh", [P, 2, T], F32R)
        gmidl = place("gmidl", [P, 2, T], F32R)
        bonus = place("bonus", [8, 2, T])
        plast = place("plast", [P, 16, 4])
        selk = place("selk", [P, 4, 8])
        kk, cs = (at("prep_" + n, [P, 4, T], F32, xt_at + 8192 * j) for j, n in enumerate(("kk", "cs")))
        pp, pi, pt = (at("prep_" + n, [P, 2, T], F32, yx_at + 4096 * j) for j, n in enumerate(("pp", "pi", "pt")))
        room = [[act_at, act_at + 32768], [yx_at, yx_at + 16384], [xt_at, xt_at + 16384], [tmp_at, tmp_at + 10240]]

        def core(name, shape):
            r = next(r for r in room if r[0] + size(shape) <= r[1])
            r[0] += size(shape)
            return at("core_" + name, shape, F32, r[0] - size(shape))

        def both(name, shape):
            return [core(name + str(j), shape) for j in range(2)]

        TMA = core("tma", [P, 4, 384])
        TZ = core("tz", [P, 4, 256])
        TBK = both("tbk", [P, 4, 256])
        AR = both("ar", [P, 4, 192])
        BE = both("be", [P, 4, 192])
        c_core = core("consts", [P, CONST_COLS["c_core"]])
        BB, KB, VB = (core(n, [P, 4, P]) for n in ("bb", "kb", "vb"))
        XX, UU, SS = (core(n, [P, 4, P]) for n in ("x", "u", "s"))
        VT, AD, ND, T1, AO32, AO64 = (both(n, [P, 4, P]) for n in ("vt", "ad", "nd", "t1", "ao32", "ao64"))
        CC = both("c", [P, 4, CH])
        m_ac = c_core[:, 0:192]
        m_n16, m_a16, m_a32, m_a64 = (c_core[:, 192 + j * P:192 + (j + 1) * P] for j in range(4))
        c_post = at("c_post", [P, 4, P], F32, yx_at)
        grs = at("grs", [P, KT, T], F32, zone)
        delta0 = at("delta0", [P, 2, T], F32, yx_at + 10240)
        g_all = at("g_all", [P, KT, T], F32, zone + 16384)

        cursor[0] = zone
        keys = place("keys", [P, KT, MEM])
        vals = place("vals", [P, KT, MEM])
        vtok = place("vtok", [P, 2, D])
        delta1 = place("delta1", [P, 2, T])
        smax, snegm, ssum, srec = (place("soft_" + n, [P, 4, 4]) for n in ("max", "negm", "sum", "rec"))
        cursor[0] = zone + 32768
        mem = place("mem", [P, KT, MEM])
        memh = place("memh", [P, KT, MEM], F32R)
        query = place("query", [P, KT, T])
        prob = place("prob", [P, 2, 4, MEM])
        probt = place("probt", [P, 2, 2, T])
        assert cursor[0] == yx_at
        cursor[0] = yx_at + 2048
        meml = place("meml", [P, KT, MEM], F32R)
        meml_end = cursor[0]
        headh = place("headh", [P, KT, T], F32R)
        headl = at("headl", [P, KT, T], F32R, zone + 32768)

        cursor[0] = zone
        hidh, hidl = place("hidh", [P, FT, T], F32R), place("hidl", [P, FT, T], F32R)
        cu_at = cursor[0]
        cu = place("cu", [P, 4, T + 2])
        cg, cv, sg = (place("ffn_" + n, [P, 2, T]) for n in ("cg", "cv", "sg"))
        delta2 = at("delta2", [P, 2, T], F32, cu_at)
        acc_y, acc_x = (at("acc_" + n, [P, T], F32, cu_at + 8256 + 2048 * j) for j, n in enumerate("yx"))

        cursor[0] = zone + 49152
        ub = place("ub", [P, KT, T])
        glu = place("glu", [P, KT, T])
        cursor[0] = meml_end
        gp = place("gp", [P, KT, T + CONVW - 1])
        diag = [place("diag1", [P, PETAPS, P])]
        cursor[0] = zone + 24576
        delta3 = place("delta3", [P, 2, T])
        diag.insert(0, place("diag0", [P, PETAPS, P]))
        assert cursor[0] <= zone + 32768

        cursor[0] = zone
        gqk = place("gqk", [P, 4, T])
        gv, fv = place("gv", [P, 4, T]), place("fv", [P, 4, T])
        fq, fk = place("fq", [P, 4, T]), place("fk", [P, 4, T])
        gr = place("gr", [P, 4, T])
        gate_a, gate_b = place("gate_a", [P, KT, T]), place("gate_b", [P, KT, T])
        small = place("small", [P, T])
        gvt, fvt = place("gvt", [P, 4, T]), place("fvt", [P, 4, T])
        ket = place("ket", [P, 4, 256])
        hyb = place("hyb", [P, CONST_COLS["c_hybrid"]])
        w2g = place("w2g", [P, 256])
        gdec = place("gdec", [P, 2, NCH])
        fmax, fneg, fsum, frec = (place("fox_" + n, [P, 8, 4]) for n in ("max", "neg", "sum", "rec"))
        assert cursor[0] <= nc.sbuf_usable_end
        over = zone + 8192
        ls, le = at("ls", [P, 3, T], F32, over), at("le", [P, 3, T], F32, over + 6144)
        eb = at("eb", [P, 2, T], F32, over + 12288)
        enb = at("enb", [P, 2, T], F32, over + 6144)
        sct = at("sct", [P, 2, T], F32, over)
        states = at("gla_states", [P, NCH - 1, 2, P], F32, over + 4096)
        frs = at("frs", [P, 2, T], F32, over + 12288)
        fp = at("fox_p", [P, 2, 10 * P], F32, zone)
        fpt = at("fox_pt", [P, 2, 10 * P], F32, zone + 10240)
        yh, yl = at("yh", [P, KT, T], F32R, zone), at("yl", [P, KT, T], F32R, zone + 16384)
        delta4 = at("delta4", [P, 2, T], F32, zone + 32768)
        gmask, fmask = hyb[:, T:T + P], hyb[:, T + P:T + 2 * P]
        FOX_OFF = [0, P, 3 * P, 6 * P]
        FOX_TOFF = [0, 4 * P, 7 * P, 9 * P]

        psum = ctx.enter_context(nc.psum_tensor("psum", [P, 8, T], F32))
        bank = [psum[:, i, :] for i in range(8)]

        raw_in = [sem(f"raw_in{i}") for i in range(SLOTS)]
        x_in = [sem(f"x_in{j}") for j in range(4)]
        par_in, common_in, selk_in, ccore_in, cpost_in, xagain_in = (
            sem(n) for n in ("par_in", "common_in", "selk_in", "ccore_in", "cpost_in", "xagain_in"))
        zero_ready = sem("zero_ready")
        split_hi = sem("split_hi")
        split_done = sem("split_done")
        units_used = sem("units_used")
        tile_full = sem("tile_full")
        evacuated = sem("evacuated")
        omu_ready, h_ready, part_ready = sem("omu_ready"), sem("h_ready"), sem("part_ready")
        sq_ready, sq_used = sem("sq_ready"), sem("sq_used")
        rstd_ready = sem("rstd_ready")
        val_ready, hi_ready, lo_ready = sem("val_ready"), sem("hi_ready"), sem("lo_ready")
        x_ready = sem("x_ready")
        sum_mm, acc_ready = sem("sum_mm"), sem("acc_ready")
        dve_chain, act_chain = sem("dve_chain"), sem("act_chain")
        bsel_in, kss_ready, rn_ready, bsel_mm, kk_ready = (
            sem(n) for n in ("bsel_in", "kss_ready", "rn_ready", "bsel_mm", "kk_ready"))
        scan_ready, decay_ready = sem("scan_ready"), sem("decay_ready")
        bonus_mm = sem("bonus_mm")
        prep_done = sem("prep_done")
        core_clear = sem("core_clear")
        core_pe, core_v, core_a = sem("core_pe"), sem("core_v"), sem("core_a")
        pro_pe, pro_v, pro_a = sem("pro_pe"), sem("pro_v"), sem("pro_a")
        mean_pe, var_pe, post_v, post_sq, post_ln, post_a = (
            sem(n) for n in ("mean_pe", "var_pe", "post_v", "post_sq", "post_ln", "post_a"))
        act_held, pe_held = sem("act_held"), sem("pe_held")
        out_in = sem("out_in")
        mem_in = [sem("mem_in0"), sem("mem_in1")]
        vt_mm, vt_ready = sem("vt_mm"), sem("vt_ready")
        sc_mm, smax_ready, p_exp, p_ready = sem("sc_mm"), sem("smax_ready"), sem("p_exp"), sem("p_ready")
        pt_mm, pt_v, pt_a = sem("pt_mm"), sem("pt_v"), sem("pt_a")
        conv_ready, gate_ready = sem("conv_ready"), sem("gate_ready")
        diag_ready, tap_mm, tap_ready = sem("diag_ready"), sem("tap_mm"), sem("tap_ready")
        pad_ready, glu_ready, u_ready, mean_mm, uc_ready = (
            sem(n) for n in ("pad_ready", "glu_ready", "u_ready", "mean_mm", "uc_ready"))

        gated = sem("gated")
        hyb_in, vt2_mm, vt2_ready, z_mm, z_ready, log_ready, cum_ready, eb_ready, qk_ready = (
            sem(n) for n in ("hyb_in", "vt2_mm", "vt2_ready", "z_mm", "z_ready", "log_ready", "cum_ready",
                             "eb_ready", "qk_ready"))
        ket_mm, ket_ready, kv_mm, kv_ready = (sem(n) for n in ("ket_mm", "ket_ready", "kv_mm", "kv_ready"))
        frs_ready, fox_scaled = sem("frs_ready"), sem("fox_scaled")
        gs_mm, gs_ready, go_mm, gla_scale, gla_done = (
            sem(n) for n in ("gs_mm", "gs_ready", "go_mm", "gla_scale", "gla_done"))
        fs_mm, fmax_ready, f_exp, fp_ready, fpt_mm, fpt_v, fpt_a, fo_mm, fo_a = (
            sem(n) for n in ("fs_mm", "fmax_ready", "f_exp", "fp_ready", "fpt_mm", "fpt_v", "fpt_a", "fo_mm", "fo_a"))

        UC = SLOTS
        SC = 2

        def numbered(*names):
            return {n: 2 * j + 1 for j, n in enumerate(names)}

        CPE = numbered("M2", "M4", "M8", "T4", "TT", "TZ", "Z", "X", "T64", "U", "Y")
        CV = numbered("T2", "T3", "T4", "TZ", "T64", "S")
        CA = numbered("M2", "M4", "M8", "TT", "Z", "X", "U", "Y")
        PPE = numbered("AC", "N", "BE", "T")
        PV, PA = {"load": 1, "AC": 2, "N": 4, "BE": 6}, {"load": 1, "V": 2, "T": 4}
        NCPE, NCV, NCA, NPPE, NPV, NPA = 22, 12, 16, 8, 7, 5

        def count(r, per, n):
            return r * per + n if isinstance(r, int) else r[0] * (2 * per) + (r[1] * per + n)

        def index(r, ahead=0):
            return count(r, 1, ahead)

        def parity(r):
            return r % 2 if isinstance(r, int) else r[1]

        block = ctx.enter_context(nc.Block())

        @block.sync
        def _(sp):
            for j in range(4):
                sp.dma_start(xt[:, 2 * j:2 * j + 2, 1:T + 1], dram["x"][:, 2 * j:2 * j + 2, :]).then_inc(x_in[j], 16)
                if j == 1:
                    sp.dma_start(par[:, :], dram["par"]).then_inc(par_in, 16)
            sp.dma_start(common[:, :], dram["c_common"]).then_inc(common_in, 16)
            sp.dma_start(selk[:, :, :], dram["c_prep"].rearrange("p (k h) -> p k h", k=4)).then_inc(selk_in, 16)
            with sp.Fori(0, UNITS // SLOTS) as i:
                for s in range(SLOTS):
                    sp.wait_ge(split_done, i * SLOTS + s + 1)
                    sp.dma_start(raw[:, s, :], dram["weights"][i * SLOTS + s]).then_inc(raw_in[s], 16)

        @block.gpsimd
        def _(pool):
            pool.sem_inc(split_done, UC)
            pool.memset(zero[:, :], 0.0).then_inc(zero_ready, 1)
            pool.wait_ge(zero_ready, 1)
            with pool.Fori(0, UNITS // SLOTS) as i:
                for s in range(SLOTS):
                    pool.wait_ge(units_used, i * SLOTS + s + 1)
                    pool.wait_ge(raw_in[s], i * 16 + 16)
                    pool.tensor_tensor(wh[:, s, :], raw[:, s, :],
                                       zero[:, :].to_broadcast([P, BLOCKS * P]), ALU.add).then_inc(split_hi, 1)
                    pool.wait_ge(split_hi, i * SLOTS + s + 1)
                    pool.tensor_tensor(wl[:, s, :], raw[:, s, :], wh[:, s, :].bitcast(F32),
                                       ALU.subtract).then_inc(split_done, 1)

        @block.tensor
        def _(pe):
            pe.sem_inc(units_used, UC)
            pe.sem_inc(sq_used, SC)
            pe.sem_inc(core_pe, NCPE)
            pe.sem_inc(bonus_mm, SC)

            def product(out, slot, b, hi, lo, start, stop):
                w_h, w_l = wh[:, slot, b * P:(b + 1) * P], wl[:, slot, b * P:(b + 1) * P]
                pe.matmul(out, w_h, hi, start=start, stop=False)
                pe.matmul(out, w_h, lo, start=False, stop=False)
                return pe.matmul(out, w_l, hi, start=False, stop=stop)

            def split_unit(u):
                pe.wait_ge(split_done, u + 1 + UC)

            def free_bank(t):
                pe.wait_ge(evacuated, t + 1)

            def part(stage, k):
                pe.wait_ge(lo_ready, plan(stage, "split") + k + 1 + SC)

            def dense(stage, source, hi, lo, n=T, units=None, skip=0, also=None):
                u0, t0 = UNIT0[stage] + skip, plan(stage, "tile") + skip
                with pe.Fori(0, (units or dict(STREAM)[stage]) // SLOTS) as i:
                    for s in range(SLOTS):
                        split_unit(i * SLOTS + (u0 + s))
                        free_bank(i * SLOTS + (t0 + s))
                        for k in range(KT):
                            if s == 0:
                                part(source, k)
                            mm = product(bank[(t0 + s) % 4][:, 0:n], (u0 + s) % SLOTS, k,
                                         hi[:, k, 0:n], lo[:, k, 0:n], k == 0, k == KT - 1)
                        mm.then_inc(units_used, 1)
                        if also:
                            also(i, s)

            def tile(stage, j, source, hi, lo):
                u, t = UNIT0[stage] + j, plan(stage, "tile") + j
                split_unit(u)
                free_bank(t)
                for k in range(KT):
                    part(source, k)
                    ins = product(bank[t % 4][:, :], u % SLOTS, k, hi[:, k, :], lo[:, k, :], k == 0, k == KT - 1)
                ins.then_inc(units_used, 1)

            def norm_total(stage):
                pe.wait_ge(sq_used, plan(stage, "sq") + KT + SC)
                pe.matmul(bank[4][:, :], ones, rstd[:, :], start=True, stop=True).then_inc(sum_mm, 1)

            def down(stage, source, hi, lo):
                u0, t0 = UNIT0[stage], plan(stage, "tile")
                with pe.Fori(0, 2) as i:
                    for s in range(4):
                        free_bank(i * 4 + (t0 + s))
                        for k in range(FT):
                            j = 3 * s + k // BLOCKS
                            if k % BLOCKS == 0:
                                split_unit(i * 12 + (u0 + j))
                            if s == 0:
                                part(source, k)
                            mm = product(bank[(t0 + s) % 4][:, :], (u0 + j) % SLOTS, k % BLOCKS,
                                         hi[:, k, :], lo[:, k, :], k == 0, k == FT - 1)
                            if k % BLOCKS == BLOCKS - 1 or k == FT - 1:
                                mm.then_inc(units_used, 1)

            def norm_sum(stage, n=T):
                for k in range(KT):
                    pe.wait_ge(sq_ready, plan(stage, "sq") + k + 1)
                    pe.matmul(bank[4][:, 0:n], ones, sq[:, k % 2, 0:n], start=(k == 0),
                              stop=(k == KT - 1)).then_inc(sq_used, 1)

            pe.wait_ge(common_in, 16)
            norm_total("norm0")
            split_unit(0)
            for j, m in enumerate("wa"):
                free_bank(j)
                for k in range(KT):
                    part("mix" + m, k)
                    mm = product(bank[j][:, :], 0, k, mixh[j][:, k, :], mixl[j][:, k, :], k == 0, k == KT - 1)
                mm.then_inc(units_used if j else tile_full, 1)
            for j in range(2):
                split_unit(1 + j)
                free_bank(2 + j)
                for k in range(KT):
                    part("mixg", k)
                    mm = product(bank[2 + j][:, :], 1 + j, k, mixh[0][:, k, :], mixl[0][:, k, :],
                                 k == 0, k == KT - 1)
                mm.then_inc(units_used, 1)
            part("mid", 0)
            for stage in ("w2", "a2"):
                u, t0 = UNIT0[stage], plan(stage, "tile")
                split_unit(u)
                for j in range(KT):
                    free_bank(t0 + j)
                    product(bank[(t0 + j) % 4][:, :], u % SLOTS, j, midh[:, :], midl[:, :], True, True)\
                        .then_inc(units_used if j == KT - 1 else tile_full, 1)
            dense("k", "mixk", mixh[1], mixl[1])
            dense("r", "mixr", mixh[0], mixl[0], units=4)
            pe.wait_ge(selk_in, 16)

            def knorm_sum(i, s):
                for j in (2 * s, 2 * s + 1):
                    pe.wait_ge(sq_ready, plan("knorm", "sq") + j + 1)
                    pe.matmul(psum[0:8, 4 + j // 4, :], selk[:, j % 4, :], sq[:, j % 2, :], start=(j % 4 == 0),
                              stop=(j % 4 == 3)).then_inc(sq_used, 1)

            dense("r", "mixr", mixh[0], mixl[0], units=4, skip=4, also=knorm_sum)
            for j in range(KT):
                tile("v", j, "mixv", mixh[1], mixl[1])
                if j % 2 == 0:
                    pe.wait_ge(rn_ready, 1)
                    pe.wait_ge(bsel_in, 16)
                    for n in (j, j + 1):
                        if n >= 2:
                            pe.wait_ge(kk_ready, n - 1)
                        pe.matmul(bank[4 + n % 2][:, :], bsel[0:8, n % 4, :], bonus[0:8, n // 4, :], start=True,
                                  stop=True).then_inc(bsel_mm, 1)
                else:
                    for n in (j - 1, j):
                        pe.wait_ge(scan_ready, n + 1)
                        pe.matmul(psum[0:8, 6 + n // 4, :], selk[:, n % 4, :], sq[:, n % 2, :], start=(n % 4 == 0),
                                  stop=(n % 4 == 3)).then_inc(bonus_mm, 1)

            pe.wait_ge(prep_done, 4 + 1)
            pe.wait_ge(evacuated, plan("v", "tile") + 8 + UC)

            def core_round(r, last=False):
                c, n = parity(r), 1 - parity(r)

                def seen_v(what, g):
                    pe.wait_ge(core_v, count(r, NCV, NCV + CV[what] + g))

                def seen_a(what, g):
                    pe.wait_ge(core_a, count(r, NCA, NCA + CA[what] + g))

                def each(step, count_=True):
                    for g in range(2):
                        for j, q in enumerate((2 * g, 2 * g + 1)):
                            ins = step(4 * g, g, j, q)
                        if count_:
                            ins.then_inc(core_pe, 1)

                def mm(out, lhsT, rhs, start=True, stop=True):
                    return pe.matmul(out, lhsT, rhs, start=start, stop=stop)

                def s2(o, g, j, q):
                    b = bank[o + c]
                    mm(b[:, j * 256:j * 256 + P], AD[c][:, q, :], ND[c][:, q, :])
                    return mm(b[:, j * 256 + P:j * 256 + 256], ND[c][:, q, :], AD[c][:, q, :])

                def s3(o, g, j, q):
                    if j == 0:
                        seen_a("M2", g)
                    b = bank[o + n]
                    mm(b[:, j * 256:j * 256 + P], TMA[:, q, 256:384], T1[c][:, q, :])
                    mm(b[:, j * 256 + P:j * 256 + 256], TMA[:, q, 256:384], TMA[:, q, P:256])
                    return mm(bank[o + 2][:, j * P:(j + 1) * P], TMA[:, q, P:256], TMA[:, q, 256:384])

                def s4(o, g, j, q):
                    if j == 0:
                        seen_v("T2", g)
                        seen_a("M4", g)
                    b = bank[o + c]
                    mm(b[:, j * 256:j * 256 + P], TMA[:, q, 256:384], TMA[:, q, 0:P])
                    return mm(b[:, j * 256 + P:j * 256 + 256], TMA[:, q, P:256], TMA[:, q, 256:384])

                def s5(o, g, j, q):
                    if j == 0:
                        seen_v("T3", g)
                        seen_a("M8", g)
                    return mm(bank[o + n][:, j * P:(j + 1) * P], TMA[:, q, 256:384], TMA[:, q, 0:P])

                def s6(o, g, j, q):
                    if j == 0:
                        seen_v("T4", g)
                    pe.transpose(bank[o + 2][:, j * 256:j * 256 + P], TMA[:, q, 0:P], ident)
                    return mm(bank[o + 2][:, j * 256 + P:j * 256 + 256], AO32[c][:, q, :], TMA[:, q, 0:P])

                def s7(o, g, j, q):
                    if j == 0:
                        seen_a("TT", g)
                    b = bank[o + c]
                    mm(b[:, j * 256:j * 256 + P], TZ[:, q, 0:P], TZ[:, q, P:256])
                    return mm(b[:, j * 256 + P:j * 256 + 256], TZ[:, q, P:256], TZ[:, q, 0:P])

                def s8(o, g, j, q):
                    if j == 0:
                        seen_v("TZ", g)
                    return mm(bank[o + n][:, j * P:(j + 1) * P], AO64[c][:, q, :], TMA[:, q, 0:P])

                def sx(o, g, j, q):
                    x_ = bank[o + 2][:, j * P:(j + 1) * P]
                    mm(x_, AR[c][:, q, 0:P], SS[:, q, :], stop=False)
                    return mm(x_, BE[c][:, q, 0:P], VT[c][:, q, :], start=False)

                def s9(o, g, j, q):
                    if j == 0:
                        seen_a("Z", g)
                    return mm(bank[o + c][:, j * P:(j + 1) * P], TZ[:, q, 0:P], TZ[:, q, P:256])

                def su(o, g, j, q):
                    if j == 0:
                        seen_v("T64", g)
                        seen_a("X", g)
                    return mm(bank[o + n][:, j * P:(j + 1) * P], TMA[:, q, 0:P], XX[:, q, :])

                def y_d(o, j):
                    return bank[o + 2][:, j * CH:(j + 1) * CH], bank[o + c][:, j * P:(j + 1) * P]

                def sy(o, g, j, q):
                    y, d = y_d(o, j)
                    mm(y, SS[:, q, :], AR[c][:, q, P:192], start=(j == 0), stop=False)
                    mm(y, VT[c][:, q, :], BE[c][:, q, P:192], start=False, stop=False)
                    return mm(d, TBK[c][:, q, P:256], VT[c][:, q, :], start=(j == 0), stop=False)

                def sz(o, g, j, q):
                    if j == 0:
                        seen_a("U", g)
                    y, d = y_d(o, j)
                    mm(y, UU[:, q, :], CC[c][:, q, :], start=False, stop=(j == 1))
                    return mm(d, TBK[c][:, q, 0:P], UU[:, q, :], start=False, stop=(j == 1))

                pe.wait_ge(pro_v, count(r, NPV, NPV))
                pe.wait_ge(pro_a, count(r, NPA, NPA))
                each(s2)
                pe.wait_ge(core_v, count(r, NCV, NCV))
                pe.wait_ge(core_a, count(r, NCA, NCA))
                def more(what, *groups):
                    if not last:
                        prepare(r, 1, what, groups)

                each(s3)
                each(s4)
                more("AC", 0)
                each(s5)
                more("AC", 1)
                each(s6)
                more("N", 0)
                each(s7)
                more("N", 1)
                each(s8)
                more("BE", 0)
                each(sx)
                more("BE", 1)
                each(s9)
                more("T", 0, 1)
                each(su)
                each(sy, False)
                each(sz)

            def prepare(r, ahead, what, groups=(0, 1)):
                c = (parity(r) + ahead) % 2

                def ready(sem_, per, n):
                    pe.wait_ge(sem_, count(r, per, ahead * per + n))

                for g in groups:
                    b = bank[4 * g + 3]
                    if what == "AC":
                        ready(pro_v, NPV, PV["load"])
                        ready(pro_a, NPA, PA["load"])
                    elif what == "N":
                        ready(pro_v, NPV, PV["AC"] + g)
                    elif what == "BE":
                        ready(pro_a, NPA, PA["V"] + g)
                    else:
                        ready(pro_v, NPV, PV["BE"] + g)
                    for j, q in enumerate((2 * g, 2 * g + 1)):
                        if what == "AC":
                            ins = pe.matmul(b[:, j * 192:(j + 1) * 192], BB[:, q, :], AR[c][:, q, :], start=True, stop=True)
                        elif what == "BE":
                            ins = pe.matmul(b[:, j * 192:(j + 1) * 192], KB[:, q, :], AR[c][:, q, :], start=True, stop=True)
                        elif what == "N":
                            pe.matmul(b[:, j * P:(j + 1) * P], AR[c][:, q, 0:P], BB[:, q, :], start=True, stop=True)
                            ins = pe.transpose(b[:, 256 + j * P:256 + (j + 1) * P], VB[:, q, :], ident)
                        else:
                            pe.transpose(b[:, j * 256:j * 256 + P], BB[:, q, :], ident)
                            ins = pe.transpose(b[:, j * 256 + P:j * 256 + 256], KB[:, q, :], ident)
                    ins.then_inc(pro_pe, 1)

            for what in ("AC", "N", "BE", "T"):
                prepare(0, 0, what)
            with pe.Fori(0, 7) as i:
                core_round((i, 0))
                core_round((i, 1))
            core_round(14)
            core_round(15, last=True)

            pe.wait_ge(core_v, NCV * 17)
            pe.wait_ge(core_a, NCA * 17)
            for j in range(KT):
                u, t = UNIT0["g2"] + j // 4, plan("g2", "tile") + j
                part("gmid", 1)
                if j % 4 == 0:
                    split_unit(u)
                free_bank(t)
                for b in range(2):
                    mm_ = product(bank[t % 4][:, :], u % SLOTS, 2 * (j % 4) + b, gmidh[:, b, :], gmidl[:, b, :],
                                  b == 0, b == 1)
                mm_.then_inc(units_used if j % 4 == 3 else tile_full, 1)
            pe.wait_ge(cpost_in, 16)
            pe.wait_ge(evacuated, plan("g2", "tile") + 8 + UC)
            for k in range(KT + 2):
                if k < KT:
                    half, q = divmod(k, 4)
                    if k >= 2:
                        pe.wait_ge(post_v, k - 1)
                    pe.matmul(bank[k % 2][:, :], blk64, seq["r"][:, 8 * half:8 * half + 8, q, :], start=True, stop=True)
                    pe.matmul(bank[6 + k % 2][:, :], c_post[0:8, q, :], bonus[0:8, half, :],
                              start=True, stop=True).then_inc(mean_pe, 1)
                if k >= 2:
                    n = k - 2
                    pe.wait_ge(post_sq, n + 1)
                    if n >= 4:
                        pe.wait_ge(post_ln, n - 3)
                    pe.matmul(bank[2 + n % 4][:, :], blk64, sq[:, n % 2, :], start=True, stop=True).then_inc(var_pe, 1)
            pe.wait_ge(post_ln, KT)
            dense("o", "post", acth, actl, units=4)
            norm_sum("norm_mem0", MEM)
            dense("o", "post", acth, actl, units=4, skip=4)

            def values_by_token(l):
                for mt in range(2):
                    for c in range(2):
                        for j in range(4):
                            ins = pe.transpose(bank[4 + 2 * mt + c][:, j * P:(j + 1) * P],
                                               vals[:, 4 * c + j, mt * P:(mt + 1) * P], ident)
                        ins.then_inc(vt_mm, 1)

            def memory_side():
                dense("kv0", "norm_mem0", memh, meml, n=MEM, units=4)
                norm_sum("norm_x0")
                dense("kv0", "norm_mem0", memh, meml, n=MEM, units=12, skip=4)
                pe.wait_ge(rstd_ready, plan("norm_x0", "rstd") + 1)
                pe.wait_ge(evacuated, plan("kv0", "tile") + 16 + UC)
                values_by_token(0)

            def attention(l):
                def scores(h):
                    for tt in range(4):
                        for k in range(2):
                            ins = pe.matmul(bank[4 + tt // 2][:, (tt % 2) * MEM:(tt % 2 + 1) * MEM],
                                            query[:, 2 * h + k, tt * P:(tt + 1) * P], keys[:, 2 * h + k, :],
                                            start=(k == 0), stop=(k == 1))
                    ins.then_inc(sc_mm, 1)

                dense(f"q{l}", f"norm_x{l}", acth, actl, units=4)
                pe.wait_ge(vt_ready, 4 * (l + 1))
                pe.wait_ge(evacuated, plan(f"q{l}", "tile") + 2 + UC)
                scores(0)
                dense(f"q{l}", f"norm_x{l}", acth, actl, units=4, skip=4)
                pe.wait_ge(evacuated, plan(f"q{l}", "tile") + 8 + UC)
                pe.wait_ge(p_exp, 4 * l + 1)
                scores(1)
                for h in range(4):
                    n = 4 * l + h
                    pe.wait_ge(p_ready, n + 1)
                    if h:
                        pe.wait_ge(pt_v, n)
                        pe.wait_ge(pt_a, n)
                    for mt in range(2):
                        for tt in range(4):
                            ins = pe.transpose(bank[6 + mt][:, tt * P:(tt + 1) * P],
                                               prob[:, h % 2, tt, mt * P:(mt + 1) * P], ident)
                    ins.then_inc(pt_mm, 1)
                    if h < 2:
                        pe.wait_ge(p_exp, n + 2)
                        scores(h + 2)
                    pe.wait_ge(pt_v, n + 1)
                    pe.wait_ge(pt_a, n + 1)
                    for dt in range(2):
                        t = plan(f"heads{l}", "tile") + 2 * h + dt
                        free_bank(t)
                        for mt in range(2):
                            ins = pe.matmul(bank[t % 4][:, :], vtok[:, mt, (2 * h + dt) * P:(2 * h + dt + 1) * P],
                                            probt[:, h % 2, mt, :], start=(mt == 0), stop=(mt == 1))
                        ins.then_inc(tile_full, 1)
                dense(f"xo{l}", f"heads{l}", headh, headl)

            def ffn(l):
                up, norm = f"up{l}", f"norm_ffn{l}"
                tile(up, 0, norm, acth, actl)
                norm_total(norm)
                dense(up, norm, acth, actl, units=2 * FT - 4, skip=1)
                for j in range(2 * FT - 3, 2 * FT):
                    tile(up, j, norm, acth, actl)
                down(f"down{l}", up, hidh, hidl)

            def convolution():
                norm_total("norm_conv")

                def taps(k0, batches=1):
                    for b in range(batches):
                        for s in range(2):
                            k = k0 + s
                            pe.wait_ge(diag_ready, k - 1 + 2 * b)
                            pe.wait_ge(glu_ready, k + 1)
                            if k >= 4:
                                pe.wait_ge(tap_ready, k - 3)
                            for j in range(PETAPS):
                                ins = pe.matmul(bank[6 + s][:, :], diag[s][:, j, :],
                                                gp[:, k, b * PETAPS + j:b * PETAPS + j + T],
                                                start=(b == 0 and j == 0), stop=(b == batches - 1 and j == PETAPS - 1))
                            ins.then_inc(tap_mm, 1)

                dense("cin", "norm_conv", acth, actl, units=4)
                norm_sum("norm_mem1", MEM)
                dense("cin", "norm_conv", acth, actl, units=8, skip=4)
                taps(2)
                dense("cin", "norm_conv", acth, actl, units=4, skip=12)
                taps(4)
                dense("kv1", "norm_mem1", memh, meml, n=MEM, units=8)
                taps(6, 2)
                dense("kv1", "norm_mem1", memh, meml, n=MEM, units=4, skip=8)
                pe.wait_ge(rstd_ready, plan("norm_mem1", "rstd") + 1)
                for k in range(KT):
                    pe.wait_ge(u_ready, k + 1)
                    ins = pe.matmul(bank[5][:, :], ones, ub[:, k, :], start=(k == 0), stop=(k == KT - 1))
                ins.then_inc(mean_mm, 1)
                norm_sum("ln")
                dense("cout", "ln", acth, actl)
                dense("kv1b", "norm_mem1", memh, meml, n=MEM)
                norm_total("norm_x1")
                pe.wait_ge(rstd_ready, plan("norm_x1", "rstd") + 1)
                pe.wait_ge(evacuated, plan("kv1b", "tile") + 4 + UC)
                values_by_token(1)

            def hybrid():
                t0 = plan("in2", "tile")
                tile("in2", 0, "norm_h", acth, actl)
                pe.wait_ge(acc_ready, 1)
                pe.matmul(bank[4][:, :], ones, acc_x[:, :], start=True, stop=True)
                pe.matmul(bank[5][:, :], ones, acc_y[:, :], start=True, stop=True).then_inc(sum_mm, 1)

                def inner(skip, n):
                    dense("in2", "norm_h", acth, actl, units=n, skip=skip)

                inner(1, 12)
                pe.wait_ge(evacuated, t0 + 13 + UC)
                pe.wait_ge(rstd_ready, plan("norm_h", "rstd") + 1)
                for j in range(8):
                    tt = j % 4
                    if j >= 4:
                        pe.wait_ge(vt2_ready, j - 3)
                    for k in range(4):
                        ins = pe.transpose(bank[4 + tt][:, k * P:(k + 1) * P],
                                           (gv if j < 4 else fv)[:, k, tt * P:(tt + 1) * P], ident)
                    ins.then_inc(vt2_mm, 1)
                inner(13, 4)
                pe.wait_ge(hyb_in, 32)
                for p in range(2):
                    pe.wait_ge(vt2_ready, 5 + p)
                    pe.matmul(bank[4 + p][:, :], w2g[:, p * P:(p + 1) * P], small[:, :], start=True,
                              stop=True).then_inc(z_mm, 1)
                inner(17, 8)

                def gate(n):
                    tile("in2", 25 + n, "norm_h", acth, actl)

                def chunk_kv(c):
                    if c >= 4:
                        pe.wait_ge(kv_ready, c - 3)
                    r = slice(64 * (c % 2), 64 * (c % 2) + 64)
                    for p in range(2):
                        ins = pe.matmul(bank[4 + c % 4][:, p * 256:(p + 1) * 256], ket[r, c // 2, p * P:(p + 1) * P],
                                        gvt[r, c // 2, p * 256:(p + 1) * 256], start=True, stop=True)
                    ins.then_inc(kv_mm, 1)

                def fox_sum(j):
                    pe.wait_ge(sq_ready, plan("fox_norm", "sq") + j + 1)
                    if j >= 2:
                        pe.wait_ge(frs_ready, j - 1)
                    pe.matmul(bank[6 + j % 2][:, :], blk64, sq[:, j % 2, :], start=True, stop=True).then_inc(sq_used, 1)

                def gla_scores(h):
                    r, p = slice(64 * (h % 2), 64 * (h % 2) + 64), h // 2
                    if h >= 2:
                        pe.wait_ge(gla_scale, h - 1)
                    for tt in range(4):
                        t_ = slice(tt * P, (tt + 1) * P)
                        ins = pe.matmul(bank[4 + h % 2][:, t_], gqk[r, 2 + p, t_], gqk[r, p, t_], start=True, stop=True)
                    ins.then_inc(gs_mm, 1)

                def gla_head(h):
                    r, p = slice(64 * (h % 2), 64 * (h % 2) + 64), h // 2
                    if h >= 2:
                        pe.wait_ge(gla_done, h - 1)
                    pe.wait_ge(gs_ready, h + 1)
                    o = bank[6 + h % 2]
                    for tt in range(4):
                        pe.matmul(o[:, tt * P:(tt + 1) * P], gvt[:, tt, h * P:(h + 1) * P],
                                  sct[:, h % 2, tt * P:(tt + 1) * P], start=(tt == 0), stop=False)
                    for c in range(1, NCH):
                        ins = pe.matmul(o[:, c * CH:(c + 1) * CH], states[r, c - 1, p, :],
                                        gqk[r, p, c * CH:(c + 1) * CH], start=False, stop=(c == NCH - 1))
                    ins.then_inc(go_mm, 1)

                def gla_sum(h):
                    pe.wait_ge(sq_ready, plan("gla", "sq") + h + 1)
                    pe.matmul(bank[4 + h % 2][:, :], ones, sq[:, h % 2, :], start=True, stop=True).then_inc(sq_used, 1)

                gate(0)
                gate(1)
                pe.wait_ge(qk_ready, 1)
                pe.wait_ge(vt2_ready, 8)
                for b in range(2):
                    for tt in range(2):
                        for p in range(2):
                            ins = pe.transpose(bank[6 + b][:, tt * 256 + p * P:tt * 256 + (p + 1) * P],
                                               gqk[:, 2 + p, (2 * b + tt) * P:(2 * b + tt + 1) * P], ident)
                    ins.then_inc(ket_mm, 1)
                gate(2)
                pe.wait_ge(ket_ready, 2)
                pe.wait_ge(z_ready, 2)
                for c in range(4):
                    chunk_kv(c)
                gate(3)
                for c in range(4, NCH - 1):
                    chunk_kv(c)
                gate(4)
                pe.wait_ge(kv_ready, NCH - 1)
                for j in range(0, 8, 2):
                    fox_sum(j)
                    fox_sum(j + 1)
                    gate(5 + j // 2)
                pe.wait_ge(frs_ready, 8)
                gla_scores(0)
                gate(9)
                for h in range(4):
                    gla_head(h)
                    if h < 3:
                        gla_scores(h + 1)
                    gate(10 + h)
                    gla_sum(h)
                gate(14)

                def fox_scores(h):
                    r, p = slice(64 * (h % 2), 64 * (h % 2) + 64), h // 2
                    for qt in range(4):
                        b, o = ((4, 0), (4, P), (5, 0), (6, 0))[qt]
                        n = (qt + 1) * P
                        pe.matmul(bank[b][:, o:o + n], fq[r, p, qt * P:n], fk[r, p, 0:n], start=True, stop=False)
                        pe.matmul(bank[b][:, o:o + n], hyb[:, T + 2 * P + h * P:T + 3 * P + h * P], small[:, 0:n],
                                  start=False, stop=False)
                        ins = pe.matmul(bank[b][:, o + qt * P:o + n], ident, fmask, start=False, stop=True)
                    ins.then_inc(fs_mm, 1)

                pe.wait_ge(fox_scaled, 8)
                pe.wait_ge(gla_scale, 4)
                pe.wait_ge(gla_done, 4)
                fox_scores(0)
                gate(15)
                pe.wait_ge(f_exp, 1)
                fox_scores(1)
                pe.wait_ge(evacuated, t0 + 41 + UC)
                for h in range(8):
                    p = h // 2
                    pe.wait_ge(fp_ready, h + 1)
                    if h:
                        pe.wait_ge(fpt_v, h)
                        pe.wait_ge(fpt_a, h)
                    for kt in range(4):
                        for qt in range(kt, 4):
                            b, o = ((0, 0), (1, 0), (2, 0), (2, 256))[kt]
                            ins = pe.transpose(bank[b][:, o + (qt - kt) * P:o + (qt - kt + 1) * P],
                                               fp[:, h % 2, FOX_OFF[qt] + kt * P:FOX_OFF[qt] + (kt + 1) * P], ident)
                    ins.then_inc(fpt_mm, 1)
                    if h < 6:
                        pe.wait_ge(f_exp, h + 2)
                        fox_scores(h + 2)
                    pe.wait_ge(fpt_v, h + 1)
                    pe.wait_ge(fpt_a, h + 1)
                    if h >= 2:
                        pe.wait_ge(fo_a, h - 1)
                    for kt in range(4):
                        n = (4 - kt) * P
                        ins = pe.matmul(bank[3 + 4 * (h % 2)][:, kt * P:T], fvt[:, kt, p * P:(p + 1) * P],
                                        fpt[:, h % 2, FOX_TOFF[kt]:FOX_TOFF[kt] + n], start=(kt == 0), stop=(kt == 3))
                    ins.then_inc(fo_mm, 1)
                pe.wait_ge(fo_a, 8)
                u0, t0 = UNIT0["branch"], plan("branch", "tile")
                with pe.Fori(0, 2) as i:
                    for s in range(4):
                        split_unit(i * 4 + (u0 + s))
                        for b, source in enumerate(("gla", "fox")):
                            free_bank(i * 8 + (t0 + 2 * s + b))
                            for k in range(4):
                                if s == 0:
                                    part(source, k)
                                ins = product(bank[(t0 + 2 * s + b) % 4][:, :], (u0 + s) % SLOTS, 4 * b + k,
                                              acth[:, 4 * b + k, :], actl[:, 4 * b + k, :], k == 0, k == 3)
                            ins.then_inc(units_used if b else tile_full, 1)
                dense("out2", "branch", yh, yl)

            def last_norm():
                norm_total("last")

            memory_side()
            attention(0)
            ffn(0)
            convolution()
            attention(1)
            ffn(1)
            hybrid()
            ffn(2)
            last_norm()

        @block.scalar
        def _(act):
            act.sem_inc(evacuated, UC)
            chain = Chain(act, act_chain)

            def hold():
                act.sem_inc(act_held, 1)

            def square(stage, source, n=T, ready=None):
                with act.Fori(0, KT // 2) as i:
                    for s in range(2):
                        if ready:
                            ready(i * 2 + s)
                        act.wait_ge(sq_used, i * 2 + (plan(stage, "sq") + s + 1))
                        hold()
                        act.activation(sq[:, s, 0:n], source(i * 2 + s), ACT.Square).then_inc(sq_ready, 1)

            def rsqrt(stage, bias, n=T):
                act.wait_ge(sq_used, plan(stage, "sq") + KT + SC)
                chain.step(act.activation(rstd[:, 0:n], bank[4][:, 0:n], ACT.Ln, bias=bias, scale=1.0 / D))
                chain.wait()
                act.activation(rstd[:, 0:n], rstd[:, 0:n], ACT.Exp, scale=-0.5).then_inc(rstd_ready, 1)

            def x_is_ready(stage):
                return lambda k: act.wait_ge(x_ready, k + (plan(stage, "x") + 1 + SC))

            def mix_part(k, name):
                act.activation(parts[:, k, :], x(k), ACT.Identity,
                               scale=omu[:, bass.ds(k + MU[name] * KT, 1)]).then_inc(part_ready, 1)

            def high_part(stage, to, n=T, count=KT, before=None, then=None):
                g0, v0 = plan(stage, "split"), plan(stage, "val")
                if before:
                    before()
                with act.Fori(0, count // 2) as i:
                    for s in range(2):
                        act.wait_ge(val_ready, i * 2 + (v0 + s + 1))
                        hold()
                        act.activation(to[:, i * 2 + s, 0:n], tmp[:, (g0 + s) % 2, 0:n],
                                       ACT.Identity).then_inc(hi_ready, 1)
                        if then:
                            mix_part(i * 2 + s, then)

            def bank_of(t):
                return bank[t % 4]

            def tile_seq(name, rounds=2):
                u0, t0 = UNIT0[name], plan(name, "tile")
                with act.Fori(0, rounds) as i:
                    for s in range(4):
                        act.wait_ge(units_used, i * 4 + (u0 + s + 1 + UC))
                        hold()
                        act.activation(seq[name][:, bass.ds(i * 8, 8), s, :],
                                       bank_of(t0 + s)[:, :].rearrange("p (c t) -> p c t", t=CH),
                                       ACT.Identity).then_inc(evacuated, 1)

            def deltas(stage, buf, per, bias=None, skip=0, count=8):
                t0, x0 = plan(stage, "tile"), plan(stage, "x") + skip
                with act.Fori(0, count // 4) as i:
                    for s in range(4):
                        act.wait_ge(units_used, i * (4 * per) + (UNIT0[stage] + (skip + s + 1) * per + UC))
                        act.wait_ge(x_ready, i * 4 + (x0 + s + 1))
                        hold()
                        act.activation(buf[:, s % 2, :], bank_of(t0 + s)[:, :], ACT.Identity,
                                       bias=bias(i * 4 + s) if bias else 0.0).then_inc(evacuated, 1)

            def deltas_normed(stage, buf, per, norm, gain=None, split=True, bias=None):
                t0, x0, sq0 = plan(stage, "tile"), plan(stage, "x"), plan(norm, "sq")
                g0, v0 = (plan(norm, "split"), plan(norm, "val")) if split else (0, 0)
                n = 2 if gain else 1
                with act.Fori(0, 2) as i:
                    for s in range(4):
                        act.wait_ge(units_used, i * (4 * per) + (UNIT0[stage] + (s + 1) * per + UC))
                        act.wait_ge(x_ready, i * 4 + (x0 + s + 1))
                        hold()
                        act.activation(buf[:, s % 2, :], bank_of(t0 + s)[:, :], ACT.Identity,
                                       bias=bias(i * 4 + s) if bias else 0.0).then_inc(evacuated, 1)
                        act.wait_ge(x_ready, i * 4 + (x0 + s + 1 + SC))
                        for j in range(n):
                            act.wait_ge(sq_used, i * (4 * n) + (sq0 + n * s + j + 1))
                            hold()
                            act.activation(sq[:, (n * s + j) % 2, :], x(i * 4 + s), ACT.Square,
                                           scale=pc(gain, i * 4 + s) if j else 1.0).then_inc(sq_ready, 1)
                        if not split:
                            continue
                        act.wait_ge(val_ready, i * 4 + (v0 + s + 1))
                        hold()
                        act.activation(acth[:, i * 4 + s, :], tmp[:, (g0 + s) % 2, :], ACT.Identity).then_inc(hi_ready, 1)

            def total_rms(norm):
                act.wait_ge(sum_mm, plan(norm, "total") + 1)
                chain.step(act.activation(rstd[:, :], bank[4], ACT.Ln, bias=b_eps, scale=1.0 / D))
                chain.wait()
                act.activation(rstd[:, :], rstd[:, :], ACT.Exp, scale=-0.5).then_inc(rstd_ready, 1)

            for k in range(KT):
                act.wait_ge(x_in[k // 2], 16)
                act.wait_ge(sq_used, plan("norm0", "sq") + k + 1)
                act.activation(sq[:, k % 2, :], x(k), ACT.Square).then_inc(sq_ready, 1)
            act.wait_ge(omu_ready, 1)
            total_rms("norm0")
            with act.Fori(0, KT) as k:
                act.wait_ge(h_ready, k + 1)
                hold()
                mix_part(k, "w")
            high_part("mixw", mixh[0], then="a")
            act.dma_start(bsel[:, :, :], dram["c_post"].rearrange("p (k m) -> p k m", k=4)).then_inc(bsel_in, 16)
            high_part("mixa", mixh[1], then="g")

            def reuse(stage):
                return lambda: act.wait_ge(units_used, UNIT0[stage] + dict(STREAM)[stage] + UC)

            high_part("mixg", mixh[0], before=reuse("lora_in"), then="k")
            g = plan("mid", "split")
            act.wait_ge(tile_full, 1)
            act.wait_ge(lo_ready, g + 1)
            act.activation(tmp[0:64, g % 2, :], bank[0][0:64, :], ACT.Tanh).then_inc(evacuated, 1)
            act.wait_ge(units_used, 1 + UC)
            act.activation(tmp[64:P, g % 2, :], bank[1][64:P, :], ACT.Identity).then_inc(evacuated, 1)
            act.wait_ge(evacuated, 2 + UC)
            act.activation(midh[:, :], tmp[:, g % 2, :], ACT.Identity).then_inc(hi_ready, 1)
            for j in range(2):
                act.wait_ge(units_used, 2 + j + UC)
                act.activation(gbuf[:, j, :], bank[2 + j][:, :], ACT.Sigmoid).then_inc(evacuated, 1)
            act.wait_ge(units_used, UNIT0["lora_in"] + 1 + UC)
            g0, v0 = plan("mixk", "split"), plan("mixk", "val")
            for n in range(4):
                for k in (2 * n, 2 * n + 1):
                    act.wait_ge(val_ready, v0 + k + 1)
                    act.activation(mixh[1][:, k, :], tmp[:, (g0 + k) % 2, :], ACT.Identity).then_inc(hi_ready, 1)
                stage, bias, to, full = (("w2", "w0", "w", 2), ("a2", "a0", "a", 9))[n // 2]
                for j in range(4 * (n % 2), 4 * (n % 2) + 4):
                    if j < KT - 1:
                        act.wait_ge(tile_full, full + j)
                    else:
                        act.wait_ge(units_used, UNIT0[stage] + 1 + UC)
                    half, q = divmod(j, 4)
                    act.activation(seq[to][:, 8 * half:8 * half + 8, q, :],
                                   bank_of(plan(stage, "tile") + j)[:, :].rearrange("p (c t) -> p c t", t=CH),
                                   ACT.Sigmoid, bias=pc(bias, j)).then_inc(evacuated, 1)
            act.wait_ge(evacuated, 4 + UC)
            for j in range(2):
                act.activation(gmidh[:, j, :], gbuf[:, j, :], ACT.Identity).then_inc(hi_ready, 1)
            high_part("mixr", mixh[0], before=reuse("gate_in"))
            tile_seq("k")
            high_part("mixv", mixh[1], before=reuse("k"))
            tile_seq("r", 1)
            assert plan("r", "tile") % 4 == 0 and plan("v", "tile") % 4 == 0
            for s in range(4):
                for j in (2 * s, 2 * s + 1):
                    act.wait_ge(sq_used, plan("knorm", "sq") + j + 1)
                    act.activation(sq[:, j % 2, :].rearrange("p (c t) -> p c t", t=CH),
                                   seq["k"][:, 8 * (j // 4):8 * (j // 4) + 8, j % 4, :], ACT.Square,
                                   scale=pc("k_k", j)).then_inc(sq_ready, 1)
                act.wait_ge(units_used, UNIT0["r"] + 5 + s + UC)
                act.activation(seq["r"][:, 8:16, s, :], bank[s].rearrange("p (c t) -> p c t", t=CH),
                               ACT.Identity).then_inc(evacuated, 1)
            act.wait_ge(kss_ready, 1)
            chain.step(act.activation(bonus[0:8, :, :], bonus[0:8, :, :], ACT.Ln))
            chain.wait()
            act.activation(bonus[0:8, :, :], bonus[0:8, :, :], ACT.Exp, bias=eps[0:8, 3:4], scale=-0.5).then_inc(rn_ready, 1)
            for p in range(4):
                for j in (2 * p, 2 * p + 1):
                    act.wait_ge(units_used, UNIT0["v"] + j + 1 + UC)
                    act.activation(seq["v"][:, 8 * (j // 4):8 * (j // 4) + 8, j % 4, :],
                                   bank[j % 4].rearrange("p (c t) -> p c t", t=CH), ACT.Identity).then_inc(evacuated, 1)
                if p:
                    act.wait_ge(prep_done, p + 1)
                for j in (2 * p, 2 * p + 1):
                    act.wait_ge(scan_ready, j + 1)
                    act.activation(pp[:, j % 2, :], cs[:, j % 4, :], ACT.Exp, scale=-RSQRT_E)
                    act.activation(pi[:, j % 2, :], cs[:, j % 4, :], ACT.Exp, scale=RSQRT_E)
                    w_ = seq["w"][:, 8 * (j // 4):8 * (j // 4) + 8, j % 4, :]
                    act.activation(w_, w_, ACT.Exp, scale=-RSQRT_E).then_inc(decay_ready, 1)
            act.wait_ge(prep_done, 4 + 1)
            act.dma_start(c_core[:, :], dram["c_core"]).then_inc(ccore_in, 16)

            act.sem_inc(core_a, NCA)

            def two(ap):
                return ap.rearrange("p (q t) -> p q t", q=2)

            def core_load(r, ahead):
                act.wait_ge(core_pe, count(r, NCPE, NCPE))
                if ahead:
                    act.wait_ge(pro_pe, count(r, NPPE, NPPE))
                hold()
                it, c = index(r, ahead), (parity(r) + ahead) % 2
                for h in range(2):
                    p = slice(64 * h, 64 * h + 64)
                    act.activation(BB[p, :, p], seq["a"][p, it, :, :], ACT.Identity)
                    act.activation(VB[p, :, p], seq["v"][p, it, :, :], ACT.Identity)
                act.activation(AR[c][:, :, P:192], seq["r"][:, it, :, :], ACT.Identity).then_inc(pro_a, 1)

            def core_prepared(r, ahead, what, groups=(0, 1)):
                c = (parity(r) + ahead) % 2
                for g in groups:
                    b = bank[4 * g + 3]
                    if what == "V":
                        act.wait_ge(pro_pe, count(r, NPPE, ahead * NPPE + PPE["N"] + g))
                        act.wait_ge(pro_v, count(r, NPV, ahead * NPV + PV["N"] + g))
                        act.activation(VT[c][:, 2 * g:2 * g + 2, :], two(b[:, 256:512]), ACT.Identity).then_inc(pro_a, 1)
                    else:
                        act.wait_ge(pro_pe, count(r, NPPE, ahead * NPPE + PPE["T"] + g))
                        act.activation(TBK[c][:, 2 * g:2 * g + 2, :], two(b), ACT.Identity).then_inc(pro_a, 1)

            def core_round(r, last=False):
                c, n = parity(r), 1 - parity(r)

                def pe_step(what, g):
                    act.wait_ge(core_pe, count(r, NCPE, NCPE + CPE[what] + g))

                for g in range(2):
                    pe_step("M2", g)
                    act.activation(TMA[:, 2 * g:2 * g + 2, P:384], two(bank[4 * g + c]), ACT.Identity).then_inc(core_a, 1)
                for g in range(2):
                    pe_step("M4", g)
                    act.activation(TMA[:, 2 * g:2 * g + 2, P:256], two(bank[4 * g + n])[:, :, P:256], ACT.Identity)
                    act.activation(TMA[:, 2 * g:2 * g + 2, 256:384], two(bank[4 * g + 2][:, 0:256]),
                                   ACT.Identity).then_inc(core_a, 1)
                if not last:
                    core_load(r, 1)
                for g in range(2):
                    pe_step("M8", g)
                    act.activation(TMA[:, 2 * g:2 * g + 2, 256:384], two(bank[4 * g + c])[:, :, P:256],
                                   ACT.Identity).then_inc(core_a, 1)
                for g in range(2):
                    pe_step("TT", g)
                    act.activation(TZ[:, 2 * g:2 * g + 2, :], two(bank[4 * g + 2]), ACT.Identity).then_inc(core_a, 1)
                if not last:
                    core_prepared(r, 1, "V", [0])
                for what, to, b in (("Z", TZ[:, :, P:256], n), ("X", XX, 2)):
                    for g in range(2):
                        pe_step(what, g)
                        act.activation(to[:, 2 * g:2 * g + 2, :], two(bank[4 * g + b][:, 0:256]),
                                       ACT.Identity).then_inc(core_a, 1)
                    if what == "Z" and not last:
                        core_prepared(r, 1, "V", [1])
                if not last:
                    core_prepared(r, 1, "T")
                for g in range(2):
                    pe_step("U", g)
                    act.activation(UU[:, 2 * g:2 * g + 2, :], two(bank[4 * g + n][:, 0:256]),
                                   ACT.Identity).then_inc(core_a, 1)
                for g in range(2):
                    pe_step("Y", g)
                    hold()
                    act.activation(seq["r"][:, index(r), 2 * g:2 * g + 2, :], two(bank[4 * g + 2][:, 0:P]),
                                   ACT.Identity).then_inc(core_a, 1)

            act.wait_ge(core_clear, 1)
            core_load(0, 0)
            core_prepared(0, 0, "V")
            core_prepared(0, 0, "T")
            with act.Fori(0, 7) as i:
                core_round((i, 0))
                core_round((i, 1))
            core_round(14)
            core_round(15, last=True)

            act.wait_ge(core_v, NCV * 17)
            act.wait_ge(core_a, NCA * 17)
            act.wait_ge(core_pe, NCPE * 17)
            act.dma_start(xt[:, :, 1:T + 1], dram["x"]).then_inc(xagain_in, 16)
            act.dma_start(mem[:, :, :], dram["mem"]).then_inc(mem_in[0], 16)
            act.dma_start(c_post[:, :, :], dram["c_post"].rearrange("p (k m) -> p k m", k=4)).then_inc(cpost_in, 16)
            for j in range(KT):
                if j % 4 == 3:
                    act.wait_ge(units_used, UNIT0["g2"] + j // 4 + 1 + UC)
                else:
                    act.wait_ge(tile_full, 16 + 3 * (j // 4) + j % 4)
                act.activation(g_all[:, j, :], bank_of(plan("g2", "tile") + j)[:, :],
                               ACT.Identity).then_inc(evacuated, 1)
            g0, v0 = plan("post", "split"), plan("post", "val")

            def post_ln_(k):
                act.wait_ge(var_pe, k + 1)
                act.activation(grs[:, k, :], bank[2 + k % 4][:, :], ACT.Ln, bias=b_gn, scale=1.0 / CH).then_inc(post_ln, 1)

            for k in range(KT):
                half, q = divmod(k, 4)
                act.wait_ge(post_v, k + 1)
                if k >= 2:
                    act.wait_ge(var_pe, k - 1)
                act.activation(sq[:, k % 2, :].rearrange("p (c t) -> p c t", t=CH),
                               seq["r"][:, 8 * half:8 * half + 8, q, :], ACT.Square).then_inc(post_sq, 1)
                if k >= 2:
                    post_ln_(k - 2)
            post_ln_(KT - 2)
            post_ln_(KT - 1)
            for k in range(KT):
                act.wait_ge(post_ln, k + 1)
                act.activation(grs[:, k, :], grs[:, k, :], ACT.Exp, scale=-0.5).then_inc(post_a, 1)
            for k in range(KT):
                act.wait_ge(val_ready, v0 + k + 1)
                act.activation(acth[:, k, :], tmp[:, (g0 + k) % 2, :], ACT.Identity).then_inc(hi_ready, 1)

            def memory_norm(l):
                stage = f"norm_mem{l}"
                square(stage, lambda k: mem[:, k, :], MEM)
                rsqrt(stage, b_eps, MEM)
                high_part(stage, memh, MEM)

            deltas("o", delta0, 1, count=4)
            act.wait_ge(mem_in[0], 16)
            memory_norm(0)
            deltas("o", delta0, 1, skip=4, count=4)


            def evac(stage, to, func=ACT.Identity, n=T, count=None, skip=0, bias=None):
                u0, t0 = UNIT0[stage] + skip, plan(stage, "tile") + skip
                with act.Fori(0, (count or dict(STREAM)[stage]) // 4) as i:
                    for s in range(4):
                        act.wait_ge(units_used, i * 4 + (u0 + s + 1 + UC))
                        hold()
                        act.activation(to(i * 4 + skip + s), bank_of(t0 + s)[:, 0:n], func).then_inc(evacuated, 1)

            def stream_norm(l):
                stage = f"norm_x{l}"
                if l == 0:
                    square(stage, x, ready=x_is_ready("o"))
                    rsqrt(stage, b_eps)
                else:
                    total_rms(stage)
                high_part(stage, acth)

            def values_by_token(l):
                for j in range(4):
                    act.wait_ge(vt_mm, 4 * l + j + 1)
                    act.activation(vtok[:, j // 2, (j % 2) * T:(j % 2 + 1) * T], bank[4 + j],
                                   ACT.Identity).then_inc(vt_ready, 1)

            def memory_side():
                evac("kv0", lambda k: keys[:, k, :], n=MEM, count=4)
                stream_norm(0)
                evac("kv0", lambda k: keys[:, k, :], n=MEM, count=4, skip=4)
                evac("kv0", lambda k: vals[:, k - 8, :], n=MEM, count=8, skip=8)
                values_by_token(0)

            def attention(l):
                def exps(h):
                    act.wait_ge(smax_ready, 4 * l + h + 1)
                    for tt in range(4):
                        ins = act.activation(prob[:, h % 2, tt, :],
                                             bank[4 + tt // 2][:, (tt % 2) * MEM:(tt % 2 + 1) * MEM], ACT.Exp,
                                             bias=snegm[:, h, tt:tt + 1], scale=1.0 / 16,
                                             accum_out=ssum[:, h, tt:tt + 1])
                    ins.then_inc(p_exp, 1)

                evac(f"q{l}", lambda k: query[:, k, :], count=4)
                exps(0)
                evac(f"q{l}", lambda k: query[:, k, :], count=4, skip=4)
                exps(1)
                g0 = plan(f"heads{l}", "split")
                for h in range(4):
                    act.wait_ge(pt_mm, 4 * l + h + 1)
                    act.activation(probt[:, h % 2, 1, :], bank[7], ACT.Identity).then_inc(pt_a, 1)
                    if h < 2:
                        exps(h + 2)
                    for j in range(2 * h, 2 * h + 2):
                        t = plan(f"heads{l}", "tile") + j
                        act.wait_ge(tile_full, plan(f"heads{l}", "full") + j + 1)
                        act.wait_ge(lo_ready, g0 + j + 1)
                        act.activation(tmp[:, (g0 + j) % 2, :], bank_of(t), ACT.Identity).then_inc(evacuated, 1)
                        act.wait_ge(evacuated, t + 1 + UC)
                        act.activation(headh[:, j, :], tmp[:, (g0 + j) % 2, :], ACT.Identity).then_inc(hi_ready, 1)
                deltas_normed(f"xo{l}", delta1, 1, f"norm_ffn{l}")

            def ffn(l):
                total_rms(f"norm_ffn{l}")
                up, c0 = f"up{l}", plan(f"up{l}", "conv")
                g0, v0 = plan(up, "split"), plan(up, "val")
                per = 2 if l < 2 else 1
                with act.Fori(0, FT // 2) as i:
                    for s in range(2):
                        act.wait_ge(conv_ready, i * (2 * per) + (c0 + per * s + 1 + UC))
                        act.activation(sg[:, s, :], cg[:, s, :],
                                       ACT.Silu if l < 2 else ACT.Gelu_apprx_tanh).then_inc(gate_ready, 1)
                    for s in range(2):
                        act.wait_ge(val_ready, i * 2 + (v0 + s + 1))
                        hold()
                        act.activation(hidh[:, i * 2 + s, :], tmp[:, (g0 + s) % 2, :],
                                       ACT.Identity).then_inc(hi_ready, 1)
                if l == 1:
                    deltas_normed("down1", delta2, 3, "norm_h", "final_norm_g")
                else:
                    deltas_normed(f"down{l}", delta2, 3, "last" if l else "norm_conv", split=False)

            def convolution():
                act.wait_ge(x_ready, plan("down0", "x") + KT + SC)
                act.dma_start(mem[:, :, :], dram["mem"]).then_inc(mem_in[1], 16)
                total_rms("norm_conv")
                high_part("norm_conv", acth)

                def gated(first, rounds):
                    u0, t0 = UNIT0["cin"] + 4 * first, plan("cin", "tile")
                    with act.Fori(0, rounds) as i:
                        for s in range(4):
                            k = i * 2 + (2 * first + s // 2)
                            act.wait_ge(units_used, i * 4 + (u0 + s + 1 + UC))
                            hold()
                            if s % 2:
                                ins = act.activation(glu[:, k, :], bank_of(t0 + s), ACT.Sigmoid,
                                                     bias=pc("conv_b_in", k + KT))
                            else:
                                ins = act.activation(gp[:, k, CONVW - 1:], bank_of(t0 + s), ACT.Identity,
                                                     bias=pc("conv_b_in", k))
                            ins.then_inc(evacuated, 1)

                gated(0, 1)
                act.wait_ge(mem_in[1], 16)
                square("norm_mem1", lambda k: mem[:, k, :], MEM)
                rsqrt("norm_mem1", b_eps, MEM)

                def diagonals(k0, first=0):
                    for s in range(2):
                        for j in range(PETAPS):
                            ins = act.activation(diag[s][:, j, :], ident, ACT.Identity,
                                                 scale=pc("conv_dw", (k0 + s) * CONVW + first + j))
                        ins.then_inc(diag_ready, 1)

                def taps(k0, batches=1):
                    for s in range(2):
                        act.wait_ge(tap_mm, k0 + s - 1 + 2 * (batches - 1))
                        act.activation(ub[:, k0 + s, :], bank[6 + s], ACT.Identity,
                                       bias=pc("conv_dw_b", k0 + s)).then_inc(tap_ready, 1)

                diagonals(2)
                gated(1, 2)
                taps(2)
                high_part("norm_mem1", memh, MEM)
                diagonals(4)
                gated(3, 1)
                taps(4)
                diagonals(6)
                evac("kv1", lambda k: keys[:, k, :], n=MEM, count=8)
                act.wait_ge(tap_mm, 6)
                diagonals(6, PETAPS)
                taps(6, 2)
                evac("kv1", lambda k: vals[:, k - 8, :], n=MEM, count=4, skip=8)
                square("ln", lambda k: ub[:, k, :], ready=lambda k: act.wait_ge(uc_ready, k + 1))
                rsqrt("ln", b_ln)
                g0 = plan("ln", "split")
                with act.Fori(0, KT // 2) as i:
                    for s in range(2):
                        act.wait_ge(lo_ready, i * 2 + (g0 + s + 1))
                        act.wait_ge(uc_ready, i * 2 + (KT + s + 1))
                        hold()
                        chain.enter(i, 2) if s == 0 else None
                        chain.step(act.activation(tmp[:, (g0 + s) % 2, :], ub[:, i * 2 + s, :], ACT.Silu,
                                                  bias=pc("conv_ln_b", i * 2 + s)))
                    for s in range(2):
                        chain.wait(1 - s)
                        hold()
                        act.activation(acth[:, i * 2 + s, :], tmp[:, (g0 + s) % 2, :],
                                       ACT.Identity).then_inc(hi_ready, 1)
                    chain.leave(KT // 2, 2)
                deltas_normed("cout", delta3, 1, "norm_x1", split=False, bias=lambda k: pc("conv_b_out", k))
                evac("kv1b", lambda k: vals[:, k + 4, :], n=MEM)
                stream_norm(1)
                values_by_token(1)

            def hybrid():
                act.wait_ge(x_ready, plan("down1", "x") + KT + SC)
                act.dma_start(hyb[:, :], dram["c_hybrid"]).then_inc(hyb_in, 16)
                act.dma_start(w2g[:, :], dram["w2g"]).then_inc(hyb_in, 16)
                act.wait_ge(sum_mm, plan("norm_h", "total") + 1)
                chain.step(act.activation(acc_x[:, :], bank[4], ACT.Ln, bias=b_eps, scale=1.0 / D))
                chain.step(act.activation(rstd[:, :], bank[5], ACT.Ln, bias=b_eps2, scale=1.0 / D))
                chain.wait(1)
                act.activation(acc_x[:, :], acc_x[:, :], ACT.Exp, scale=-0.5)
                chain.wait()
                act.activation(rstd[:, :], rstd[:, :], ACT.Exp, scale=-0.5).then_inc(rstd_ready, 1)
                t0 = plan("in2", "tile")

                for j in range(8):
                    act.wait_ge(vt2_mm, j + 1)
                    act.activation((gvt if j < 4 else fvt)[:, j % 4, :], bank[4 + j % 4],
                                   ACT.Identity).then_inc(vt2_ready, 1)
                act.wait_ge(evacuated, t0 + 17 + UC)
                act.activation(gr[:, :, :], gr[:, :, :], ACT.Silu)
                act.wait_ge(vt2_ready, 8)
                act.activation(ls[:, 2, :], small[:, :], ACT.Identity, bias=pc("fox_fb"))
                for p in range(2):
                    act.wait_ge(z_mm, p + 1)
                    act.activation(ls[:, p, :], bank[4 + p], ACT.Identity, bias=pc("gla_b", p)).then_inc(z_ready, 1)
                act.wait_ge(z_ready, 2)
                chain.step(act.activation(le[:, :, :], ls[:, :, :], ACT.Abs))
                chain.wait()
                chain.step(act.activation(le[:, :, :], le[:, :, :], ACT.Exp, scale=-1.0))
                chain.wait()
                act.activation(le[:, :, :], le[:, :, :], ACT.Ln, bias=ones[:, 0:1]).then_inc(log_ready, 1)
                act.wait_ge(cum_ready, 1)
                act.activation(eb[:, :, :], ls[:, 0:2, :], ACT.Exp, scale=1.0 / 16)
                act.activation(enb[:, :, :], ls[:, 0:2, :], ACT.Exp, scale=-1.0 / 16).then_inc(eb_ready, 1)

                def gate(n):
                    act.wait_ge(evacuated, t0 + 25 + n + 1 + UC)
                    g_ = (gate_b if n // KT else gate_a)[:, n % KT, :]
                    act.activation(g_, g_, ACT.Sigmoid, bias=pc("gate_b_2", n)).then_inc(gated, 1)

                def fox_square(j):
                    act.wait_ge(sq_used, plan("fox_norm", "sq") + j + 1)
                    act.activation(sq[:, j % 2, :], (fq if j < 4 else fk)[:, j % 4, :],
                                   ACT.Square).then_inc(sq_ready, 1)

                def fox_rms(j):
                    for s in range(2):
                        act.wait_ge(sq_used, plan("fox_norm", "sq") + j + s + 1 + SC)
                        if j:
                            act.wait_ge(fox_scaled, j + s - 1)
                        chain.step(act.activation(frs[:, s, :], bank[6 + s], ACT.Ln, bias=b_eps, scale=1.0 / 64))
                    for s in range(2):
                        chain.wait(1 - s)
                        act.activation(frs[:, s, :], frs[:, s, :], ACT.Exp, bias=b_q if j < 4 else 0.0,
                                       scale=-0.5).then_inc(frs_ready, 1)

                def gla_square(h):
                    act.wait_ge(sq_used, plan("gla", "sq") + h + 1)
                    act.wait_ge(go_mm, h + 1)
                    act.activation(sq[:, h % 2, :], bank[6 + h % 2], ACT.Square).then_inc(sq_ready, 1)

                def gla_rms(h):
                    act.wait_ge(sq_used, plan("gla", "sq") + h + 1 + SC)
                    if h >= 2:
                        act.wait_ge(gla_done, h - 1)
                    chain.step(act.activation(frs[:, h % 2, :], bank[4 + h % 2], ACT.Ln, bias=b_eps, scale=1.0 / P))
                    chain.wait()
                    act.activation(frs[:, h % 2, :], frs[:, h % 2, :], ACT.Exp, scale=-0.5).then_inc(gla_scale, 1)

                gate(0)
                gate(1)
                for b in range(2):
                    act.wait_ge(ket_mm, b + 1)
                    act.activation(ket[:, 2 * b:2 * b + 2, :], bank[6 + b].rearrange("p (a m) -> p a m", a=2),
                                   ACT.Identity).then_inc(ket_ready, 1)
                gate(2)
                act.wait_ge(evacuated, t0 + 25 + UC)
                fox_square(0)
                fox_square(1)
                gate(3)
                act.wait_ge(qk_ready, 1)
                for j in range(0, 8, 2):
                    gate(4 + j // 2)
                    fox_rms(j)
                    if j < 6:
                        for s in range(2, 4):
                            fox_square(j + s)
                gate(8)
                act.wait_ge(fox_scaled, 8)
                gate(9)
                for h in range(4):
                    gla_square(h)
                    gate(10 + h)
                    gla_rms(h)
                gate(14)

                def fox_exps(h):
                    act.wait_ge(fmax_ready, h + 1)
                    if h >= 2:
                        act.wait_ge(fpt_mm, h - 1)
                    for qt in range(4):
                        b, o = ((4, 0), (4, P), (5, 0), (6, 0))[qt]
                        n = (qt + 1) * P
                        ins = act.activation(fp[:, h % 2, FOX_OFF[qt]:FOX_OFF[qt] + n], bank[b][:, o:o + n], ACT.Exp,
                                             bias=fneg[:, h, qt:qt + 1], accum_out=fsum[:, h, qt:qt + 1])
                    ins.then_inc(f_exp, 1)

                fox_exps(0)
                gate(15)
                act.wait_ge(units_used, UNIT0["in2"] + 41 + UC)
                for h in range(4):
                    act.activation(acth[:, h, :], gr[:, h, :], ACT.Identity).then_inc(hi_ready, 1)
                fox_exps(1)
                g0 = plan("fox", "split")
                for h in range(8):
                    act.wait_ge(fpt_mm, h + 1)
                    act.activation(fpt[:, h % 2, 4 * P:7 * P], bank[1][:, 0:3 * P], ACT.Identity)
                    act.activation(fpt[:, h % 2, 7 * P:10 * P], bank[2][:, 0:3 * P], ACT.Identity).then_inc(fpt_a, 1)
                    if h < 6:
                        fox_exps(h + 2)
                    r, p = slice(64 * (h % 2), 64 * (h % 2) + 64), h // 2
                    act.wait_ge(fo_mm, h + 1)
                    act.wait_ge(lo_ready, g0 + p + 1)
                    act.activation(tmp[r, (g0 + p) % 2, :], bank[3 + 4 * (h % 2)][r, :],
                                   ACT.Identity).then_inc(fo_a, 1)
                    if h % 2:
                        act.wait_ge(fo_a, h + 1)
                        act.activation(acth[:, 4 + p, :], tmp[:, (g0 + p) % 2, :], ACT.Identity).then_inc(hi_ready, 1)
                high_part("branch", yh)
                deltas_normed("out2", delta4, 1, "norm_ffn2")

            def last_norm():
                total_rms("last")
                for k in range(0, KT, 2):
                    act.wait_ge(x_ready, plan("last", "x") + k + 2 + SC)
                    act.dma_start(dram["out"][:, k:k + 2, :], xt[:, k:k + 2, 1:T + 1]).then_inc(out_in, 16)
                act.wait_ge(out_in, 16 * (KT // 2))

            memory_side()
            attention(0)
            ffn(0)
            convolution()
            attention(1)
            ffn(1)
            hybrid()
            ffn(2)
            last_norm()

        @block.vector
        def _(dve):
            dve.sem_inc(x_ready, SC)
            dve.sem_inc(lo_ready, SC)
            dve.sem_inc(prep_done, 1)
            dve.sem_inc(conv_ready, UC)
            chain = Chain(dve, dve_chain)
            mul, add, sub = ALU.mult, ALU.add, ALU.subtract

            def bank_of(t):
                return bank[t % 4]

            def lows(stage, h, l, i, n=T):
                g = plan(stage, "split")
                for s in range(2):
                    dve.wait_ge(hi_ready, i * 2 + (g + s + 1))
                    dve.tensor_tensor(l[:, i * 2 + s, 0:n], tmp[:, (g + s) % 2, 0:n],
                                      h[:, i * 2 + s, 0:n].bitcast(F32), sub).then_inc(lo_ready, 1)

            def normed(stage, source, gain, h=None, l=None, n=T):
                dve.wait_ge(rstd_ready, plan(stage, "rstd") + 1)
                with dve.Fori(0, KT // 2) as i:
                    for s in range(2):
                        dve.wait_ge(lo_ready, i * 2 + (plan(stage, "split") + s + 1))
                        dve.scalar_tensor_tensor(
                            out=tmp[:, (plan(stage, "split") + s) % 2, 0:n], in0=source(i * 2 + s),
                            scalar=gain(i * 2 + s), in1=rstd[:, 0:n], op0=mul, op1=mul).then_inc(val_ready, 1)
                    lows(stage, h or acth, l or actl, i, n)

            def residual(stage, buf, skip=0, count=KT):
                t0 = plan(stage, "tile") + skip
                with dve.Fori(0, count // 2) as i:
                    for s in range(2):
                        xk = xt[:, i * 2 + (skip + s), 1:T + 1]
                        dve.wait_ge(evacuated, i * 2 + (t0 + s + 1 + UC))
                        dve.tensor_tensor(xk, xk, buf[:, s, :], add).then_inc(x_ready, 1)

            def residual_normed(stage, buf, norm, gain, acc, col=0):
                t0, x0, sq0 = plan(stage, "tile"), plan(stage, "x"), plan(norm, "sq")
                g0, n = plan(norm, "split") if gain else 0, len(acc)
                for b in acc:
                    chain.step(dve.memset(b[:, :], 0.0))
                chain.wait()
                with dve.Fori(0, KT // 2) as i:
                    for s in range(2):
                        k = i * 2 + s
                        xk, t_ = xt[:, k, 1:T + 1], tmp[:, (g0 + s) % 2, :]
                        dve.wait_ge(evacuated, i * 2 + (t0 + s + 1 + UC))
                        dve.tensor_tensor(xk, xk, buf[:, s, :], add).then_inc(x_ready, 1)
                        dve.wait_ge(x_ready, i * 2 + (x0 + s + 1 + SC))
                        if gain:
                            dve.wait_ge(lo_ready, i * 2 + (g0 + s + 1))
                            dve.tensor_scalar(t_, xk, pc(gain[0], k + col), pc(gain[1], k) if n == 2 else None,
                                              mul, mul if n == 2 else ALU.bypass).then_inc(val_ready, 1)
                        for j, b in enumerate(acc):
                            dve.wait_ge(sq_ready, i * (2 * n) + (sq0 + n * s + j + 1))
                            dve.wait_ge(sq_used, i * (2 * n) + (sq0 + n * (s - 1) + j + 1 + SC))
                            dve.tensor_tensor(b[:, :], b[:, :], sq[:, (n * s + j) % 2, :], add).then_inc(sq_used, 1)
                        if gain:
                            dve.wait_ge(hi_ready, i * 2 + (g0 + s + 1))
                            dve.tensor_tensor(actl[:, k, :], t_, acth[:, k, :].bitcast(F32), sub).then_inc(lo_ready, 1)

            dve.memset(xt[:, :, 0:1], 0.0)
            for j, v in enumerate((EPS, LN_EPS, GN_EPS, 10 * LN2, -3 * LN2, EPS ** 2)):
                dve.memset(eps[:, j:j + 1], v)
            dve.memset(plast[:, 7:16:8, :], 0.0)
            dve.wait_ge(par_in, 16)
            dve.tensor_scalar(omu[:, 0:6 * KT], par[:, PCOL["mu"]:PCOL["mu"] + 6 * KT], -1.0, 1.0, mul, add)
            dve.tensor_scalar(omu[:, 6 * KT:7 * KT], par[:, PCOL["k_a"]:PCOL["k_a"] + KT], -1.0, 1.0,
                              mul, add).then_inc(omu_ready, 1)
            chain.step(dve.memset(rstd[:, :], 0.0))
            chain.wait()
            for k in range(KT):
                dve.wait_ge(sq_ready, plan("norm0", "sq") + k + 1)
                dve.wait_ge(sq_used, plan("norm0", "sq") + k + SC)
                dve.tensor_tensor(rstd[:, :], rstd[:, :], sq[:, k % 2, :], add).then_inc(sq_used, 1)
            dve.wait_ge(rstd_ready, 1)
            with dve.Fori(0, KT) as k:
                xk = xt[:, k, 1:T + 1]
                dve.scalar_tensor_tensor(out=xk, in0=xk, scalar=pc("norm_mix_g", k), in1=rstd[:, :],
                                         op0=mul, op1=mul).then_inc(h_ready, 1)
            dve.wait_ge(h_ready, KT)
            after = {"mixg": "lora_in", "mixk": "lora_in", "mixr": "gate_in", "mixv": "k"}

            def mix(m, name):
                stage = "mix" + name
                j = MU[name]
                if stage in after:
                    st = after[stage]
                    dve.wait_ge(units_used, UNIT0[st] + dict(STREAM)[st] + UC)
                if name in "wagk":
                    with dve.Fori(0, KT // 2) as i:
                        for s in range(2):
                            k = i * 2 + s
                            dve.wait_ge(lo_ready, i * 2 + (plan(stage, "split") + s + 1))
                            dve.wait_ge(part_ready, i * 2 + ("wagk".index(name) * KT + s + 1))
                            dve.scalar_tensor_tensor(out=tmp[:, (plan(stage, "split") + s) % 2, :], in0=xt[:, k, 0:T],
                                                     scalar=pc("mu", k + j * KT), in1=parts[:, k, :], op0=mul,
                                                     op1=add).then_inc(val_ready, 1)
                        lows(stage, mixh[m], mixl[m], i)
                    return
                with dve.Fori(0, KT // 2) as i:
                    chain.enter(i, 2)
                    for s in range(2):
                        k = i * 2 + s
                        dve.wait_ge(lo_ready, i * 2 + (plan(stage, "split") + s + 1))
                        chain.step(dve.tensor_scalar(tmp[:, (plan(stage, "split") + s) % 2, :],
                                                     xt[:, k, 1:T + 1],
                                                     omu[:, bass.ds(k + j * KT, 1)], None, mul))
                    for s in range(2):
                        k = i * 2 + s
                        t_ = tmp[:, (plan(stage, "split") + s) % 2, :]
                        chain.wait(1 - s)
                        dve.scalar_tensor_tensor(out=t_, in0=xt[:, k, 0:T], scalar=pc("mu", k + j * KT),
                                                 in1=t_, op0=mul, op1=add).then_inc(val_ready, 1)
                    lows(stage, mixh[m], mixl[m], i)
                    chain.leave(KT // 2, 2)

            mix(0, "w")
            mix(1, "a")
            mix(0, "g")
            g = plan("mid", "split")
            dve.wait_ge(hi_ready, g + 1)
            dve.tensor_tensor(midl[:, :], tmp[:, g % 2, :], midh[:, :].bitcast(F32), sub).then_inc(lo_ready, 1)
            mix(1, "k")
            g = plan("gmid", "split")
            for j in range(2):
                dve.wait_ge(hi_ready, g + j + 1)
                dve.tensor_tensor(gmidl[:, j, :], gbuf[:, j, :], gmidh[:, j, :].bitcast(F32),
                                  sub).then_inc(lo_ready, 1)
            mix(0, "r")
            mix(1, "v")
            def seq_tile(name, half, q):
                return seq[name][:, 8 * half:8 * half + 8, q, :]

            def chunks(ap):
                return ap.rearrange("p (c t) -> p c t", t=CH)

            def cumulate(k):
                half, q = divmod(k, 4)
                c_, W_ = cs[:, k % 4, :], seq_tile("w", half, q)
                for c in range(NCH):
                    ins = dve.tensor_tensor_scan(c_[:, c * CH:(c + 1) * CH], ones[:, 0:CH],
                                                 seq["w"][:, 8 * half + c, q, :], 0.0, mul, add)
                chain.step(ins)
                chain.wait()
                chain.step(dve.tensor_tensor(W_, chunks(c_), W_, sub))

            def scans(p):
                if p >= 2:
                    dve.wait_ge(prep_done, p)
                for k in (2 * p, 2 * p + 1):
                    s, (half, q) = k % 2, divmod(k, 4)
                    W_, A_, K_, R_ = (seq_tile(n, half, q) for n in "wakr")
                    k_ = kk[:, k % 4, :]
                    dve.wait_ge(bsel_mm, k + 1)
                    dve.scalar_tensor_tensor(out=chunks(k_), in0=K_, scalar=pc("k_k", k), in1=chunks(bank[4 + s]),
                                             op0=mul, op1=mul).then_inc(kk_ready, 1)
                    chain.step(dve.tensor_scalar(chunks(pt[:, s, :]), A_, pc("k_a", k),
                                                 omu[:, k + 6 * KT:k + 6 * KT + 1], mul, add))
                    chain.wait()
                    dve.wait_ge(kk_ready, k + 1)
                    chain.step(dve.tensor_tensor(K_, K_, chunks(pt[:, s, :]), mul))
                    if p >= 2:
                        cumulate(k)
                    dve.wait_ge(bonus_mm, k + 1)
                    chain.wait()
                    chain.step(dve.scalar_tensor_tensor(out=chunks(sq[:, s, :]), in0=R_, scalar=pc("r_k", k),
                                                        in1=K_, op0=mul, op1=mul))
                    dve.tensor_tensor(A_, chunks(k_), A_, mul).then_inc(scan_ready, 1)

            def decays(p):
                for k in (2 * p, 2 * p + 1):
                    s, (half, q) = k % 2, divmod(k, 4)
                    W_, A_, K_, R_ = (seq_tile(n, half, q) for n in "wakr")
                    dve.wait_ge(decay_ready, k + 1)
                    chain.wait()
                    dve.tensor_tensor(R_, R_, chunks(pp[:, s, :]), mul)
                    dve.tensor_tensor(K_, K_, chunks(pi[:, s, :]), mul)
                    dve.tensor_tensor(A_, A_, chunks(pi[:, s, :]), mul)
                    dve.scalar_tensor_tensor(out=W_, in0=chunks(kk[:, k % 4, :]), scalar=-1.0, in1=W_,
                                             op0=mul, op1=mul)
                    ins = dve.tensor_scalar(plast[:, 8 * half:8 * half + 7, q],
                                            chunks(pp[:, s, :])[:, 0:7, CH - 1], 1.0, None, mul)
                ins.then_inc(prep_done, 1)

            dve.wait_ge(evacuated, plan("w2", "tile") + 8 + UC)
            for k in range(4):
                cumulate(k)
            dve.wait_ge(sq_used, plan("knorm", "sq") + KT + SC)
            dve.tensor_scalar(bonus[0:8, :, :], psum[0:8, 4:6, :], 2.0 ** 20, 1e-24 * 2.0 ** 20, mul,
                              ALU.max).then_inc(kss_ready, 1)
            dve.wait_ge(evacuated, plan("r", "tile") + 8 + UC)
            scans(0)
            for p in range(4):
                if p < 3:
                    scans(p + 1)
                decays(p)
            dve.wait_ge(bonus_mm, KT + SC)
            dve.tensor_copy(bonus[0:8, :, :], psum[0:8, 6:8, :])
            dve.wait_ge(evacuated, plan("v", "tile") + 8 + UC)
            dve.wait_ge(prep_done, 4 + 1)
            for b in (AR[0], AR[1], BB, KB, VB):
                dve.memset(b[:, :, :], 0.0)
            dve.memset(SS[:, :, :], 0.0).then_inc(core_clear, 1)
            dve.wait_ge(core_clear, 1)
            dve.wait_ge(ccore_in, 16)
            dve.sem_inc(core_v, NCV)

            def two(ap):
                return ap.rearrange("p (q t) -> p q t", q=2)

            def mask(m, n):
                return m.rearrange("p (o t) -> p o t", o=1).to_broadcast([P, 2, n])

            def core_load(r, ahead):
                dve.wait_ge(core_pe, count(r, NCPE, NCPE))
                if ahead:
                    dve.wait_ge(pro_pe, count(r, NPPE, NPPE))
                it, c = index(r, ahead), (parity(r) + ahead) % 2
                for h in range(2):
                    p = slice(64 * h, 64 * h + 64)
                    dve.tensor_scalar(AR[c][p, :, p], seq["w"][p, it, :, :], 1.0, None, mul)
                    ins = dve.tensor_scalar(KB[p, :, p], seq["k"][p, it, :, :], 1.0, None, mul)
                ins.then_inc(pro_v, 1)

            def core_prepared(r, ahead, what, groups=(0, 1)):
                c = (parity(r) + ahead) % 2
                for g in groups:
                    b, q = bank[4 * g + 3], slice(2 * g, 2 * g + 2)
                    dve.wait_ge(pro_pe, count(r, NPPE, ahead * NPPE + PPE[what] + g))
                    if what == "AC":
                        ac = two(b[:, 0:384])
                        chain.step(dve.tensor_tensor(ND[c][:, q, :], ac[:, :, 0:P], mask(m_n16, P), mul))
                        dve.tensor_tensor(CC[c][:, q, :], ac[:, :, P:192], mask(m_ac[:, P:192], CH), mul)
                        chain.wait()
                        dve.tensor_tensor(T1[c][:, q, :], ND[c][:, q, :], mask(ident, P), add).then_inc(pro_v, 1)
                    elif what == "N":
                        for to, m in ((AD, m_a16), (AO32, m_a32), (AO64, m_a64)):
                            ins = dve.tensor_tensor(to[c][:, q, :], two(b[:, 0:256]), mask(m, P), mul)
                        ins.then_inc(pro_v, 1)
                    else:
                        dve.tensor_tensor(BE[c][:, q, :], two(b[:, 0:384]), mask(m_ac, 192), mul).then_inc(pro_v, 1)

            def core_round(r, last=False):
                c, n = parity(r), 1 - parity(r)

                def pe_step(what, g):
                    dve.wait_ge(core_pe, count(r, NCPE, NCPE + CPE[what] + g))

                def act_done(what, g):
                    dve.wait_ge(core_a, count(r, NCA, NCA + CA[what] + g))

                def tt(g):
                    return TMA[:, 2 * g:2 * g + 2, 0:P]

                if not last:
                    core_load(r, 1)
                for g in range(2):
                    pe_step("M4", g)
                    act_done("M4", g)
                    dve.tensor_tensor(tt(g), two(bank[4 * g + n])[:, :, 0:P], T1[c][:, 2 * g:2 * g + 2, :],
                                      add).then_inc(core_v, 1)
                for g in range(2):
                    pe_step("M8", g)
                    act_done("M8", g)
                    dve.tensor_tensor(tt(g), two(bank[4 * g + c])[:, :, 0:P], tt(g), add).then_inc(core_v, 1)
                def more(what, *groups):
                    if not last:
                        core_prepared(r, 1, what, groups)

                more("AC", 0)
                for g in range(2):
                    pe_step("T4", g)
                    dve.tensor_tensor(tt(g), two(bank[4 * g + n][:, 0:256]), tt(g), add).then_inc(core_v, 1)
                more("AC", 1)
                more("N", 0)
                for g in range(2):
                    pe_step("TZ", g)
                    z = two(bank[4 * g + c])
                    dve.tensor_tensor(tt(g), z[:, :, 0:P], tt(g), add)
                    t_ = TZ[:, 2 * g:2 * g + 2, 0:P]
                    dve.tensor_tensor(t_, z[:, :, P:256], t_, add).then_inc(core_v, 1)
                more("N", 1)
                more("BE", 0)
                more("BE", 1)
                for g in range(2):
                    pe_step("T64", g)
                    dve.tensor_tensor(tt(g), two(bank[4 * g + c][:, 0:256]), tt(g), add).then_inc(core_v, 1)
                for g in range(2):
                    pe_step("Y", g)
                    s_ = SS[:, 2 * g:2 * g + 2, :]
                    chain.step(dve.tensor_tensor(s_, two(bank[4 * g + c][:, 0:256]), s_, add))
                    chain.wait()
                    for p in (2 * g, 2 * g + 1):
                        ins = dve.tensor_scalar(SS[:, p, :], SS[:, p, :], plast[:, index(r), p:p + 1], None, mul)
                    ins.then_inc(core_v, 1)

            core_load(0, 0)
            for what in ("AC", "N", "BE"):
                core_prepared(0, 0, what)
            with dve.Fori(0, 7) as i:
                chain.enter(i, 8)
                core_round((i, 0))
                core_round((i, 1))
                chain.leave(7, 8)
            core_round(14)
            core_round(15, last=True)

            for k in range(KT):
                y_, v_ = (seq_tile(n, k // 4, k % 4) for n in "rv")
                dve.wait_ge(mean_pe, k + 1)
                dve.scalar_tensor_tensor(out=y_, in0=chunks(bank[k % 2]), scalar=-1.0 / CH, in1=y_, op0=mul, op1=add)
                dve.tensor_tensor(v_, chunks(bank[6 + k % 2]), v_, mul).then_inc(post_v, 1)
            dve.wait_ge(evacuated, plan("g2", "tile") + 8 + UC)
            dve.wait_ge(post_v, KT)
            for k in range(0, KT, 2):
                y_, v_ = ([seq_tile(n, k // 4, (k + s) % 4) for s in range(2)] for n in "rv")
                for s in range(2):
                    dve.wait_ge(post_a, k + s + 1)
                    chain.step(dve.scalar_tensor_tensor(out=y_[s], in0=y_[s], scalar=pc("ln_g", k + s),
                                                        in1=chunks(grs[:, k + s, :]), op0=mul, op1=mul))
                for s in range(2):
                    chain.wait(1)
                    chain.step(dve.scalar_tensor_tensor(out=y_[s], in0=y_[s], scalar=pc("ln_b", k + s),
                                                        in1=v_[s], op0=add, op1=add))
                for s in range(2):
                    chain.wait(1 - s)
                    dve.wait_ge(lo_ready, plan("post", "split") + k + s + 1)
                    dve.tensor_tensor(chunks(tmp[:, (plan("post", "split") + s) % 2, :]), y_[s],
                                      chunks(g_all[:, k + s, :]), mul).then_inc(val_ready, 1)
                lows("post", acth, actl, k // 2)
            dve.wait_ge(xagain_in, 16)
            def memory_norm(l):
                dve.wait_ge(mem_in[l], 16)
                normed(f"norm_mem{l}", lambda k: mem[:, k, :], lambda k: pc("mem_norm_g", k), memh, meml, MEM)

            residual("o", delta0, count=4)
            memory_norm(0)
            residual("o", delta0, skip=4, count=4)

            def attention(l):
                normed(f"norm_x{l}", x, lambda k: pc("norm_xattn_g", k + l * KT))

                def soft_max(h):
                    dve.wait_ge(sc_mm, 4 * l + h + 1)
                    chain.step(dve.tensor_reduce(smax[:, h, :], psum[:, 4:6, :].rearrange(
                        "p b (a m) -> p (b a) m", m=MEM), AX.X, ALU.max))
                    chain.wait()
                    dve.tensor_scalar(snegm[:, h, :], smax[:, h, :], -1.0 / 16, None, mul).then_inc(smax_ready, 1)

                def head_lows(h):
                    for j in range(2 * h, 2 * h + 2):
                        dve.wait_ge(hi_ready, g0 + j + 1)
                        dve.tensor_tensor(headl[:, j, :], tmp[:, (g0 + j) % 2, :], headh[:, j, :].bitcast(F32),
                                          sub).then_inc(lo_ready, 1)

                soft_max(0)
                soft_max(1)
                g0 = plan(f"heads{l}", "split")
                for h in range(4):
                    n = 4 * l + h
                    dve.wait_ge(p_exp, n + 1)
                    chain.step(dve.reciprocal(srec[:, h, :], ssum[:, h, :]))
                    chain.wait()
                    dve.tensor_tensor(prob[:, h % 2, :, :], prob[:, h % 2, :, :],
                                      srec[:, h, :].rearrange("p (a o) -> p a o", o=1).to_broadcast([P, 4, MEM]),
                                      mul).then_inc(p_ready, 1)
                    dve.wait_ge(pt_mm, n + 1)
                    dve.tensor_copy(probt[:, h % 2, 0, :], bank[6]).then_inc(pt_v, 1)
                    if h:
                        head_lows(h - 1)
                    if h < 2:
                        soft_max(h + 2)
                head_lows(3)
                residual_normed(f"xo{l}", delta1, f"norm_ffn{l}", ["norm_ffn_g"], [rstd], l * KT)

            def ffn(l):
                dve.memset(cu[:, :, 0:2], 0.0).then_inc(pad_ready, 1)
                dve.wait_ge(pad_ready, l + 1)
                t0, u0, c0 = plan(f"up{l}", "tile"), UNIT0[f"up{l}"], plan(f"up{l}", "conv")
                g0, v0 = plan(f"up{l}", "split"), plan(f"up{l}", "val")
                dve.wait_ge(rstd_ready, plan(f"norm_ffn{l}", "rstd") + 1)

                def scaled(i, s):
                    dve.wait_ge(units_used, i * 4 + (u0 + s + 1 + UC))
                    if l < 2 or s % 2 == 0:
                        dve.wait_ge(conv_ready, i * 4 + (c0 + s + 1) if l < 2 else i * 2 + (c0 + s // 2 + 1 + UC - 2))
                    else:
                        dve.wait_ge(val_ready, i * 2 + (v0 - 1 + s // 2))
                    dve.tensor_tensor(cu[:, s, 2:T + 2], bank_of(t0 + s), rstd[:, :], mul).then_inc(evacuated, 1)

                if l == 2:
                    ffn2(scaled)
                    return
                with dve.Fori(0, FT // 2) as i:
                    chain.enter(i, 8)
                    for s in range(4):
                        col = (i * 2 + s // 2) * 3 + ((s % 2) * FT * 3 + l * 2 * FT * 3)
                        to = (cv if s % 2 else cg)[:, s // 2, :]
                        scaled(i, s)
                        dve.wait_ge(evacuated, i * 4 + (t0 + s + 1 + UC))
                        chain.step(dve.tensor_scalar(to, cu[:, s, 2:T + 2], pc("ffn_dw", col + 2), None, mul))
                    for s in range(4):
                        col = (i * 2 + s // 2) * 3 + ((s % 2) * FT * 3 + l * 2 * FT * 3)
                        to = (cv if s % 2 else cg)[:, s // 2, :]
                        chain.wait(3)
                        chain.step(dve.scalar_tensor_tensor(out=to, in0=cu[:, s, 1:T + 1], scalar=pc("ffn_dw", col + 1),
                                                            in1=to, op0=mul, op1=add))
                    for s in range(4):
                        col = (i * 2 + s // 2) * 3 + ((s % 2) * FT * 3 + l * 2 * FT * 3)
                        to = (cv if s % 2 else cg)[:, s // 2, :]
                        chain.wait(3 - s)
                        dve.scalar_tensor_tensor(out=to, in0=cu[:, s, 0:T], scalar=pc("ffn_dw", col),
                                                 in1=to, op0=mul, op1=add).then_inc(conv_ready, 1)
                    for s in range(2):
                        dve.wait_ge(gate_ready, i * 2 + (c0 // 2 + s + 1))
                        dve.wait_ge(conv_ready, i * 4 + (c0 + 2 * s + 2 + UC))
                        dve.wait_ge(lo_ready, i * 2 + (g0 + s + 1))
                        dve.tensor_tensor(tmp[:, (g0 + s) % 2, :], sg[:, s, :], cv[:, s, :], mul).then_inc(val_ready, 1)
                    lows(f"up{l}", hidh, hidl, i)
                    chain.leave(FT // 2, 8)
                if l == 1:
                    residual_normed("down1", delta2, "norm_h", ["final_norm_g", "norm_mix_g_2"], [acc_x, acc_y])
                    dve.wait_ge(sq_used, plan("norm_h", "sq") + 2 * KT + SC)
                    dve.scalar_tensor_tensor(out=acc_y[:, :], in0=acc_x[:, :], scalar=EPS, in1=acc_y[:, :],
                                             op0=mul, op1=add).then_inc(acc_ready, 1)
                else:
                    residual_normed("down0", delta2, "norm_conv", None, [rstd])

            def convolution():
                normed("norm_conv", x, lambda k: pc("norm_mix_g", k + KT))
                chain.step(dve.memset(gp[:, :, 0:CONVW - 1], 0.0))
                chain.wait()
                t0 = plan("cin", "tile")

                def gate(k0, i=None):
                    for s in range(2):
                        at_ = (k0 + s) if i is None else i * 2 + (k0 + s)
                        t = 2 * (k0 + s) + 2
                        dve.wait_ge(evacuated, t0 + t + UC if i is None else i * 4 + (t0 + t + UC))
                        u_ = gp[:, at_, CONVW - 1:]
                        dve.tensor_tensor(u_, u_, glu[:, at_, :], mul).then_inc(glu_ready, 1)

                def convolve(k0, first, last, i=None):
                    for j in range(last, first - 1, -1):
                        for s in range(2):
                            k = (k0 + s) if i is None else i * 2 + (k0 + s)
                            if j < last or i is None:
                                chain.wait(1 if j > first or s == 0 else 0)
                            ins = dve.scalar_tensor_tensor(out=ub[:, k, :], in0=gp[:, k, j:j + T],
                                                           scalar=pc("conv_dw", k * CONVW + j), in1=ub[:, k, :],
                                                           op0=mul, op1=add)
                            if j > first:
                                chain.step(ins)
                            else:
                                ins.then_inc(u_ready, 1)

                gate(0)
                for s in range(2):
                    dve.wait_ge(glu_ready, s + 1)
                    chain.step(dve.tensor_scalar(ub[:, s, :], gp[:, s, CONVW - 1:], pc("conv_dw", s * CONVW + CONVW - 1),
                                                 pc("conv_dw_b", s), mul, add))
                convolve(0, 0, CONVW - 2)
                gate(2)
                memory_norm(1)
                stride = 2 * (CONVW - 1 - PETAPS)
                with dve.Fori(0, 2) as i:
                    chain.enter(i, stride)
                    gate(4, i)
                    dve.wait_ge(glu_ready, i * 2 + 4)
                    dve.wait_ge(tap_ready, i * 2 + 2)
                    convolve(2, PETAPS, CONVW - 1, i)
                    chain.leave(2, stride)
                dve.wait_ge(tap_ready, 6)
                convolve(6, 2 * PETAPS, CONVW - 1)
                dve.wait_ge(mean_mm, 1)
                with dve.Fori(0, KT) as k:
                    dve.wait_ge(u_ready, KT)
                    dve.scalar_tensor_tensor(out=ub[:, k, :], in0=bank[5], scalar=-1.0 / D, in1=ub[:, k, :],
                                             op0=mul, op1=add).then_inc(uc_ready, 1)
                dve.wait_ge(rstd_ready, plan("ln", "rstd") + 1)
                with dve.Fori(0, KT) as k:
                    dve.scalar_tensor_tensor(out=ub[:, k, :], in0=ub[:, k, :], scalar=pc("conv_ln_g", k),
                                             in1=rstd[:, :], op0=mul, op1=mul).then_inc(uc_ready, 1)
                with dve.Fori(0, KT // 2) as i:
                    lows("ln", acth, actl, i)
                residual_normed("cout", delta3, "norm_x1", None, [rstd])

            def norm_in_place(stage, gain):
                dve.wait_ge(rstd_ready, plan(stage, "rstd") + 1)
                with dve.Fori(0, KT) as k:
                    xk = xt[:, k, 1:T + 1]
                    dve.scalar_tensor_tensor(out=xk, in0=xk, scalar=pc(gain, k), in1=rstd[:, :],
                                             op0=mul, op1=mul).then_inc(x_ready, 1)

            def hybrid():
                t0, u0 = plan("in2", "tile"), UNIT0["in2"]
                dve.wait_ge(rstd_ready, plan("norm_h", "rstd") + 1)

                def scaled(to, j):
                    dve.wait_ge(units_used, u0 + j + 1 + UC)
                    dve.tensor_tensor(to, bank_of(t0 + j), rstd[:, :], mul).then_inc(evacuated, 1)

                def four(to, skip):
                    for s in range(4):
                        scaled(to[:, s, :], skip + s)

                def gate(n):
                    scaled((gate_b if n // KT else gate_a)[:, n % KT, :], 25 + n)

                scaled(small[:, :], 0)
                for to, skip in ((gv, 1), (fv, 5), (gqk, 9), (gr, 13), (fq, 17)):
                    four(to, skip)
                dve.wait_ge(log_ready, 1)
                chain.step(dve.tensor_scalar(ls[:, :, :], ls[:, :, :], 0.0, None, ALU.min))
                chain.wait()
                chain.step(dve.tensor_tensor(ls[:, :, :], ls[:, :, :], le[:, :, :], sub))
                chain.wait()
                chain.step(dve.memset(le[:, 0, :], 1.0))
                dve.wait_ge(hyb_in, 32)
                for p in range(2):
                    dve.tensor_tensor_scan(ls[:, p, :], hyb[:, 0:T], ls[:, p, :], 0.0, mul, add)
                chain.wait()
                dve.tensor_tensor_scan(small[:, :], le[:, 0, :], ls[:, 2, :], 0.0, mul, add).then_inc(cum_ready, 1)
                with dve.Fori(0, KT) as k:
                    xk = xt[:, k, 1:T + 1]
                    dve.scalar_tensor_tensor(out=xk, in0=xk, scalar=pc("final_norm_g", k), in1=acc_x[:, :],
                                             op0=mul, op1=mul).then_inc(x_ready, 1)
                four(fk, 21)
                dve.wait_ge(eb_ready, 1)
                dve.scalar_tensor_tensor(out=gqk[:, 0:2, :], in0=gqk[:, 0:2, :], scalar=0.125, in1=eb[:, :, :],
                                         op0=mul, op1=mul)
                dve.tensor_tensor(gqk[:, 2:4, :], gqk[:, 2:4, :], enb[:, :, :], mul)
                dve.tensor_copy(gdec[:, :, :], eb[:, :, :].rearrange("p a (c t) -> p a c t", t=CH)[:, :, :, CH - 1])\
                    .then_inc(qk_ready, 1)
                dve.wait_ge(qk_ready, 1)
                gate(0)
                gate(1)
                gate(2)
                for c in range(NCH - 1):
                    if c == 4:
                        gate(3)
                    dve.wait_ge(kv_mm, c + 1)
                    kv = bank[4 + c % 4].rearrange("p (a m) -> p a m", a=2)
                    for h in range(2):
                        r, m = slice(64 * h, 64 * h + 64), slice(P * h, P * h + P)
                        if c:
                            chain.wait()
                            ins = dve.tensor_tensor(states[r, c, :, :], kv[r, :, m], states[r, c - 1, :, :], add)
                        else:
                            ins = dve.tensor_scalar(states[r, c, :, :], kv[r, :, m], 1.0, None, mul)
                    ins.then_inc(kv_ready, 1)
                    dve.wait_ge(kv_ready, c + 1)
                    for p in range(2):
                        ins = dve.tensor_scalar(states[:, c, p, :], states[:, c, p, :], gdec[:, p, c:c + 1], None, mul)
                    chain.step(ins)
                gate(4)
                for j in range(8):
                    if j and j % 2 == 0:
                        gate(4 + j // 2)
                    dve.wait_ge(frs_ready, j + 1)
                    t_ = (fq if j < 4 else fk)[:, j % 4, :]
                    dve.scalar_tensor_tensor(out=t_, in0=t_, scalar=pc("fox_q_g" if j < 4 else "fox_k_g"),
                                             in1=frs[:, j % 2, :], op0=mul, op1=mul).then_inc(fox_scaled, 1)

                def gla_mask(h):
                    dve.wait_ge(gs_mm, h + 1)
                    if h >= 2:
                        dve.wait_ge(gla_done, h - 1)
                    dve.tensor_tensor(sct[:, h % 2, :].rearrange("p (a m) -> p a m", a=4),
                                      bank[4 + h % 2].rearrange("p (a m) -> p a m", a=4),
                                      gmask.rearrange("p (o m) -> p o m", o=1).to_broadcast([P, 4, P]),
                                      mul).then_inc(gs_ready, 1)

                chain.wait()
                gate(8)
                gla_mask(0)
                gate(9)
                for h in range(4):
                    if h < 3:
                        gla_mask(h + 1)
                    gate(10 + h)
                    dve.wait_ge(gla_scale, h + 1)
                    chain.step(dve.scalar_tensor_tensor(out=sct[:, h % 2, :], in0=bank[6 + h % 2],
                                                        scalar=pc("gla_norm_g", h), in1=frs[:, h % 2, :],
                                                        op0=mul, op1=mul))
                    chain.wait()
                    dve.tensor_tensor(gr[:, h, :], sct[:, h % 2, :], gr[:, h, :], mul).then_inc(gla_done, 1)

                def fox_max(h):
                    dve.wait_ge(fs_mm, h + 1)
                    for qt in range(4):
                        b, o = ((4, 0), (4, P), (5, 0), (6, 0))[qt]
                        ins = dve.tensor_reduce(fmax[:, h, qt:qt + 1], bank[b][:, o:o + (qt + 1) * P], AX.X, ALU.max)
                    chain.step(ins)
                    chain.wait()
                    dve.tensor_scalar(fneg[:, h, :], fmax[:, h, :], -1.0, None, mul).then_inc(fmax_ready, 1)

                def fox_lows(p):
                    dve.wait_ge(hi_ready, g0 + p + 1)
                    dve.tensor_tensor(actl[:, 4 + p, :], tmp[:, (g0 + p) % 2, :], acth[:, 4 + p, :].bitcast(F32),
                                      sub).then_inc(lo_ready, 1)

                gate(14)
                fox_max(0)
                gate(15)
                for h in range(4):
                    dve.wait_ge(hi_ready, plan("gla", "split") + h + 1)
                    dve.wait_ge(gla_done, h + 1)
                    dve.tensor_tensor(actl[:, h, :], gr[:, h, :], acth[:, h, :].bitcast(F32), sub).then_inc(lo_ready, 1)
                fox_max(1)
                g0 = plan("fox", "split")
                for h in range(8):
                    dve.wait_ge(f_exp, h + 1)
                    chain.step(dve.reciprocal(frec[:, h, :], fsum[:, h, :]))
                    chain.wait()
                    for qt in range(4):
                        p_ = fp[:, h % 2, FOX_OFF[qt]:FOX_OFF[qt] + (qt + 1) * P]
                        ins = dve.tensor_scalar(p_, p_, frec[:, h, qt:qt + 1], None, mul)
                    ins.then_inc(fp_ready, 1)
                    dve.wait_ge(fpt_mm, h + 1)
                    dve.tensor_copy(fpt[:, h % 2, 0:4 * P], bank[0]).then_inc(fpt_v, 1)
                    if h % 2 == 0 and h:
                        fox_lows(h // 2 - 1)
                    if h < 6:
                        fox_max(h + 2)
                fox_lows(3)
                t0, u0, f0 = plan("branch", "tile"), UNIT0["branch"], plan("branch", "full")
                g0 = plan("branch", "split")
                with dve.Fori(0, KT // 2) as i:
                    for s in range(2):
                        dve.wait_ge(tile_full, i * 2 + (f0 + s + 1))
                        ga, gb = gate_a[:, i * 2 + s, :], gate_b[:, i * 2 + s, :]
                        dve.tensor_tensor(ga, ga, bank_of(t0 + 2 * s), mul).then_inc(evacuated, 1)
                        dve.wait_ge(units_used, i * 2 + (u0 + s + 1 + UC))
                        dve.tensor_tensor(gb, gb, bank_of(t0 + 2 * s + 1), mul).then_inc(evacuated, 1)
                        dve.wait_ge(evacuated, i * 4 + (t0 + 2 * s + 2 + UC))
                        dve.wait_ge(lo_ready, i * 2 + (g0 + s + 1))
                        dve.tensor_tensor(tmp[:, (g0 + s) % 2, :], ga, gb, add).then_inc(val_ready, 1)
                    lows("branch", yh, yl, i)
                residual_normed("out2", delta4, "norm_ffn2", ["norm_ffn_g_2"], [rstd])

            def ffn2(scaled):
                t0, v0, g0 = plan("up2", "tile"), plan("up2", "val"), plan("up2", "split")
                with dve.Fori(0, FT // 2) as i:
                    chain.enter(i, 4)
                    for s in range(2):
                        j = i * 2 + s
                        scaled(i, 2 * s)
                        scaled(i, 2 * s + 1)
                        dve.wait_ge(evacuated, i * 4 + (t0 + 2 * s + 1 + UC))
                        chain.step(dve.tensor_scalar(cg[:, s, :], cu[:, 2 * s, 2:T + 2], pc("conv_w_2", j * 3 + 2),
                                                     pc("conv_b_2", j), mul, add))
                    for s in range(2):
                        chain.wait(1)
                        chain.step(dve.scalar_tensor_tensor(
                            out=cg[:, s, :], in0=cu[:, 2 * s, 1:T + 1], scalar=pc("conv_w_2", (i * 2 + s) * 3 + 1),
                            in1=cg[:, s, :], op0=mul, op1=add))
                    for s in range(2):
                        chain.wait(1 - s)
                        dve.scalar_tensor_tensor(
                            out=cg[:, s, :], in0=cu[:, 2 * s, 0:T], scalar=pc("conv_w_2", (i * 2 + s) * 3),
                            in1=cg[:, s, :], op0=mul, op1=add).then_inc(conv_ready, 1)
                    for s in range(2):
                        dve.wait_ge(evacuated, i * 4 + (t0 + 2 * s + 2 + UC))
                        dve.wait_ge(gate_ready, i * 2 + (2 * FT + s + 1))
                        dve.wait_ge(lo_ready, i * 2 + (g0 + s + 1))
                        dve.tensor_tensor(tmp[:, (g0 + s) % 2, :], sg[:, s, :], cu[:, 2 * s + 1, 2:T + 2],
                                          mul).then_inc(val_ready, 1)
                    lows("up2", hidh, hidl, i)
                    chain.leave(FT // 2, 4)
                residual_normed("down2", delta2, "last", None, [rstd])

            def last_norm():
                norm_in_place("last", "norm_final_g_2")

            attention(0)
            ffn(0)
            convolution()
            attention(1)
            ffn(1)
            hybrid()
            ffn(2)
            last_norm()


def units_of(w):
    k, n = w.shape
    assert k == BLOCKS * P
    return w.reshape(BLOCKS, P, n // P, P).transpose(2, 1, 0, 3).reshape(n // P, P, BLOCKS * P)


def blocks_of(blocks):
    blocks = list(blocks) + [np.zeros((P, P), np.float32)] * (-len(blocks) % BLOCKS)
    a = np.stack(blocks).reshape(-1, BLOCKS, P, P)
    return a.transpose(0, 2, 1, 3).reshape(-1, P, BLOCKS * P)


def padded(w, rows, cols, r0=0):
    out = np.zeros((rows, cols), np.float32)
    out[r0:r0 + w.shape[0], :w.shape[1]] = w
    return out


def down_units(w):
    return np.concatenate([blocks_of([w[k * P:(k + 1) * P, j * P:(j + 1) * P] for k in range(FT)])
                           for j in range(KT)])


def paired(w, half):
    u = units_of(w)
    return np.stack([u[:half], u[half:]], 1).reshape(2 * half, P, BLOCKS * P)


def pack(i):
    g = lambda n: np.asarray(i[n], np.float32)
    cut = lambda w, k, j: w[k * P:(k + 1) * P, j * P:(j + 1) * P]
    g1 = padded(g("rwkv_g1")[0], D, 2 * P)
    g2 = padded(g("rwkv_g2")[0], 2 * P, D)
    stream = {
        "lora_in": units_of(np.concatenate([g("rwkv_w1")[0], g("rwkv_a1")[0]], 1)),
        "gate_in": units_of(g1),
        "w2": blocks_of([padded(g("rwkv_w2")[0][:, j * P:(j + 1) * P], P, P) for j in range(KT)]),
        "a2": blocks_of([padded(g("rwkv_a2")[0][:, j * P:(j + 1) * P], P, P, 64) for j in range(KT)]),
        "k": units_of(g("rwkv_w_k")[0]), "r": units_of(g("rwkv_w_r")[0]), "v": units_of(g("rwkv_w_v")[0]),
        "g2": blocks_of([cut(g2, b, j) for j in range(KT) for b in range(2)]),
        "o": units_of(g("rwkv_w_o")[0]),
        "cin": paired(g("conv_w_in")[0], KT), "cout": units_of(g("conv_w_out")[0]),
        "out2": units_of(g("w_out_2")[0]), "up2": paired(g("w_up_2")[0], FT),
        "down2": down_units(g("w_down_2")[0]),
    }
    for l in range(2):
        stream[f"kv{l}"] = units_of(g("xattn_w_kv")[l])
        stream[f"q{l}"] = units_of(g("xattn_w_q")[l])
        stream[f"xo{l}"] = units_of(g("xattn_w_o")[l])
        stream[f"up{l}"] = paired(g("ffn_w_in")[l], FT)
        stream[f"down{l}"] = down_units(g("ffn_w_out")[l])
    stream["kv1"], stream["kv1b"] = stream["kv1"][:12], stream["kv1"][12:]
    w = g("w_in_2")[0]
    gq, gk, gv, gr, glr, fq, fk, fv, ff, gg, gf = np.split(
        w, np.cumsum([256, 256, 512, 512, 16, 512, 512, 512, 8, D])[:].tolist(), axis=1)
    small = np.concatenate([padded(glr, D, 32), padded(ff, D, 96)], 1)
    stream["in2"] = units_of(np.concatenate([small, gv, fv, gq, gk, gr, fq, fk, gg, gf], 1))
    wg, wf = g("w_gla_branch_2")[0], g("w_fox_branch_2")[0]
    stream["branch"] = blocks_of([cut(m, k, j) for j in range(KT) for m in (wg, wf) for k in range(4)])
    weights = np.concatenate([stream[n] for n, _ in STREAM])
    for n, c in STREAM:
        assert stream[n].shape[0] == c, (n, stream[n].shape)

    vec = lambda a: np.asarray(a, np.float32).reshape(-1, P).T
    taps = lambda a, n: np.asarray(a, np.float32).reshape(a.shape[0], n, P).transpose(2, 1, 0).reshape(P, -1)
    cols = {
        "mem_norm_g": vec(g("mem_norm_g")), "norm_mix_g": vec(g("norm_mix_g")),
        "norm_xattn_g": vec(g("norm_xattn_g")), "norm_ffn_g": vec(g("norm_ffn_g")),
        "final_norm_g": vec(g("final_norm_g")), "mu": vec(g("rwkv_mu")), "w0": vec(g("rwkv_w0")),
        "a0": vec(g("rwkv_a0")), "k_k": vec(g("rwkv_k_k")), "k_a": vec(g("rwkv_k_a")),
        "r_k": vec(g("rwkv_r_k")), "ln_g": vec(g("rwkv_ln_g")), "ln_b": vec(g("rwkv_ln_b")),
        "conv_b_in": vec(g("conv_b_in")), "conv_dw": taps(g("conv_dw")[0], KT),
        "conv_dw_b": vec(g("conv_dw_b")), "conv_ln_g": vec(g("conv_ln_g")), "conv_ln_b": vec(g("conv_ln_b")),
        "conv_b_out": vec(g("conv_b_out")),
        "ffn_dw": np.concatenate([taps(g("ffn_dw")[l], 2 * FT) for l in range(2)], 1),
        "norm_mix_g_2": vec(g("norm_mix_g_2")), "gla_b": vec(g("gla_alpha_b_2")),
        "gla_norm_g": vec(g("gla_out_norm_g_2")),
        "fox_q_g": vec(np.tile(g("fox_q_norm_g_2")[0], 2)), "fox_k_g": vec(np.tile(g("fox_k_norm_g_2")[0], 2)),
        "gate_b_2": vec(g("gate_b_2")), "norm_ffn_g_2": vec(g("norm_ffn_g_2")),
        "conv_w_2": taps(g("conv_w_2")[0], FT), "conv_b_2": vec(g("conv_b_2")),
        "norm_final_g_2": vec(g("norm_final_g_2")), "fox_fb": padded(g("fox_forget_b_2")[0][:, None], P, 1, 32),
    }
    par = np.concatenate([cols[n] for n, _ in PARAMS], 1)
    assert par.shape == (P, NPAR), par.shape
    feature_major = lambda a: np.ascontiguousarray(a.T.reshape(KT, P, -1).transpose(1, 0, 2))
    return {"weights": weights, "par": np.ascontiguousarray(par), "x": feature_major(g("x")[0]),
            "mem": feature_major(g("mem")[0]),
            "w2g": padded(g("gla_alpha_w2_2")[0], P, 256), **constants()}


def kernel(**inputs):
    import concourse.bacc as bacc
    from concourse.bass_utils import run_bass_kernel_spmd

    nc = bacc.Bacc("TRN2", target_bir_lowering=False, num_devices=1, dynamic_dma_scratch_size=1024)
    arrays = {f"in_{n}": np.ascontiguousarray(a) for n, a in pack(inputs).items()}
    dram = {n[3:]: nc.dram_tensor(n, a.shape, F32, kind="ExternalInput").ap() for n, a in arrays.items()}
    dram["out"] = nc.dram_tensor("out_x", (P, KT, T), F32, kind="ExternalOutput").ap()
    build_program(nc, dram)
    r = run_bass_kernel_spmd(nc, [arrays], core_ids=[0])
    out = r.results[0]["out_x"]
    return np.ascontiguousarray(out.transpose(2, 1, 0).reshape(1, T, D))
```
